# Optimizing a Trainium2 kernel written in Bass

```python
import jax
import jax.numpy as jnp
from jax import lax
import numpy as np
import jax, jax.numpy as jnp

D_MODEL = 1024
BATCH = 1
SEQ = 256
DEPTH = 1

GRID_W = 64
CTX_LEN = 256
FNET_DIM = 512
FNET_GROUPS = 4
FNET_GROUP_DIM = FNET_DIM // FNET_GROUPS
HG_DIM = 512
HG_HEADS = 4
HG_HEAD_DIM = HG_DIM // HG_HEADS
HG_CHUNK = 16
D_FF = 2816
CONV_K = 3
N_MOD = 6
EPS = 1e-6

OFF_FNET = 0
OFF_Q = OFF_FNET + FNET_DIM
OFF_FF = OFF_Q + HG_DIM
OFF_FB = OFF_FF + HG_DIM
OFF_I = OFF_FB + HG_DIM
OFF_G = OFF_I + HG_DIM
OFF_GA = OFF_G + HG_DIM
OFF_GB = OFF_GA + D_MODEL
IN_DIM = OFF_GB + D_MODEL


def rmsnorm(x, g):
    xf = x.astype(jnp.float32)
    y = xf * lax.rsqrt(jnp.mean(xf * xf, axis=-1, keepdims=True) + EPS) * g.astype(jnp.float32)
    return y.astype(x.dtype)

def modulate(h, shift, scale):
    return h * (1.0 + scale) + shift

def fourier_mix(u):
    b, l, _ = u.shape
    ug = u.astype(jnp.float32).reshape(b, l, FNET_GROUPS, FNET_GROUP_DIM)
    y = jnp.fft.fft2(ug, axes=(1, 3), norm='ortho').real
    return y.reshape(b, l, FNET_DIM).astype(u.dtype)

def hgrn_chunk_scan(q, k, v, logf, s0):
    b, l, h, _ = q.shape
    dv = v.shape[-1]
    n = l // HG_CHUNK

    def to_chunks(t):
        return t.reshape(b, n, HG_CHUNK, h, t.shape[-1]).transpose(1, 0, 3, 2, 4)

    qc, kc, vc, gc = to_chunks(q), to_chunks(k), to_chunks(v), to_chunks(logf)
    lower = jnp.tril(jnp.ones((HG_CHUNK, HG_CHUNK), dtype=bool))[:, :, None]

    def step(state, inp):
        qi, ki, vi, gi = inp
        cum = jnp.cumsum(gi, axis=-2)
        total = cum[..., -1:, :]
        rel = cum[..., :, None, :] - cum[..., None, :, :]
        decay = jnp.exp(jnp.where(lower, rel, -jnp.inf))
        attn = jnp.einsum('bhtd,bhsd,bhtsd->bhts', qi, ki, decay)
        o = (jnp.einsum('bhts,bhsv->bhtv', attn, vi)
             + jnp.einsum('bhtd,bhdv->bhtv', qi * jnp.exp(cum), state))
        k_dec = ki * jnp.exp(total - cum)
        new_state = state * jnp.exp(total)[..., 0, :, None] + jnp.einsum('bhsd,bhsv->bhdv', k_dec, vi)
        return new_state, o

    s_final, o = lax.scan(step, s0, (qc, kc, vc, gc))
    o = o.transpose(1, 0, 3, 2, 4).reshape(b, l, h, dv)
    return o, s_final

def hgrn_inputs(u, lb):
    uf = u.astype(jnp.float32)
    b, l, _ = u.shape

    def heads(t):
        return t.reshape(b, l, HG_HEADS, HG_HEAD_DIM)

    q = heads(jax.nn.silu(uf[..., OFF_Q:OFF_Q + HG_DIM]))
    v = heads(uf[..., OFF_I:OFF_I + HG_DIM])
    f_fwd = lb + (1.0 - lb) * jax.nn.sigmoid(uf[..., OFF_FF:OFF_FF + HG_DIM])
    f_bwd = lb + (1.0 - lb) * jax.nn.sigmoid(uf[..., OFF_FB:OFF_FB + HG_DIM])
    return (q, v, heads(1.0 - f_fwd), heads(jnp.log(f_fwd)), heads(1.0 - f_bwd), heads(jnp.log(f_bwd)))

def hgrn_bidir(q, v, k_f, g_f, k_b, g_b, s0_f, s0_b):
    o_f, s_f = hgrn_chunk_scan(q, k_f, v, g_f, s0_f)
    flip = lambda t: jnp.flip(t, axis=1)
    o_b, s_b = hgrn_chunk_scan(flip(q), flip(k_b), flip(v), flip(g_b), s0_b)
    return o_f + flip(o_b), s_f, s_b

def hgrn_readout(u, o, onorm_g):
    b, l = o.shape[0], o.shape[1]
    on = o * lax.rsqrt(jnp.mean(o * o, axis=-1, keepdims=True) + EPS)
    on = on.reshape(b, l, HG_DIM) * onorm_g.astype(jnp.float32)
    on = on * jax.nn.silu(u[..., OFF_G:OFF_G + HG_DIM].astype(jnp.float32))
    return on.astype(u.dtype)

def merge_branches(u, y_hgrn, w_a, w_b, w_out):
    y_a = fourier_mix(u[..., OFF_FNET:OFF_FNET + FNET_DIM]) @ w_a
    y_b = y_hgrn @ w_b
    g_a = jax.nn.sigmoid(u[..., OFF_GA:OFF_GB])
    g_b = jax.nn.sigmoid(u[..., OFF_GB:IN_DIM])
    return (g_a * y_a + g_b * y_b) @ w_out

def conv_ffn(h, w_up, conv_w, conv_b, w_down, rows, cols):
    b, l, _ = h.shape
    z = (h @ w_up).reshape(b, rows, cols, 2 * D_FF)
    z = lax.conv_general_dilated(z, conv_w[:, :, None, :], window_strides=(1, 1), padding='SAME',
                                 dimension_numbers=('NHWC', 'HWIO', 'NHWC'),
                                 feature_group_count=2 * D_FF)
    z = z.reshape(b, l, 2 * D_FF) + conv_b
    return (jax.nn.silu(z[..., :D_FF]) * z[..., D_FF:]) @ w_down

def first_inputs(seed: int = 0) -> dict:
    key = jax.random.key(seed)
    ks = jax.random.split(key, 19)

    def nrm(k, shape):
        return jax.random.normal(k, shape, jnp.float32)

    def w(k, shape, fan_in, scale=1.0):
        return nrm(k, shape) * (scale * fan_in ** -0.5)

    def gain(k, shape):
        return 1.0 + 0.1 * nrm(k, shape)

    return {
        'x': nrm(ks[0], (BATCH, SEQ, D_MODEL)),
        'c': nrm(ks[1], (BATCH, D_MODEL)),
        'ctx': nrm(ks[2], (BATCH, CTX_LEN, D_MODEL)),
        'c_ctx': nrm(ks[3], (D_MODEL,)),
        'ada_w': w(ks[4], (DEPTH, D_MODEL, N_MOD * D_MODEL), D_MODEL, 0.5),
        'ada_b': 0.02 * nrm(ks[5], (DEPTH, N_MOD * D_MODEL)),
        'norm1_g': gain(ks[6], (DEPTH, D_MODEL)),
        'w_in': w(ks[7], (DEPTH, D_MODEL, IN_DIM), D_MODEL),
        'hg_lb': 0.1 * nrm(ks[8], (DEPTH + 1, HG_DIM)),
        'hg_onorm_g': gain(ks[9], (DEPTH, HG_DIM)),
        'w_a': w(ks[10], (DEPTH, FNET_DIM, D_MODEL), FNET_DIM),
        'w_b': w(ks[11], (DEPTH, HG_DIM, D_MODEL), HG_DIM),
        'w_out': w(ks[12], (DEPTH, D_MODEL, D_MODEL), D_MODEL),
        'norm2_g': gain(ks[13], (DEPTH, D_MODEL)),
        'ffn_up': w(ks[14], (DEPTH, D_MODEL, 2 * D_FF), D_MODEL),
        'ffn_conv_w': w(ks[15], (DEPTH, CONV_K, CONV_K, 2 * D_FF), CONV_K * CONV_K),
        'ffn_conv_b': 0.02 * nrm(ks[16], (DEPTH, 2 * D_FF)),
        'ffn_down': w(ks[17], (DEPTH, D_FF, D_MODEL), D_FF),
        'final_g': gain(ks[18], (D_MODEL,)),
    }

def first_block(x, c, ctx, c_ctx, ada_w, ada_b, norm1_g, w_in, hg_lb, hg_onorm_g, w_a, w_b, w_out,
              norm2_g, ffn_up, ffn_conv_w, ffn_conv_b, ffn_down, final_g):
    b, seq, _ = x.shape
    rows = seq // GRID_W
    ctx_len = ctx.shape[1]
    lb_all = jnp.cumsum(jax.nn.softmax(hg_lb.astype(jnp.float32), axis=0), axis=0)
    s_zero = jnp.zeros((b, HG_HEADS, HG_HEAD_DIM, HG_HEAD_DIM), jnp.float32)
    for layer in range(DEPTH):
        last = layer == DEPTH - 1
        mx = (jax.nn.silu(c) @ ada_w[layer] + ada_b[layer]).reshape(b, 1, N_MOD, D_MODEL)
        mc = (jax.nn.silu(c_ctx) @ ada_w[layer] + ada_b[layer]).reshape(N_MOD, D_MODEL)
        lb = lb_all[layer]

        hx = modulate(rmsnorm(x, norm1_g[layer]), mx[:, :, 0], mx[:, :, 1])
        hc = modulate(rmsnorm(ctx, norm1_g[layer]), mc[0], mc[1])
        ux = hx @ w_in[layer]
        uc = hc @ w_in[layer]
        oc, sc_f, sc_b = hgrn_bidir(*hgrn_inputs(uc, lb), s_zero, s_zero)
        ox, _, _ = hgrn_bidir(*hgrn_inputs(ux, lb), sc_f, sc_b)
        yx = merge_branches(ux, hgrn_readout(ux, ox, hg_onorm_g[layer]), w_a[layer], w_b[layer], w_out[layer])
        x = x + mx[:, :, 2] * yx
        if not last:
            yc = merge_branches(uc, hgrn_readout(uc, oc, hg_onorm_g[layer]), w_a[layer], w_b[layer], w_out[layer])
            ctx = ctx + mc[2] * yc

        h2 = modulate(rmsnorm(x, norm2_g[layer]), mx[:, :, 3], mx[:, :, 4])
        x = x + mx[:, :, 5] * conv_ffn(h2, ffn_up[layer], ffn_conv_w[layer], ffn_conv_b[layer],
                                       ffn_down[layer], rows, GRID_W)
        if not last:
            h2c = modulate(rmsnorm(ctx, norm2_g[layer]), mc[3], mc[4])
            ctx = ctx + mc[5] * conv_ffn(h2c, ffn_up[layer], ffn_conv_w[layer], ffn_conv_b[layer],
                                         ffn_down[layer], 1, ctx_len)
    return rmsnorm(x, final_g)


CHUNK = 64
N_PREV_CHUNKS = 8
BAND = N_PREV_CHUNKS + 1

D_MIX = D_MODEL
HEAD_DIM = 64
ATTN_WIDTH = D_MIX // 2
N_ATTN_HEADS = ATTN_WIDTH // HEAD_DIM
CONV_WIDTH = D_MIX // 4
POOL_WIDTH = D_MIX - ATTN_WIDTH - CONV_WIDTH
POOL_WINDOWS = (2, 4, 8, 16)
N_POOL_GROUPS = len(POOL_WINDOWS)
POOL_GROUP = POOL_WIDTH // N_POOL_GROUPS
REL_CLIP = 128

D_IN = 3 * ATTN_WIDTH + 3 * CONV_WIDTH + POOL_WIDTH
D_FF_2 = 4 * D_MODEL
NEG_INF = -1e30


def rms_norm(x, g):
    x32 = x.astype(jnp.float32)
    y = x32 * lax.rsqrt(jnp.mean(x32 * x32, axis=-1, keepdims=True) + EPS)
    return (y * g.astype(jnp.float32)).astype(x.dtype)

def chunked_band_attention(q, k, v, rel_bias):
    b, s, h, d = q.shape
    nc = s // CHUNK
    qc = q.reshape(b, nc, CHUNK, h, d)
    pad = ((0, 0), (N_PREV_CHUNKS, 0), (0, 0), (0, 0), (0, 0))
    kp = jnp.pad(k.reshape(b, nc, CHUNK, h, d), pad)
    vp = jnp.pad(v.reshape(b, nc, CHUNK, h, d), pad)
    band_idx = jnp.arange(nc)[:, None] + jnp.arange(BAND)[None, :]
    kb = kp[:, band_idx].reshape(b, nc, BAND * CHUNK, h, d)
    vb = vp[:, band_idx].reshape(b, nc, BAND * CHUNK, h, d)
    scores = jnp.einsum('bnqhd,bnkhd->bnhqk', qc, kb).astype(jnp.float32) * (d ** -0.5)
    qi = jnp.arange(CHUNK)[:, None]
    kj = jnp.arange(BAND * CHUNK)[None, :]
    dist = qi + N_PREV_CHUNKS * CHUNK - kj
    bias = rel_bias[:, jnp.clip(dist, -REL_CLIP, REL_CLIP) + REL_CLIP].astype(jnp.float32)
    valid = jnp.repeat(band_idx >= N_PREV_CHUNKS, CHUNK, axis=1)
    scores = jnp.where(valid[None, :, None, None, :], scores + bias[None, None], NEG_INF)
    p = jax.nn.softmax(scores, axis=-1).astype(v.dtype)
    out = jnp.einsum('bnhqk,bnkhd->bnqhd', p, vb)
    return out.reshape(b, s, h * d)

def gated_short_conv(gb, gc, hin, conv_w):
    z = gc * hin
    s = z.shape[1]
    zp = jnp.pad(z, ((0, 0), (CONV_K - 1, 0), (0, 0)))
    y = sum(conv_w[i] * zp[:, i:i + s] for i in range(CONV_K))
    return gb * y

def multiscale_pool(u, pool_w, pool_scale):
    b, s, c = u.shape
    u32 = u.astype(jnp.float32)
    cs = jnp.concatenate([jnp.zeros((b, 1, c), jnp.float32), jnp.cumsum(u32, axis=1)], axis=1)
    pos1 = jnp.arange(s) + 1
    outs = []
    for g, w in enumerate(POOL_WINDOWS):
        sl = slice(g * POOL_GROUP, (g + 1) * POOL_GROUP)
        csg = cs[:, :, sl]
        lag = jnp.pad(csg[:, :s + 1 - w], ((0, 0), (w - 1, 0), (0, 0)))
        cnt = jnp.minimum(pos1, w).astype(jnp.float32)[None, :, None]
        m = (csg[:, 1:] - lag) / cnt - u32[:, :, sl]
        outs.append(jnp.einsum('bsc,cd->bsd', m.astype(u.dtype), pool_w[g]))
    return jnp.concatenate(outs, axis=-1) * pool_scale

def second_inputs(seed: int = 0) -> dict:
    key = jax.random.key(seed)
    ks = jax.random.split(key, 13)
    f32 = jnp.float32
    L = DEPTH
    x = jax.random.normal(ks[0], (BATCH, SEQ, D_MODEL), f32)
    norm1_g = 1.0 + 0.05 * jax.random.normal(ks[1], (L, D_MODEL), f32)
    w_in = jax.random.normal(ks[2], (L, D_MODEL, D_IN), f32) * D_MODEL ** -0.5
    q_norm_g = 1.0 + 0.05 * jax.random.normal(ks[3], (L, HEAD_DIM), f32)
    k_norm_g = 1.0 + 0.05 * jax.random.normal(ks[4], (L, HEAD_DIM), f32)
    rel_bias = 0.1 * jax.random.normal(ks[5], (L, N_ATTN_HEADS, 2 * REL_CLIP + 1), f32)
    conv_w = jax.random.normal(ks[6], (L, CONV_K, CONV_WIDTH), f32) * CONV_K ** -0.5
    pool_w = jax.random.normal(ks[7], (L, N_POOL_GROUPS, POOL_GROUP, POOL_GROUP), f32) * POOL_GROUP ** -0.5
    pool_scale = 0.5 + 0.1 * jax.random.normal(ks[8], (L, POOL_WIDTH), f32)
    w_out = jax.random.normal(ks[9], (L, D_MIX, D_MODEL), f32) * D_MIX ** -0.5
    norm2_g = 1.0 + 0.05 * jax.random.normal(ks[10], (L, D_MODEL), f32)
    w_mlp1 = jax.random.normal(ks[11], (L, D_MODEL, D_FF_2), f32) * D_MODEL ** -0.5
    w_mlp2 = jax.random.normal(ks[12], (L, D_FF_2, D_MODEL), f32) * D_FF_2 ** -0.5
    return {"x": x, "norm1_g": norm1_g, "w_in": w_in, "q_norm_g": q_norm_g,
            "k_norm_g": k_norm_g, "rel_bias": rel_bias, "conv_w": conv_w,
            "pool_w": pool_w, "pool_scale": pool_scale, "w_out": w_out,
            "norm2_g": norm2_g, "w_mlp1": w_mlp1, "w_mlp2": w_mlp2}

def second_block(x, norm1_g, w_in, q_norm_g, k_norm_g, rel_bias, conv_w, pool_w,
              pool_scale, w_out, norm2_g, w_mlp1, w_mlp2):
    b, s, _ = x.shape
    a = ATTN_WIDTH
    c = CONV_WIDTH
    for l in range(DEPTH):
        h = rms_norm(x, norm1_g[l])
        p = jnp.einsum('bsd,de->bse', h, w_in[l])
        q = p[..., 0:a].reshape(b, s, N_ATTN_HEADS, HEAD_DIM)
        k = p[..., a:2 * a].reshape(b, s, N_ATTN_HEADS, HEAD_DIM)
        v = p[..., 2 * a:3 * a].reshape(b, s, N_ATTN_HEADS, HEAD_DIM)
        o = 3 * a
        gb = p[..., o:o + c]
        gc = p[..., o + c:o + 2 * c]
        hin = p[..., o + 2 * c:o + 3 * c]
        u = p[..., o + 3 * c:]
        q = rms_norm(q, q_norm_g[l])
        k = rms_norm(k, k_norm_g[l])
        y_attn = chunked_band_attention(q, k, v, rel_bias[l])
        y_conv = gated_short_conv(gb, gc, hin, conv_w[l])
        y_pool = multiscale_pool(u, pool_w[l], pool_scale[l])
        mix = jnp.concatenate([y_attn, y_conv, y_pool], axis=-1)
        x = x + jnp.einsum('bse,ed->bsd', mix, w_out[l])
        h2 = rms_norm(x, norm2_g[l])
        f = jnp.square(jax.nn.relu(jnp.einsum('bsd,df->bsf', h2, w_mlp1[l])))
        x = x + jnp.einsum('bsf,fd->bsd', f, w_mlp2[l])
    return x


def setup_inputs(seed=0):
    out = dict(first_inputs(seed))
    for name, value in second_inputs(seed + 1).items():
        if name != "x":
            out[name + "_2"] = value
    return out


def reference(
    x, c, ctx, c_ctx, ada_w, ada_b, norm1_g, w_in, hg_lb, hg_onorm_g, w_a, w_b, w_out, norm2_g,
    ffn_up, ffn_conv_w, ffn_conv_b, ffn_down, final_g, norm1_g_2, w_in_2, q_norm_g_2,
    k_norm_g_2, rel_bias_2, conv_w_2, pool_w_2, pool_scale_2, w_out_2, norm2_g_2, w_mlp1_2,
    w_mlp2_2,
):
    x = first_block(
        x, c, ctx, c_ctx, ada_w, ada_b, norm1_g, w_in, hg_lb, hg_onorm_g, w_a, w_b, w_out,
        norm2_g, ffn_up, ffn_conv_w, ffn_conv_b, ffn_down, final_g,
    )
    return second_block(
        x, norm1_g_2, w_in_2, q_norm_g_2, k_norm_g_2, rel_bias_2, conv_w_2, pool_w_2,
        pool_scale_2, w_out_2, norm2_g_2, w_mlp1_2, w_mlp2_2,
    )


_drawn_inputs = setup_inputs


def setup_inputs(seed=0):
    import zlib

    import numpy as np

    out = dict(_drawn_inputs(seed))
    spreads = {}
    factors = {'ctx': 8.0,
     'c_ctx': 8.0,
     'hg_lb': 8.0,
     'hg_onorm_g': 4.155,
     'ffn_conv_b': 7.899,
     'q_norm_g_2': 8.0,
     'k_norm_g_2': 8.0,
     'rel_bias_2': 6.403}
    for name, (base, spread) in spreads.items():
        noise = np.random.default_rng([zlib.crc32(name.encode()), seed]).standard_normal(out[name].shape)
        drawn = base * np.exp(spread * noise) if base else spread * noise
        out[name] = jnp.asarray(drawn.astype(out[name].dtype))
    for name, factor in factors.items():
        out[name] = (out[name] * factor).astype(out[name].dtype)
    return out
```

```python
import numpy as np

import concourse.bass as bass
from concourse import mybir

F32 = mybir.dt.float32
F32R = mybir.dt.float32r
U8 = mybir.dt.uint8
ALU = mybir.AluOpType
ACT = mybir.ActivationFunctionType
AX = mybir.AxisListType

P = 128
T = 256
D = 1024
KT = D // P
NH = 4
CH = 2048
NRAW, NHI = 4, 3
EPS = 1e-6
LEVELS = [1, 2, 4, 8, 16, 32, 64]
HORDER = [0, 2, 4, 6, 1, 3, 5, 7]

VEC = {}
_at = 0
for _n, _w in [("norm1_g", 8), ("ada_b", 48), ("hg_lb", 8), ("onorm", 4), ("norm2_g", 8), ("conv_b", 44),
               ("conv_w", 44 * 9), ("final_g", 8), ("norm1_g_2", 8), ("q_g", 1), ("k_g", 1), ("conv_w_2", 6),
               ("pool_scale", 2), ("norm2_g_2", 8), ("c2", 16)]:
    VEC[_n] = (_at, _w)
    _at += _w
NV = _at

CON = {}
_at = 0
for _n, _w in [("ident", 128), ("dft_c", 256), ("dft_l", 1024), ("blk", 128), ("poolr", 32)]:
    CON[_n] = (_at, _w)
    _at += _w
NC = _at


class Queue:

    def __init__(self, sem):
        self.sem, self.count, self.ops, self.seen = sem, 0, [], {}

    def wait(self, *marks):
        for sem, value in marks:
            if self.seen.get(sem.name, 0) < value:
                self.seen[sem.name] = value
                self.ops.append(lambda e, s=sem, v=value: e.wait_ge(s, v))

    def do(self, fn):
        self.count += 1
        self.ops.append(lambda e, f=fn: f(e).then_inc(self.sem, 1))
        return self.sem, self.count

    def go(self, fn):
        self.ops.append(fn)

    def replay(self, e):
        for op in self.ops:
            op(e)


def chunk_plan():
    plan = []
    for i in range(4):
        plan += [("ada_s", i, 2048), ("ada_p", i, 2048)]
    for i in range(20):
        plan.append(("w_in", i, 2048))
        if 2 <= i < 10:
            plan += [("ada_hi", 2 * (i - 2), 2048), ("ada_hi", 2 * (i - 2) + 1, 2048)]
    for name, n in (("w_a", 2), ("w_b", 2), ("w_out", 4)):
        plan += [(name, i, 2048) for i in range(n)]
    for i in range(22):
        plan.append(("ffn_up", i, 2048))
        if i >= 5 and i % 2:
            plan.append(("ffn_down", (i - 5) // 2, 2048))
    plan += [("ffn_down", 9, 2048), ("ffn_down", 10, 2048)]
    for name, n in (("w_in_2", 10), ("w_out_2", 4)):
        plan += [(name, i, 2048) for i in range(n)]
    for i in range(16):
        plan.append(("w_mlp1", i, 2048))
        if i >= 2:
            plan.append(("w_mlp2", i - 2, 2048))
    return plan + [("w_mlp2", 14, 2048), ("w_mlp2", 15, 2048)]


def build(nc, io):
    sems = []

    def sem(name):
        s = nc.alloc_semaphore(name)
        sems.append(s)
        return s

    PE, SC, VE, PO, SY = (Queue(sem(n)) for n in ("pe_done", "act_done", "dve_done", "pool_done", "sp_done"))

    start = 16512
    cursor = [start]

    def place(name, shape, dt, offset):
        return nc.alloc_sbuf_tensor_at(name, shape, dt, offset=offset)

    def keep(name, shape, dt=F32):
        size = int(np.prod(shape[1:])) * (1 if dt == U8 else 4)
        t = place(name, shape, dt, cursor[0])
        cursor[0] += (size + 31) // 32 * 32
        return t

    raw = [keep(f"raw{i}", [P, CH]) for i in range(NRAW)]
    whi = [keep(f"whi{i}", [P, CH], F32R) for i in range(NHI)]
    wlo = [keep(f"wlo{i}", [P, CH], F32R) for i in range(NHI)]
    XR = keep("XR", [P, KT, T])
    con = keep("con", [P, NC])
    masks = keep("masks", [P, len(LEVELS), P], U8)
    vec = keep("vec", [P, NV])
    CB = keep("CB", [P, D])
    RC = keep("RC", [P, 64])
    ones = keep("ones", [P, T])
    eps = keep("eps", [P, 1])
    C2 = keep("C2", [P, KT, 2])
    MOD = keep("MOD", [P, 16, 2])
    warmed = keep("warmed", [P, 1])
    A1 = keep("A1", [P, KT, 2])
    MODX = keep("MODX", [P, 32])
    A2 = keep("A2", [P, KT])
    LBE = keep("LBE", [P, 8])
    LBM = keep("LBM", [P, 4])
    LB = keep("LB", [P, 4])
    LB1 = keep("LB1", [P, 4])
    MX = keep("MX", [P, 16])
    SM = keep("SM", [P, 16])
    base = cursor[0]

    def area(name, shape, kb, dt=F32):
        return place(name, shape, dt, base + int(kb * 1024))

    def v(name, i=0, n=None):
        a, w = VEC[name]
        return vec[:, a + i:a + i + (w if n is None else n)]

    def c(name):
        a, w = CON[name]
        return con[:, a:a + w]

    ident = c("ident")
    bank = [nc.alloc_psum_tensor(f"bank{i}", [P, 512], F32) for i in range(8)]
    freed = {i: [] for i in range(8)}
    ring = {"g": [0, 1, 2], "m": [3, 4, 5, 6, 7]}
    turn = {"g": 0, "m": 0}

    def claim(b):
        PE.wait(*freed[b])
        freed[b] = []
        return b

    def take(kind):
        turn[kind] += 1
        return claim(ring[kind][turn[kind] % len(ring[kind])])

    def load(eng, name, dst, src):
        s = sem(f"in_{name}")
        eng.go(lambda e: e.dma_start(dst, src).then_inc(s, 16))
        return s, 16

    CX = area("CX", [P, KT, T], 32)
    MASKF = area("MASKF", [P, len(LEVELS), P], 40)
    CBX = area("CBX", [P, D], 44)
    x_in = load(SY, "x", XR[:, :, :], io["xT"])
    ctx_in = load(SY, "ctx", CX[:, :, :], io["ctxT"])
    c_in = [load(SC, "c", CB[:, :], io["c_row"].to_broadcast([P, D])),
            load(SC, "c_ctx", CBX[:, :], io["c_ctx_row"].to_broadcast([P, D]))]
    vec_in = load(SC, "vec", vec[:, :], io["vec"])
    con_in = load(SC, "con", con[:, :], io["con"])
    masks_in = load(SC, "masks", MASKF[:, :, :], io["masks"])

    plan = chunk_plan()
    s_raw = [sem(f"raw{i}") for i in range(NRAW)]
    n_raw = [0] * NRAW
    arrived, raw_free = {}, {}
    split_hi, split_lo = {}, {}
    hi_free = {}
    order = {}
    for n, (name, i, cols) in enumerate(plan):
        order[(name, i)] = n
    slot_of = {}
    nsplit = [0]
    issued = [0]
    prepped = [0]

    def issue_loads(upto):
        while issued[0] < min(upto, len(plan)):
            n = issued[0]
            name, i, cols = plan[n]
            s = n % NRAW
            if n >= NRAW:
                SY.wait(*raw_free[n - NRAW])
            SY.go(lambda e, s=s, name=name, i=i, cols=cols:
                  e.dma_start(raw[s][:, 0:cols], io[name][i]).then_inc(s_raw[s], 16))
            n_raw[s] += 16
            arrived[n] = (s_raw[s], n_raw[s])
            issued[0] += 1

    def lo_engine(name, i):
        return PO if name in ("w_in", "w_a", "w_b", "w_out", "ffn_up", "w_in_2", "w_out_2") else VE

    def prep(n):
        name, i, cols = plan[n]
        r = raw[n % NRAW]
        if name == "ada_hi":
            VE.wait(arrived[n], c_rows[0])
            for j in range(2):
                f = 2 * i + j
                m = VE.do(lambda e, j=j, f=f: e.tensor_tensor_reduce(
                    out=r[:, j * D:(j + 1) * D], in0=r[:, j * D:(j + 1) * D], in1=CB[:, :], scale=1.0, scalar=0.0,
                    op0=ALU.mult, op1=ALU.add, accum_out=MODX[:, f:f + 1]))
            side_done[i] = m
            raw_free[n] = [m]
            issue_loads(n + NRAW + 1)
            return
        s = nsplit[0] % NHI
        nsplit[0] += 1
        slot_of[n] = s
        h, l = whi[s], wlo[s]
        prev = hi_free.get(s, [])
        SC.wait(arrived[n], *prev)
        a = SC.do(lambda e: e.activation(h[:, 0:cols], r[:, 0:cols], ACT.Copy))
        L = lo_engine(name, i)
        L.wait(arrived[n], a, *prev)
        b = L.do(lambda e: e.tensor_tensor(l[:, 0:cols], r[:, 0:cols], h[:, 0:cols].bitcast(F32), ALU.subtract))
        split_hi[n], split_lo[n] = a, b
        raw_free[n] = [a, b]
        issue_loads(n + NRAW + 1)

    def prep_upto(n):
        while prepped[0] <= min(n, len(plan) - 1):
            prep(prepped[0])
            prepped[0] += 1

    side_done = {}

    def chunk(name, i):
        n = order[(name, i)]
        look, more = n, NHI - 1
        while more and look + 1 < len(plan):
            look += 1
            more -= plan[look][0] != "ada_hi"
        prep_upto(look)
        PE.wait(split_hi[n], split_lo[n])
        s = slot_of[n]
        return s, whi[s], wlo[s]

    def chunk_done(s, mark):
        hi_free[s] = [mark]

    def mm3(out, h, l, col, xh, xl, first, last, tell=False):
        PE.go(lambda e: e.matmul(out, h[:, col:col + P], xh, start=first, stop=False))
        PE.go(lambda e: e.matmul(out, h[:, col:col + P], xl, start=False, stop=False))
        op = lambda e: e.matmul(out, l[:, col:col + P], xh, start=False, stop=last)
        return PE.do(op) if last or tell else PE.go(op)

    m_ones = PO.do(lambda e: e.memset(ones[:, :], 1.0))
    m_eps = PO.do(lambda e: e.memset(eps[:, :], EPS))
    one128 = ones[:, 0:P]

    issue_loads(NRAW)

    HN = area("HN", [P, 2, KT, T], 72)
    H1h = area("H1h", [P, 2, KT, T], 0, F32R)
    H1l = area("H1l", [P, 2, KT, T], 16, F32R)
    SPARE = [area(f"SPARE{i}", [P, D], 48 + 4 * i) for i in range(2)]
    c_rows = []
    SC.wait(c_in[0])
    c_rows.append(SC.do(lambda e: e.activation(CB[:, :], CB[:, :], ACT.Silu)))
    SC.wait(c_in[1])
    c_rows.append(SC.do(lambda e: e.activation(CBX[:, :], CBX[:, :], ACT.Silu)))
    SC.wait(vec_in)
    c2 = SC.do(lambda e: e.activation(C2[:, :, :], v("c2").rearrange("p (k j) -> p k j", j=2), ACT.Silu))
    SC.wait(x_in, m_eps)
    VE.wait(ctx_in)
    sq = [SC.do(lambda e: e.activation(HN[:, 0, :, :], XR[:, :, :], ACT.Square)),
          VE.do(lambda e: e.tensor_tensor(HN[:, 1, :, :], CX[:, :, :], CX[:, :, :], ALU.mult))]

    def column(b, i, sq, first, last):
        op = lambda e: e.matmul(bank[b][:, i:i + 1], sq, ones[:, 0:1], start=first, stop=last, skip_group_check=True)
        return PE.do(op) if last else PE.go(op)

    def rstd_columns(b, n, width, at, after):
        SC.wait(after)
        m = SC.do(lambda e: e.activation(RC[:, at:at + n], bank[b][:, 0:n], ACT.Sqrt, bias=eps[:, 0:1],
                                         scale=1.0 / width))
        freed[b].append(m)
        VE.wait(m)
        return VE.do(lambda e: e.reciprocal(RC[:, at:at + n], RC[:, at:at + n]))

    def rows(b, cols, ready):
        PE.wait(ready, con_in)
        for i, col in enumerate(cols):
            op = lambda e, i=i, col=col: e.matmul(bank[b][:, i * P:(i + 1) * P], col, ident, start=True, stop=True)
            m = PE.do(op) if i == len(cols) - 1 else PE.go(op)
        return m

    def wide(i):
        return RC[:, i:i + 1].to_broadcast([P, P])

    PE.wait(*sq, m_ones)
    b = take("m")
    for x in range(2):
        for t in range(2):
            for k in range(KT):
                m = column(b, 2 * x + t, HN[:, x, k, t * P:(t + 1) * P], (x, t, k) == (0, 0, 0),
                           (x, t, k) == (1, 1, KT - 1))
    rc = rstd_columns(b, 4, D, 0, m)
    br = take("m")
    rs = rows(br, [wide(i) for i in range(4)], rc)
    VE.wait(rs)
    hn = [VE.do(lambda e, x=x, src=src, br=br: e.tensor_tensor(
        HN[:, x, :, :], src[:, :, :], bank[br][:, x * T:(x + 1) * T].unsqueeze(1).to_broadcast([P, KT, T]), ALU.mult))
        for x, src in enumerate((XR, CX))]
    freed[br].append(hn[1])

    PE.wait(c2)
    VE.wait(*c_rows)
    bm = take("m")
    modp = bank[bm][:, 0:16].rearrange("p (f j) -> p f j", j=2)
    spare_free = [[], []]
    for i in range(4):
        n = order[("ada_s", i)]
        VE.wait(arrived[n])
        r = raw[n % NRAW]
        for f in range(2):
            VE.wait(*spare_free[f])
            for j, (row, out) in enumerate(((CB, SPARE[f][:, :]), (CBX, r[:, f * D:(f + 1) * D]))):
                scale_done = VE.do(lambda e, r=r, f=f, j=j, i=i, row=row, out=out: e.tensor_tensor_reduce(
                    out=out, in0=r[:, f * D:(f + 1) * D], in1=row[:, :], scale=1.0, scalar=0.0,
                    op0=ALU.mult, op1=ALU.add, accum_out=MOD[:, 8 + 2 * i + f, j:j + 1]))
                if j == 0:
                    spare_free[f] = [scale_done]
        raw_free[n] = [scale_done]
        issue_loads(n + NRAW + 1)
        n = order[("ada_p", i)]
        PE.wait(arrived[n])
        r = raw[n % NRAW]
        for f in range(2):
            for k in range(KT):
                op = lambda e, r=r, f=f, k=k, i=i: e.matmul(
                    modp[:, 2 * i + f, :], r[:, (f * KT + k) * P:(f * KT + k + 1) * P], C2[:, k, :],
                    start=k == 0, stop=k == KT - 1)
                m = PE.do(op) if f == 1 and k == KT - 1 else PE.go(op)
        raw_free[n] = [m]
        issue_loads(n + NRAW + 1)
    prepped[0] = 8
    prep_upto(9)
    VE.wait(vec_in, scale_done)
    both = lambda ap: ap.unsqueeze(2).to_broadcast([P, KT, 2])
    a = VE.do(lambda e: e.tensor_tensor(MOD[:, 8:16, :], MOD[:, 8:16, :], both(v("ada_b", 8, 8)), ALU.add))
    VE.wait(a)
    a1 = VE.do(lambda e: e.scalar_tensor_tensor(A1[:, :, :], MOD[:, 8:16, :], 1.0, both(v("norm1_g")), ALU.add,
                                                ALU.mult))
    VE.wait(m)
    m = VE.do(lambda e: e.tensor_tensor(MOD[:, 0:8, :], modp, both(v("ada_b", 0, 8)), ALU.add))
    freed[bm].append(m)
    VE.wait(m, a1, *hn)
    his, h1 = [[], []], [[], []]
    for x in range(2):
        for k in range(KT + 1):
            if k < KT:
                m = VE.do(lambda e, k=k, x=x: e.tensor_scalar(HN[:, x, k, :], HN[:, x, k, :], A1[:, k, x:x + 1],
                                                              MOD[:, k, x:x + 1], ALU.mult, ALU.add))
                SC.wait(m)
                his[x].append(SC.do(lambda e, k=k, x=x: e.activation(H1h[:, x, k, :], HN[:, x, k, :], ACT.Copy)))
            if k:
                VE.wait(his[x][k - 1])
                h1[x].append(VE.do(lambda e, k=k - 1, x=x: e.tensor_tensor(
                    H1l[:, x, k, :], HN[:, x, k, :], H1h[:, x, k, :].bitcast(F32), ALU.subtract)))
    h1_all = [his[1][-1], h1[1][-1]]

    VE.wait(masks_in)
    m_masks = VE.do(lambda e: e.tensor_copy(masks[:, :, :], MASKF[:, :, :]))

    lbr = v("hg_lb").rearrange("p (r h) -> p r h", r=2)
    LBE2 = LBE[:, :].rearrange("p (r h) -> p r h", r=2)
    m = VE.do(lambda e: e.tensor_tensor(LBM[:, :], lbr[:, 0, :], lbr[:, 1, :], ALU.max))
    VE.wait(m)
    m = VE.do(lambda e: e.tensor_tensor(LBE2, lbr, LBM[:, :].unsqueeze(1).to_broadcast([P, 2, 4]), ALU.subtract))
    SC.wait(m)
    m = SC.do(lambda e: e.activation(LBE[:, :], LBE[:, :], ACT.Exp))
    VE.wait(m)
    m = VE.do(lambda e: e.tensor_tensor(LBM[:, :], LBE2[:, 0, :], LBE2[:, 1, :], ALU.add))
    VE.wait(m)
    m = VE.do(lambda e: e.reciprocal(LBM[:, :], LBM[:, :]))
    VE.wait(m)
    m = VE.do(lambda e: e.tensor_tensor(LB[:, :], LBE2[:, 0, :], LBM[:, :], ALU.mult))
    VE.wait(m)
    lb_ready = VE.do(lambda e: e.tensor_scalar(LB1[:, :], LB[:, :], -1.0, 1.0, ALU.mult, ALU.add))

    F = area("F", [P, 2, 2, NH, T], 32)
    K = area("K", [P, 2, 2, NH, T], 48)
    VT = area("VT", [P, 2, NH, T], 64)
    f_ready = {0: [], 1: []}
    vt_ready = []
    Q = area("Q", [P, NH, T], 96)
    XS = area("XS", [P, 2, NH, T], 72)
    FU = area("FU", [P, NH, T], 76)
    SG = area("SG", [P, NH, T], 88)
    GA = area("GA", [P, 2 * NH, T], 8)
    GB = area("GB", [P, 2 * NH, T], 24)
    QF = area("QF", [P, 2, NH, T], 40)
    A = area("A", [P, 2, NH, T], 56)
    VX = area("VX", [P, 2, NH, P], 68)
    KS = area("KS", [P, NH, T], 72)
    KTT = area("KTT", [P, 2, 2, NH, P], 80)
    VC = area("VC", [P, 2, NH, P], 88)
    ST = area("ST", [P, 2, NH, P], 92)
    T1 = area("T1", [P, 2, NH, T], 80)
    YFh = area("YFh", [P, NH, T], 72, F32R)
    YFl = area("YFl", [P, NH, T], 76, F32R)
    SQo = area("SQo", [P, NH, T], 80)
    RSo = area("RSo", [P, NH, T], 84)
    ON = area("ON", [P, NH, T], 64)
    YHh = area("YHh", [P, NH, T], 48, F32R)
    YHl = area("YHl", [P, NH, T], 52, F32R)
    MGh = area("MGh", [P, KT, T], 0, F32R)
    MGl = area("MGl", [P, KT, T], 16, F32R)
    kk, kc = {}, []

    def both_inputs(i):
        s, h, l = chunk("w_in", i)
        for j in range(2):
            b = take("g")
            for k in range(KT):
                PE.wait(his[1][k], h1[1][k])
                m = mm3(bank[b][:, :].rearrange("p (x t) -> p x t", x=2), h, l, (j * KT + k) * P,
                        H1h[:, :, k, :], H1l[:, :, k, :], k == 0, k == KT - 1)
            if j == 1:
                chunk_done(s, m)
            f = 2 * (i - 2) + j
            d, head = f // 4, f % 4
            src = bank[b][:, :].rearrange("p (x t) -> p x t", x=2)
            SC.wait(m, *hn, m_masks, scale_done)
            if d == 2:
                a = SC.do(lambda e, src=src, head=head: e.activation(VT[:, :, head, :], src, ACT.Copy))
                vt_ready.append(a)
            else:
                a = SC.do(lambda e, src=src, d=d, head=head: e.activation(F[:, :, d, head, :], src, ACT.Sigmoid))
                VE.wait(a, lb_ready)
                f_ready[d].append(VE.do(lambda e, d=d, head=head: e.tensor_scalar(
                    F[:, :, d, head, :], F[:, :, d, head, :], LB1[:, head:head + 1], LB[:, head:head + 1],
                    ALU.mult, ALU.add)))
            freed[b].append(a)
        return m

    def ctx_decay():
        PO.wait(*h1_all)
        m_xs = [PO.do(lambda e: e.memset(XS[:, 0, :, T - 1:T], 1.0)),
                PO.do(lambda e: e.memset(XS[:, 1, :, 0:1], 1.0))]
        for x in (1, 0):
            for d in range(2):
                VE.wait(f_ready[d][-1])
                kk[x, d] = VE.do(lambda e, x=x, d=d: e.tensor_scalar(K[:, x, d, :, :], F[:, x, d, :, :], -1.0, 1.0,
                                                                     ALU.mult, ALU.add))
        VE.wait(*m_xs, m_ones)
        for d in range(2):
            for head in range(NH):
                if d == 0:
                    o, i0 = XS[:, 0, head, T - 2::-1], F[:, 1, 0, head, T - 1:0:-1]
                else:
                    o, i0 = XS[:, 1, head, 1:T], F[:, 1, 1, head, 0:T - 1]
                m = VE.do(lambda e, o=o, i0=i0: e.tensor_tensor_scan(o, i0, ones[:, 0:T - 1], 1.0, ALU.mult,
                                                                     ALU.mult))
            VE.wait(m, kk[1, d])
            kc.append(VE.do(lambda e, d=d: e.tensor_tensor(K[:, 1, d, :, :], K[:, 1, d, :, :], XS[:, d, :, :],
                                                           ALU.mult)))

    def pair(name, i, xh, xl, nk=KT, ready=()):
        s, h, l = chunk(name, i)
        b = take("g")
        PE.wait(*ready)
        for j in range(2):
            for k in range(nk):
                m = mm3(bank[b][:, j * T:(j + 1) * T], h, l, (j * nk + k) * P, xh[:, k, :], xl[:, k, :],
                        k == 0, k == nk - 1)
        chunk_done(s, m)
        return b, m

    def evict(b, m, out, func=ACT.Copy, after=()):
        SC.wait(m, *after)
        a = SC.do(lambda e: e.activation(out, bank[b][:, :], func))
        freed[b].append(a)
        return a

    def flat(ap):
        return ap.rearrange("p a b -> p (a b)")

    hx, hl = H1h[:, 0, :, :], H1l[:, 0, :, :]
    marks = {}

    def transposes(srcs, outs, after, before):
        PE.wait(*after)
        done = []
        for four, out in zip(srcs, outs):
            b = take("m")
            for n, src in enumerate(four):
                op = lambda e, b=b, n=n, src=src: e.transpose(bank[b][:, n * P:(n + 1) * P], src, ident)
                m = PE.do(op) if n == len(four) - 1 else PE.go(op)
            done.append(evict(b, m, out, after=before))
        return done

    def ctx_turn():
        srcs, outs = [], []
        for d in range(2):
            for t in range(2):
                srcs.append([K[:, 1, d, h, t * P:(t + 1) * P] for h in range(NH)])
                outs.append(flat(KTT[:, d, t, :, :]))
        marks["turned"] = transposes(srcs, outs, kc, h1_all)

    def v_turn():
        for x, name, dst in ((1, "vc", VC), (0, "vx", VX)):
            srcs = [[VT[:, x, h, t * P:(t + 1) * P] for h in range(NH)] for t in range(2)]
            marks[name] = transposes(srcs, [flat(dst[:, t, :, :]) for t in range(2)], vt_ready,
                                     marks["turned"] + marks.get("vc", []))

    def ctx_state():
        PE.wait(*marks["turned"], *marks["vc"])
        st = []
        for d in range(2):
            b = take("m")
            for h in range(NH):
                for t in range(2):
                    op = lambda e, b=b, d=d, h=h, t=t: e.matmul(
                        bank[b][:, h * P:(h + 1) * P], KTT[:, d, t, h, :], VC[:, t, h, :], start=t == 0, stop=t == 1)
                    m = PE.do(op) if (h, t) == (NH - 1, 1) else PE.go(op)
            st.append(evict(b, m, flat(ST[:, d, :, :])))
        marks["state"] = st
        marks["state_pe"] = m

    def x_start():
        VE.wait(*marks["q"], *kc)
        marks["qf"] = [VE.do(lambda e, d=d: e.tensor_tensor(QF[:, d, :, :], Q[:, :, :], F[:, 0, d, :, :], ALU.mult))
                       for d in range(2)]
        VE.wait(kk[0, 0], kk[0, 1])
        marks["ks"] = VE.do(lambda e: e.tensor_tensor(KS[:, :, :], K[:, 0, 0, :, :], K[:, 0, 1, :, :], ALU.add))

    def diagonal():
        PE.wait(marks["ks"], *marks["q"])
        marks["a"] = []
        for t in range(2):
            b = take("m")
            cols = slice(t * P, (t + 1) * P)
            for h in range(NH):
                op = lambda e, b=b, h=h, cols=cols: e.matmul(bank[b][:, h * P:(h + 1) * P], KS[:, h, cols],
                                                            Q[:, h, cols], start=True, stop=True)
                m = PE.do(op) if h == NH - 1 else PE.go(op)
            SC.wait(m, *marks["turned"])
            a = SC.do(lambda e, b=b, t=t: e.activation(A[:, t, :, t * P:(t + 1) * P],
                                                       bank[b][:, :].rearrange("p (h t) -> p h t", h=NH), ACT.Copy))
            freed[b].append(a)
            marks["a"].append(a)
        marks["diag_pe"] = m

    def halves(ap, h):
        return ap.rearrange("p (b two h) -> p b two h", two=2, h=h)

    def level(li):
        h = LEVELS[li]
        PE.wait(*marks["qf"])
        PE.wait(*marks.get("kf", []))
        got = []
        for t in range(2):
            b = take("m")
            cols = slice(t * P, (t + 1) * P)
            for hd in range(NH):
                o = halves(bank[b][:, hd * P:(hd + 1) * P], h)
                qr = halves(QF[:, 0, hd, cols], h)
                ql = halves(QF[:, 1, hd, cols], h)
                PE.go(lambda e, o=o, qr=qr, hd=hd, cols=cols: e.matmul(o[:, :, 1, :], K[:, 0, 0, hd, cols],
                                                                      qr[:, :, 1, :], start=True, stop=True))
                op = lambda e, o=o, ql=ql, hd=hd, cols=cols: e.matmul(o[:, :, 0, :], K[:, 0, 1, hd, cols],
                                                                     ql[:, :, 0, :], start=True, stop=True)
                m = PE.do(op) if hd == NH - 1 else PE.go(op)
            got.append((b, m))
        for t, (b, m) in enumerate(got):
            VE.wait(m, *marks["a"])
            a = VE.do(lambda e, b=b, t=t: e.copy_predicated(
                A[:, t, :, t * P:(t + 1) * P],
                masks[:, li, :].unsqueeze(1).to_broadcast([P, NH, P]),
                bank[b][:, :].rearrange("p (h t) -> p h t", h=NH)))
            freed[b].append(a)
            marks["ap"] = a
        grow(h, got[-1][1])

    def blocks(d, h):
        f = F[:, 0, d, :, :].rearrange("p a t -> p (a t)")
        return f.rearrange("p (b two h) -> p b two h", two=2, h=h)[:, :, :, 0]

    def grow(h, read):
        nb = NH * T // (2 * h)
        VE.wait(read)
        q0, q1 = (halves(QF[:, d, :, :].rearrange("p a t -> p (a t)"), h) for d in range(2))
        k0, k1 = (halves(K[:, 0, d, :, :].rearrange("p a t -> p (a t)"), h) for d in range(2))
        f0, f1 = blocks(0, h), blocks(1, h)

        def times(x, f):
            return VE.do(lambda e: e.tensor_tensor(x, x, f.unsqueeze(2).to_broadcast([P, nb, h]), ALU.mult))

        VE.wait(*marks.get("bp", f_ready[0] + f_ready[1]))
        marks["qf"] = [times(q0[:, :, 1, :], f0[:, :, 0]), times(q1[:, :, 0, :], f1[:, :, 1])]
        if 2 * h < T:
            marks["kf"] = [times(k0[:, :, 0, :], f0[:, :, 1]), times(k1[:, :, 1, :], f1[:, :, 0])]
            VE.wait(*marks["kf"])
            marks["bp"] = [VE.do(lambda e, f=f: e.tensor_tensor(f[:, :, 0], f[:, :, 0], f[:, :, 1], ALU.mult))
                           for f in (f0, f1)]

    def level_wide():
        PE.wait(*marks["qf"], *marks["kf"])
        marks["aw"] = []
        for d in range(2):
            b = take("m")
            ks, ts = (slice(0, P), slice(P, T)) if d == 0 else (slice(P, T), slice(0, P))
            for h in range(NH):
                op = lambda e, b=b, d=d, h=h, ks=ks, ts=ts: e.matmul(
                    bank[b][:, h * P:(h + 1) * P], K[:, 0, d, h, ks], QF[:, d, h, ts], start=True, stop=True)
                m = PE.do(op) if h == NH - 1 else PE.go(op)
            SC.wait(m, *marks["turned"])
            a = SC.do(lambda e, b=b, d=d, ts=ts: e.activation(
                A[:, d, :, ts], bank[b][:, :].rearrange("p (h t) -> p h t", h=NH), ACT.Copy))
            freed[b].append(a)
            marks["aw"].append(a)
        marks["wide_pe"] = m
        grow(P, m)

    def outputs():
        PE.wait(marks["ap"], *marks["aw"], *marks["a"], *marks["qf"], *marks["state"], *marks["vx"])
        marks["o"] = []
        for hp in range(2):
            b = take("m")
            for j in range(2):
                h = 2 * hp + j
                o = bank[b][:, j * T:(j + 1) * T]
                for t in range(2):
                    PE.go(lambda e, o=o, h=h, t=t: e.matmul(o, VX[:, t, h, :], A[:, t, h, :], start=t == 0,
                                                            stop=False))
                PE.go(lambda e, o=o, h=h: e.matmul(o, ST[:, 0, h, :], QF[:, 0, h, :], start=False, stop=False))
                op = lambda e, o=o, h=h: e.matmul(o, ST[:, 1, h, :], QF[:, 1, h, :], start=False, stop=True)
                m = PE.do(op) if j == 1 else PE.go(op)
            marks["o"].append((b, m))

    def readout_squares():
        for hp, (b, m) in enumerate(marks["o"]):
            a = evict(b, m, flat(ON[:, 2 * hp:2 * hp + 2, :]), after=marks["vx"])
            SC.wait(a, *marks["t1_free"])
            a = SC.do(lambda e, hp=hp: e.activation(SQo[:, 2 * hp:2 * hp + 2, :], ON[:, 2 * hp:2 * hp + 2, :],
                                                    ACT.Square))
            marks["sqo", hp] = a

    def readout_columns():
        b = take("m")
        for h in range(NH):
            PE.wait(marks["sqo", h // 2])
            for t in range(2):
                m = column(b, 2 * h + t, SQo[:, h, t * P:(t + 1) * P], h + t == 0, h + t == NH)
        marks["rco"] = rstd_columns(b, 8, P, 8, m)

    def readout_norm():
        for hp in range(2):
            b = take("m")
            r = rows(b, [wide(8 + 4 * hp + i) for i in range(4)], marks["rco"])
            VE.wait(r, marks["sg"])
            for j in range(2):
                h = 2 * hp + j
                g = VE.do(lambda e, h=h, b=b, j=j: e.scalar_tensor_tensor(
                    RSo[:, h, :], bank[b][:, j * T:(j + 1) * T], v("onorm", h, 1), SG[:, h, :], ALU.mult, ALU.mult))
            freed[b].append(g)
            VE.wait(g)
            y = VE.do(lambda e, hp=hp: e.tensor_tensor(ON[:, 2 * hp:2 * hp + 2, :], ON[:, 2 * hp:2 * hp + 2, :],
                                                       RSo[:, 2 * hp:2 * hp + 2, :], ALU.mult))
            SC.wait(y, marks["wide_pe"])
            yh = SC.do(lambda e, hp=hp: e.activation(YHh[:, 2 * hp:2 * hp + 2, :], ON[:, 2 * hp:2 * hp + 2, :],
                                                     ACT.Copy))
            VE.wait(yh)
            yl = VE.do(lambda e, hp=hp: e.tensor_tensor(YHl[:, 2 * hp:2 * hp + 2, :], ON[:, 2 * hp:2 * hp + 2, :],
                                                        YHh[:, 2 * hp:2 * hp + 2, :].bitcast(F32), ALU.subtract))
            marks["yh", hp] = [yh, yl]

    dft_l = c("dft_l").rearrange("p (t s n) -> p t s n", t=2, s=2)

    def fourier_1():
        PE.wait(*marks["fu"])
        marks["t1"] = []
        for t in range(2):
            for gp in range(2):
                b = take("m")
                for j in range(2):
                    op = lambda e, b=b, t=t, g=2 * gp + j, j=j: e.matmul(
                        bank[b][:, j * T:(j + 1) * T], FU[:, g, t * P:(t + 1) * P], c("dft_c"), start=True, stop=True)
                    m = PE.do(op) if j == 1 else PE.go(op)
                marks["t1"].append(evict(b, m, flat(T1[:, t, 2 * gp:2 * gp + 2, :]),
                                         after=[marks["state_pe"]]))
        marks["fu_free"] = m

    def fourier_2():
        PE.wait(*marks["t1"])
        for gp in range(2):
            b = take("m")
            for j in range(2):
                g = 2 * gp + j
                for n, (t, s) in enumerate([(0, 0), (1, 0), (0, 1), (1, 1)]):
                    op = lambda e, b=b, g=g, j=j, t=t, s=s, n=n: e.matmul(
                        bank[b][:, j * T:(j + 1) * T], T1[:, t, g, s * P:(s + 1) * P], dft_l[:, t, s, :],
                        start=n == 0, stop=n == 3)
                    m = PE.do(op) if (j, n) == (1, 3) else PE.go(op)
            a = evict(b, m, flat(YFh[:, 2 * gp:2 * gp + 2, :]), after=[marks["diag_pe"], marks["fu_free"]])
            VE.wait(a)
            y = VE.do(lambda e, b=b, gp=gp: e.tensor_tensor(
                flat(YFl[:, 2 * gp:2 * gp + 2, :]), bank[b][:, :], flat(YFh[:, 2 * gp:2 * gp + 2, :]).bitcast(F32),
                ALU.subtract))
            freed[b].append(y)
            marks["yf", gp] = [a, y]
        marks["t1_free"] = [m]

    for i in range(20):
        if 2 <= i < 8:
            m = h1c_done = both_inputs(i)
        else:
            s, h, l = chunk("w_in", i)
            b = take("g")
            for j in range(2):
                for k in range(KT):
                    PE.wait(his[0][k], h1[0][k])
                    m = mm3(bank[b][:, j * T:(j + 1) * T], h, l, (j * KT + k) * P, hx[:, k, :], hl[:, k, :],
                            k == 0, k == KT - 1)
            chunk_done(s, m)
        if i < 2:
            marks.setdefault("q", []).append(evict(b, m, flat(Q[:, 2 * i:2 * i + 2, :]), ACT.Silu))
        elif i < 8:
            if i == 5:
                ctx_decay()
                x_start()
        elif i < 10:
            marks.setdefault("fu", []).append(
                evict(b, m, flat(FU[:, 2 * (i - 8):2 * (i - 8) + 2, :]), after=kc))
        elif i < 12:
            marks["sg"] = evict(b, m, flat(SG[:, 2 * (i - 10):2 * (i - 10) + 2, :]), ACT.Silu,
                                after=[marks["state_pe"]])
        elif i < 16:
            marks["ga"] = evict(b, m, flat(GA[:, 2 * (i - 12):2 * (i - 12) + 2, :]), ACT.Sigmoid, after=[h1c_done])
        else:
            marks["gb"] = evict(b, m, flat(GB[:, 2 * (i - 16):2 * (i - 16) + 2, :]), ACT.Sigmoid, after=[h1c_done])
        if i == 6:
            ctx_turn()
            diagonal()
            level(0)
        elif i == 7:
            level(1)
        elif i == 8:
            v_turn()
            level(2)
        elif i == 9:
            ctx_state()
            level(3)
        elif i == 10:
            fourier_1()
            level(4)
        elif i == 11:
            level(5)
        elif i == 12:
            fourier_2()
            level(6)
        elif i == 13:
            level_wide()
        elif i == 14:
            outputs()
            readout_squares()
        elif i == 15:
            readout_columns()
        elif i == 16:
            readout_norm()
    hx_done = m

    def quad(name, i, xh, xl):
        s, h, l = chunk(name, i)
        out = []
        for jp in range(2):
            b = take("g")
            for j in range(2):
                for k in range(NH):
                    m = mm3(bank[b][:, j * T:(j + 1) * T], h, l, ((2 * jp + j) * NH + k) * P, xh[:, k, :], xl[:, k, :],
                            k == 0, k == NH - 1)
            out.append((b, m))
        chunk_done(s, m)
        return out

    def gated(b, m, g, ready, f):
        VE.wait(m, ready)
        a = VE.do(lambda e: e.tensor_tensor(flat(g[:, f:f + 2, :]), bank[b][:, :], flat(g[:, f:f + 2, :]), ALU.mult))
        freed[b].append(a)
        return a

    PE.wait(*marks["yf", 0], *marks["yf", 1])
    ya = {}
    for i in range(2):
        for jp, (b, m) in enumerate(quad("w_a", i, YFh, YFl)):
            f = 4 * i + 2 * jp
            ya[f] = gated(b, m, GA, marks["ga"], f)
    PE.wait(*marks["yh", 0], *marks["yh", 1])
    mg = []
    for i in range(2):
        for jp, (b, m) in enumerate(quad("w_b", i, YHh, YHl)):
            f = 4 * i + 2 * jp
            yb = gated(b, m, GB, marks["gb"], f)
            VE.wait(yb, ya[f])
            s = VE.do(lambda e, f=f: e.tensor_tensor(GA[:, f:f + 2, :], GA[:, f:f + 2, :], GB[:, f:f + 2, :],
                                                     ALU.add))
            SC.wait(s, hx_done)
            a = SC.do(lambda e, f=f: e.activation(MGh[:, f:f + 2, :], GA[:, f:f + 2, :], ACT.Copy))
            VE.wait(a)
            y = VE.do(lambda e, f=f: e.tensor_tensor(MGl[:, f:f + 2, :], GA[:, f:f + 2, :],
                                                     MGh[:, f:f + 2, :].bitcast(F32), ALU.subtract))
            mg += [a, y]

    mod_ready = {}

    def mods(a, n):
        prep_upto(max(order[("ada_hi", i)] for i in range(a // 2, (a + n) // 2)))
        VE.wait(side_done[(a + n) // 2 - 1])
        mod_ready[a] = VE.do(lambda e: e.tensor_tensor(MODX[:, a:a + n], MODX[:, a:a + n], v("ada_b", 16 + a, n),
                                                       ALU.add))

    mods(0, 24)
    VE.wait(mod_ready[0])
    a2 = VE.do(lambda e: e.scalar_tensor_tensor(A2[:, :], MODX[:, 16:24], 1.0, v("norm2_g"), ALU.add, ALU.mult))

    def add_to_x(b, m, f, gate):
        VE.wait(m)
        for j in range(2):
            g = 1.0 if gate is None else MODX[:, gate + f + j:gate + f + j + 1]
            a = VE.do(lambda e, j=j, g=g: e.scalar_tensor_tensor(
                XR[:, f + j, :], bank[b][:, j * T:(j + 1) * T], g, XR[:, f + j, :], ALU.mult, ALU.add))
        freed[b].append(a)
        return a

    def squares(sq, f, after, gain=None):
        SC.wait(after)
        if gain is None:
            return SC.do(lambda e: e.activation(sq[:, f:f + 2, :], XR[:, f:f + 2, :], ACT.Square))
        for k in (f, f + 1):
            m = SC.do(lambda e, k=k: e.activation(sq[:, k, :], XR[:, k, :], ACT.Square, scale=gain[:, k:k + 1]))
        return m

    def square_columns(b, at, sq, f, ready, opens):
        PE.wait(ready)
        for k in (f, f + 1):
            for t in range(2):
                m = column(b, at + t, sq[:, k, t * P:(t + 1) * P], opens and k == 0 and t == 0,
                           k == KT - 1 and t == 1)
        return m

    def warm(func):
        SC.do(lambda e: e.activation(warmed[:, 0:1], eps[:, 0:1], func))

    def normed(rs, b, gain, shift, tmp, xh, xl):
        out = []
        VE.wait(rs)
        hs = []
        for k in range(KT + 1):
            if k < KT:
                t = VE.do(lambda e, k=k: e.scalar_tensor_tensor(tmp[:, k, :], XR[:, k, :], gain[:, k:k + 1],
                                                                bank[b][:, 0:T], ALU.mult, ALU.mult))
                SC.wait(t)
                if shift is None:
                    hs.append(SC.do(lambda e, k=k: e.activation(xh[:, k, :], tmp[:, k, :], ACT.Copy)))
                else:
                    hs.append(SC.do(lambda e, k=k: e.activation(xh[:, k, :], tmp[:, k, :], ACT.Identity,
                                                                bias=shift[:, k:k + 1])))
                if k == KT - 1:
                    freed[b].append(t)
            if k:
                j = k - 1
                VE.wait(hs[j])
                if shift is None:
                    op = lambda e, k=j: e.tensor_tensor(xl[:, k, :], tmp[:, k, :], xh[:, k, :].bitcast(F32),
                                                        ALU.subtract)
                else:
                    op = lambda e, k=j: e.scalar_tensor_tensor(xl[:, k, :], tmp[:, k, :], shift[:, k:k + 1],
                                                               xh[:, k, :].bitcast(F32), ALU.add, ALU.subtract)
                out.append([hs[j], VE.do(op)])
        return out

    def pair_when(name, i, xh, xl, ready, ks=range(KT)):
        s, h, l = chunk(name, i)
        b = take("g")
        for j in range(2):
            for n, k in enumerate(ks):
                PE.wait(*ready[k])
                m = mm3(bank[b][:, j * T:(j + 1) * T], h, l, (j * KT + k) * P, xh[:, k, :], xl[:, k, :],
                        n == 0, n == KT - 1)
        chunk_done(s, m)
        return b, m

    SQ1 = area("SQ1", [P, KT, T], 48)
    TMP1 = area("TMP1", [P, KT, T], 40)
    H2h = area("H2h", [P, KT, T], 24, F32R)
    H2l = area("H2l", [P, KT, T], 32, F32R)
    PE.wait(*mg)
    bs = take("m")
    warm(ACT.Sqrt)
    sq = {}
    for i in range(4):
        b, m = pair("w_out", i, MGh, MGl)
        sq[i] = squares(SQ1, 2 * i, add_to_x(b, m, 2 * i, 0))
        if i:
            square_columns(bs, 0, SQ1, 2 * i - 2, sq[i - 1], i == 1)
    merge_done = m
    m = square_columns(bs, 0, SQ1, 6, sq[3], False)
    rc = rstd_columns(bs, 2, D, 0, m)
    warm(ACT.Silu)
    br = take("m")
    h2 = normed(rows(br, [wide(0), wide(1)], rc), br, A2, MODX[:, 8:16], TMP1, H2h, H2l)

    BI = area("BI", [P, 8, 384], 72)
    PW = area("PW", [P, 2, P], 96)
    SY.wait(merge_done)
    bias_in = load(SY, "bias", BI[:, :, :], io["bias"])
    pw_in = load(SY, "pool_w", PW[:, :, :], io["pool_w"])
    NA = 8
    AH = area("AH", [P, NA, T], 0, F32R)
    AL = area("AL", [P, NA, T], 8, F32R)
    Y = [area(f"Y{i}", [P, 2, T], 56 + 2 * i) for i in range(2)]
    SI = [area(f"SI{i}", [P, T], 60 + i) for i in range(2)]
    AT = [area(f"AT{i}", [P, T], 62 + i) for i in range(2)]
    cw = v("conv_w").rearrange("p (f w) -> p f w", w=9)
    taps = [(dr, dc) for dr in (0, -1, 1) for dc in (0, -1, 1) if (dr, dc) != (0, 0)]
    ring["m"] = [3]
    acc = [claim(b) for b in (4, 5, 6, 7)]
    a_done, a_read, conv_done, at_done, ah_done = {}, {}, {}, {}, {}
    y_free = [[], []]

    def up(i):
        b, m = pair_when("ffn_up", i, H2h, H2l, h2)
        y = Y[i % 2]
        SC.wait(m, *y_free[i % 2])
        for s in range(2):
            f = i + 22 * s
            mid = SC.do(lambda e, s=s, f=f: e.activation(
                y[:, s, :], bank[b][:, s * T:(s + 1) * T], ACT.Identity, bias=v("conv_b", f, 1), scale=cw[:, f, 4:5]))
        VE.wait(mid)
        prev = [mid, mid]
        for dr, dc in taps:
            for s in range(2):
                f = i + 22 * s
                z = bank[b][:, s * T:(s + 1) * T].rearrange("p (r c) -> p r c", c=64)
                o = y[:, s, :].rearrange("p (r c) -> p r c", c=64)
                r0, r1, c0, c1 = max(0, -dr), min(4, 4 - dr), max(0, -dc), min(64, 64 - dc)
                w = cw[:, f, 3 * (dr + 1) + dc + 1:3 * (dr + 1) + dc + 2]
                VE.wait(prev[s])
                prev[s] = VE.do(lambda e, o=o[:, r0:r1, c0:c1], z=z[:, r0 + dr:r1 + dr, c0 + dc:c1 + dc], w=w:
                                e.scalar_tensor_tensor(o, z, w, o, ALU.mult, ALU.add))
        freed[b].append(prev[1])
        conv_done[i] = prev

    def gate(i):
        y, si, at = Y[i % 2], SI[i % 2], AT[i % 2]
        SC.wait(conv_done[i][0])
        m = SC.do(lambda e: e.activation(si[:, :], y[:, 0, :], ACT.Silu))
        VE.wait(m, conv_done[i][1])
        at_done[i] = VE.do(lambda e: e.tensor_tensor(at[:, :], si[:, :], y[:, 1, :], ALU.mult))
        y_free[i % 2] = [at_done[i]]
        SC.wait(at_done[i], merge_done, *a_read.get(i - NA, []))
        ah_done[i] = SC.do(lambda e: e.activation(AH[:, i % NA, :], at[:, :], ACT.Copy))

    def gate_low(i):
        at = AT[i % 2]
        VE.wait(ah_done[i], *a_read.get(i - NA, []))
        a_done[i] = [ah_done[i], VE.do(lambda e: e.tensor_tensor(
            AL[:, i % NA, :], at[:, :], AH[:, i % NA, :].bitcast(F32), ALU.subtract))]

    def contract(name, j, xh, xl, slots, ready, last):
        s, h, l = chunk(name, j)
        for kk_ in range(2):
            k = 2 * j + kk_
            PE.wait(*ready[k])
            for f in range(KT):
                out = bank[acc[f // 2]][:, f % 2 * T:(f % 2 + 1) * T]
                col = (kk_ * KT + f) * P
                x0, x1 = xh[:, k % slots, :], xl[:, k % slots, :]
                PE.go(lambda e, out=out, h=h, col=col, x0=x0, k=k, f=f: e.matmul(
                    out, h[:, col:col + P], x0, start=k == 0 and f % 2 == 0, stop=False, skip_group_check=True))
                PE.go(lambda e, out=out, h=h, col=col, x1=x1: e.matmul(
                    out, h[:, col:col + P], x1, start=False, stop=False, skip_group_check=True))
                op = lambda e, out=out, l=l, col=col, x0=x0, end=k == last: e.matmul(
                    out, l[:, col:col + P], x0, start=False, stop=end, skip_group_check=True)
                m = PE.do(op) if f == KT - 1 or (k == last and f % 2) else PE.go(op)
                if k == last and f % 2:
                    acc_done[f // 2] = m
        chunk_done(s, m)
        return m

    acc_done = {}

    def down(j):
        m = contract("ffn_down", j, AH, AL, NA, a_done, 21)
        a_read[2 * j] = a_read[2 * j + 1] = [m]

    for i in range(22):
        up(i)
        if i >= 2:
            gate_low(i - 2)
        if i >= 1:
            gate(i - 1)
        if i >= 5 and i % 2:
            down((i - 5) // 2)
    gate_low(20)
    gate(21)
    down(9)
    gate_low(21)
    down(10)
    down_done = acc_done[3]
    mods(24, 8)
    VE.wait(mod_ready[24])

    SQ2 = area("SQ2", [P, KT, T], 48)
    SQG = area("SQG", [P, KT, T], 64)
    ring["m"] = [3]
    bs = take("m")
    warm(ACT.Sqrt)
    for i in range(4):
        a = add_to_x(acc[i], acc_done[i], 2 * i, 24)
        sq = squares(SQ2, 2 * i, a)
        sqg = squares(SQG, 2 * i, a, v("final_g"))
        square_columns(bs, 0, SQ2, 2 * i, sq, i == 0)
        m = square_columns(bs, 2, SQG, 2 * i, sqg, False)
    ring["m"] = [3, 4, 5, 6, 7]
    SC.wait(m)
    ms = SC.do(lambda e, bs=bs: e.activation(RC[:, 0:2], bank[bs][:, 0:2], ACT.Sqrt, bias=eps[:, 0:1], scale=1.0 / D))
    VE.wait(ms)
    r1 = VE.do(lambda e: e.reciprocal(RC[:, 0:2], RC[:, 0:2]))
    VE.wait(r1)
    t = VE.do(lambda e, bs=bs: e.tensor_tensor(RC[:, 2:4], RC[:, 0:2], bank[bs][:, 2:4], ALU.mult))
    freed[bs] += [ms, t]
    VE.wait(t)
    t = VE.do(lambda e: e.tensor_tensor(RC[:, 2:4], RC[:, 0:2], RC[:, 2:4], ALU.mult))
    SC.wait(t)
    t = SC.do(lambda e: e.activation(RC[:, 2:4], RC[:, 2:4], ACT.Sqrt, bias=eps[:, 0:1], scale=1.0 / D))
    b1 = take("m")
    rs1 = rows(b1, [wide(0), wide(1)], r1)
    VE.wait(t)
    r2 = VE.do(lambda e: e.reciprocal(RC[:, 2:4], RC[:, 2:4]))
    b2 = take("m")
    rs2 = rows(b2, [wide(2), wide(3)], r2)
    VE.wait(rs1)
    for f in range(KT):
        x = VE.do(lambda e, f=f: e.scalar_tensor_tensor(XR[:, f, :], XR[:, f, :], v("final_g", f, 1),
                                                        bank[b1][:, 0:T], ALU.mult, ALU.mult))
    freed[b1].append(x)
    VE.wait(x)

    H3h = area("H3h", [P, KT, T], 24, F32R)
    H3l = area("H3l", [P, KT, T], 32, F32R)
    TMP2 = area("TMP2", [P, KT, T], 40)
    h3 = normed(rs2, b2, v("norm1_g_2"), None, TMP2, H3h, H3l)
    PP = area("PP", [P, 20, T], 0)
    SQq = [area(f"SQq{i}", [P, 2, T], 20 + 2 * i) for i in range(2)]
    PT = area("PT", [P, 3, 8, P], 56)
    VV = area("VV", [P, 2, NH, P], 68)
    SCR = area("SCR", [P, 8 * 384], 84)
    S0 = SCR[:, 0:8 * P].rearrange("p (h s) -> p h s", h=8)
    S1 = SCR[:, 8 * P:8 * 384].rearrange("p (h s) -> p h s", h=8)
    MXh = area("MXh", [P, KT, T], 40, F32R)
    MXl = area("MXl", [P, KT, T], 48, F32R)
    Z = area("Z", [P, 2, T], 24)
    YC = area("YC", [P, 2, T], 26)
    M2 = area("M2", [P, 2, T], 28)
    M4 = area("M4", [P, 2, T], 30)
    M8 = area("M8", [P, T], 32)
    M16 = area("M16", [P, T], 33)
    PM = area("PM", [P, 2, T], 34)
    UP = area("UP", [P, 2, T], 36)
    pp, qk, qk_sq, qk_rc, qk_cols = {}, {}, {}, {}, {}
    halves2 = c("blk")[:, 0:P:64]

    def qk_columns(i):
        PE.wait(qk_sq[i], con_in)
        b = take("m")
        for j in range(2):
            for t in range(2):
                o = 2 * (2 * j + t)
                op = lambda e, j=j, t=t, o=o: e.matmul(bank[b][:, o:o + 2], SQq[i % 2][:, j, t * P:(t + 1) * P],
                                                       halves2, start=True, stop=True)
                m = PE.do(op) if j + t == 2 else PE.go(op)
        qk_cols[i] = m
        qk_rc[i] = rstd_columns(b, 8, 64, 16 + 8 * i, m)

    def qk_norm(i):
        b = take("m")
        at = 16 + 8 * i
        PE.wait(qk_rc[i], con_in)
        for n in range(8):
            half = slice(64 * (n % 2), 64 * (n % 2) + 64)
            col = RC[:, at + n:at + n + 1].to_broadcast([P, 64])
            op = lambda e, n=n, half=half, col=col: e.matmul(bank[b][half, n // 2 * P:(n // 2 + 1) * P], col, ident,
                                                            start=True, stop=True)
            r = PE.do(op) if n == 7 else PE.go(op)
        g = v("q_g") if i < 2 else v("k_g")
        VE.wait(r, pp[i])
        x = PP[:, 2 * i:2 * i + 2, :].rearrange("p a b -> p (a b)")
        qk[i] = VE.do(lambda e: e.scalar_tensor_tensor(x, x, g, bank[b][:, :], ALU.mult, ALU.mult))
        freed[b].append(qk[i])

    S = [S0, S1]
    probs = {}

    def scores():
        PE.wait(*qk.values())
        VE.wait(bias_in)
        bi = BI[:, :, :].rearrange("p a b -> p (a b)")
        for g in range(2):
            ready = []
            for t, n0, per in ((0, 4 * g, 4), (1, 4 * g, 2), (1, 4 * g + 2, 2)):
                ns = P * (t + 1)
                b = take("m")
                for n in range(per):
                    h = HORDER[n0 + n]
                    lo_p, tile = 64 * (h % 2), h // 2
                    op = lambda e, b=b, n=n, ns=ns, lo_p=lo_p, tile=tile, t=t: e.matmul(
                        bank[b][:, n * ns:(n + 1) * ns], PP[lo_p:lo_p + 64, tile, t * P:(t + 1) * P],
                        PP[lo_p:lo_p + 64, 4 + tile, 0:ns], start=True, stop=True)
                    m = PE.do(op) if n == per - 1 else PE.go(op)
                VE.wait(m)
                dst = S[t][:, n0:n0 + per, :].rearrange("p a b -> p (a b)")
                off = 8 * P * t + n0 * ns
                a = VE.do(lambda e, b=b, dst=dst, off=off: e.scalar_tensor_tensor(
                    dst, bank[b][:, :], 0.125, bi[:, off:off + 512], ALU.mult, ALU.add))
                freed[b].append(a)
                ready.append(a)
            VE.wait(*ready)
            mx = [VE.do(lambda e, t=t, g=g: e.tensor_reduce(MX[:, 8 * t + 4 * g:8 * t + 4 * g + 4],
                                                           S[t][:, 4 * g:4 * g + 4, :], AX.X, ALU.max, negate=True))
                  for t in range(2)]
            SC.wait(*mx)
            for t in range(2):
                for n in range(4 * g, 4 * g + 4):
                    ex = SC.do(lambda e, t=t, n=n, g=g: e.activation(
                        S[t][:, n, :], S[t][:, n, :], ACT.Exp, bias=MX[:, 8 * t + n:8 * t + n + 1],
                        accum_out=SM[:, 8 * g + 4 * t + n % 4:8 * g + 4 * t + n % 4 + 1]))
            probs[g] = ex

    def probabilities(g):
        VE.wait(probs[g])
        rc = VE.do(lambda e: e.reciprocal(SM[:, 8 * g:8 * g + 8], SM[:, 8 * g:8 * g + 8]))
        VE.wait(rc)
        probs["n", g] = [VE.do(lambda e, t=t: e.tensor_tensor(
            S[t][:, 4 * g:4 * g + 4, :], S[t][:, 4 * g:4 * g + 4, :],
            SM[:, 8 * g + 4 * t:8 * g + 4 * t + 4].unsqueeze(2).to_broadcast([P, 4, P * (t + 1)]), ALU.mult))
            for t in range(2)]

    def turn_probabilities(g):
        srcs = [[S[t][:, 4 * g + n, s:s + P] for n in range(4)] for t, s in ((0, 0), (1, 0), (1, P))]
        outs = [PT[:, blk, 4 * g:4 * g + 4, :].rearrange("p a b -> p (a b)") for blk in range(3)]
        probs["t", g] = transposes(srcs, outs, probs["n", g], [down_done])

    pool_m = {}

    def pooling():
        U = PP[:, 12:14, :]
        VE.wait(pp[6], h3_read)

        def shifted(dst, src, w):
            a = VE.do(lambda e: e.tensor_copy(dst[..., 0:w], src[..., 0:w]))
            return [a, VE.do(lambda e: e.tensor_tensor(dst[..., w:T], src[..., w:T], src[..., 0:T - w], ALU.add))]

        VE.wait(*shifted(M2[:, :, :], U, 1))
        VE.wait(*shifted(M4[:, :, :], M2[:, :, :], 2))
        VE.wait(*shifted(M8[:, :], M4[:, 1, :], 4))
        VE.wait(*shifted(M16[:, :], M8[:, :], 8))
        pr = c("poolr").rearrange("p (f n) -> p f n", f=2)
        groups = [(0, M2[0:64, 0, :], 2), (0, M4[64:128, 0, :], 4), (1, M8[0:64, :], 8), (1, M16[64:128, :], 16)]
        for n, (f, src, w) in enumerate(groups):
            lo_p = 64 * (n % 2)
            y = VE.do(lambda e, f=f, src=src, w=w, lo_p=lo_p: e.tensor_scalar(
                PM[lo_p:lo_p + 64, f, :], src, 1.0 / w, None, ALU.mult))
        VE.wait(y)
        y = VE.do(lambda e: e.tensor_tensor(PM[:, :, 0:16], PM[:, :, 0:16], pr, ALU.mult))
        VE.wait(y)
        pool_m["m"] = VE.do(lambda e: e.tensor_tensor(PM[:, :, :], PM[:, :, :], U, ALU.subtract))

    def pool_product():
        PE.wait(pool_m["m"], pw_in)
        b = take("m")
        for f in range(2):
            m = PE.do(lambda e, f=f: e.matmul(bank[b][:, f * T:(f + 1) * T], PW[:, f, :], PM[:, f, :], start=True,
                                              stop=True))
        VE.wait(m)
        for f in range(2):
            y = VE.do(lambda e, f=f: e.tensor_scalar(UP[:, f, :], bank[b][:, f * T:(f + 1) * T],
                                                     v("pool_scale", f, 1), None, ALU.mult))
        freed[b].append(y)
        mix[6] = mix[7] = to_mix(UP[:, :, :], 6, 2, y)

    def short_conv():
        VE.wait(pp[7], pp[8], pp[9], h3_read)
        z = VE.do(lambda e: e.tensor_tensor(Z[:, :, :], PP[:, 16:18, :], PP[:, 18:20, :], ALU.mult))
        VE.wait(z)
        cw2 = v("conv_w_2").rearrange("p (f w) -> p f w", w=3)
        for f in range(2):
            y = VE.do(lambda e, f=f: e.tensor_scalar(YC[:, f, :], Z[:, f, :], cw2[:, f, 2:3], None, ALU.mult))
        for s in (1, 2):
            VE.wait(y)
            for f in range(2):
                y = VE.do(lambda e, f=f, s=s: e.scalar_tensor_tensor(
                    YC[:, f, s:T], Z[:, f, 0:T - s], cw2[:, f, 2 - s:3 - s], YC[:, f, s:T], ALU.mult, ALU.add))
        VE.wait(y)
        y = VE.do(lambda e: e.tensor_tensor(YC[:, :, :], YC[:, :, :], PP[:, 14:16, :], ALU.mult))
        mix[4] = mix[5] = to_mix(YC[:, :, :], 4, 2, y)

    mix = {}

    def to_mix(src, k, n, after):
        SC.wait(after, *h3[-1])
        a = SC.do(lambda e: e.activation(MXh[:, k:k + n, :], src, ACT.Copy))
        VE.wait(a)
        return [a, VE.do(lambda e: e.tensor_tensor(MXl[:, k:k + n, :], src, MXh[:, k:k + n, :].bitcast(F32),
                                                   ALU.subtract))]

    for i in range(10):
        b, h3_read = pair_when("w_in_2", i, H3h, H3l, h3)
        pp[i] = evict(b, h3_read, flat(PP[:, 2 * i:2 * i + 2, :]), after=[down_done])
        if i < 4:
            SC.wait(pp[i], *([qk_cols[i - 2]] if i >= 2 else []))
            qk_sq[i] = SC.do(lambda e, i=i: e.activation(SQq[i % 2][:, :, :], PP[:, 2 * i:2 * i + 2, :], ACT.Square))
        if 2 <= i < 6:
            qk_norm(i - 2)
        if 1 <= i < 5:
            qk_columns(i - 1)
        if i == 5:
            srcs = [[PP[:, 8 + n, t * P:(t + 1) * P] for n in range(4)] for t in range(2)]
            vv = transposes(srcs, [flat(VV[:, t, :, :]) for t in range(2)], [pp[4], pp[5]], [down_done, x])
        if i == 6:
            scores()
        if i == 7:
            probabilities(0)
    probabilities(1)
    turn_probabilities(0)
    pooling()
    pool_product()
    short_conv()
    turn_probabilities(1)
    PE.wait(*probs["t", 0], *probs["t", 1], *vv)
    for tp in range(2):
        b = take("m")
        for j in range(2):
            for par in range(2):
                h = 2 * (2 * tp + j) + par
                n = HORDER.index(h)
                o = bank[b][64 * par:64 * par + 64, j * T:(j + 1) * T]
                w = [VV[:, t, h // 2, 64 * par:64 * par + 64] for t in range(2)]
                PE.go(lambda e, o=o, w=w, n=n: e.matmul(o[:, 0:P], w[0], PT[:, 0, n, :], start=True, stop=True))
                PE.go(lambda e, o=o, w=w, n=n: e.matmul(o[:, P:T], w[0], PT[:, 1, n, :], start=True, stop=False))
                m = PE.do(lambda e, o=o, w=w, n=n: e.matmul(o[:, P:T], w[1], PT[:, 2, n, :], start=False, stop=True))
        src = bank[b][:, :].rearrange("p (a t) -> p a t", a=2)
        mix[2 * tp] = mix[2 * tp + 1] = to_mix(src, 2 * tp, 2, m)
        freed[b].append(mix[2 * tp][1])

    SQ3 = area("SQ3", [P, KT, T], 72)
    TMP3 = area("TMP3", [P, KT, T], 0)
    H4h = area("H4h", [P, KT, T], 8, F32R)
    H4l = area("H4l", [P, KT, T], 16, F32R)
    ready = [mix[k] for k in range(KT)]
    bs = take("m")
    warm(ACT.Sqrt)
    sq = {}
    for i in range(4):
        b, m = pair_when("w_out_2", i, MXh, MXl, ready, [6, 7, 4, 5, 0, 1, 2, 3])
        sq[i] = squares(SQ3, 2 * i, add_to_x(b, m, 2 * i, None))
        if i:
            square_columns(bs, 0, SQ3, 2 * i - 2, sq[i - 1], i == 1)
    out2_done = m
    m = square_columns(bs, 0, SQ3, 6, sq[3], False)
    rc = rstd_columns(bs, 2, D, 0, m)
    br = take("m")
    h4 = normed(rows(br, [wide(0), wide(1)], rc), br, v("norm2_g_2"), None, TMP3, H4h, H4l)

    NF = 8
    FH = area("FH", [P, NF, T], 24, F32R)
    FL = area("FL", [P, NF, T], 32, F32R)
    FR = [area(f"FR{i}", [P, 2, T], 88 + 2 * i) for i in range(2)]
    FQ = [area(f"FQ{i}", [P, 2, T], 92 + 2 * i) for i in range(2)]
    f_done, f_read = {}, {}
    fr_free = [[], []]
    ring["m"] = [3]
    acc = [claim(b) for b in (4, 5, 6, 7)]

    def mlp_up(i):
        b, m = pair_when("w_mlp1", i, H4h, H4l, h4)
        fr, fq = FR[i % 2], FQ[i % 2]
        at = 2 * i % NF
        SC.wait(m, *fr_free[i % 2])
        r = SC.do(lambda e: e.activation(flat(fr[:, :, :]), bank[b][:, :], ACT.Relu))
        freed[b].append(r)
        VE.wait(r)
        q = VE.do(lambda e: e.tensor_tensor(fq[:, :, :], fr[:, :, :], fr[:, :, :], ALU.mult))
        SC.wait(q, out2_done, *f_read.get(i - NF // 2, []))
        a = SC.do(lambda e: e.activation(FH[:, at:at + 2, :], fq[:, :, :], ACT.Copy))
        VE.wait(a, *f_read.get(i - NF // 2, []))
        l = VE.do(lambda e: e.tensor_tensor(FL[:, at:at + 2, :], fq[:, :, :], FH[:, at:at + 2, :].bitcast(F32),
                                            ALU.subtract))
        fr_free[i % 2] = [l]
        f_done[2 * i] = f_done[2 * i + 1] = [a, l]

    for i in range(18):
        if i < 16:
            mlp_up(i)
        if i >= 2:
            f_read[i - 2] = [contract("w_mlp2", i - 2, FH, FL, NF, f_done, 31)]
    s_out = sem("stores")
    for i in range(4):
        x = add_to_x(acc[i], acc_done[i], 2 * i, None)
        SY.wait(x)
        SY.go(lambda e, i=i: e.dma_start(io["out"][:, 2 * i:2 * i + 2, :], XR[:, 2 * i:2 * i + 2, :])
              .then_inc(s_out, 16))
    SY.wait((s_out, 64))

    with nc.Block() as block:
        block.sync(SY.replay)
        block.scalar(SC.replay)
        block.vector(VE.replay)
        block.gpsimd(PO.replay)
        block.tensor(PE.replay)


def tiles(w, ft, order=None):
    k, n = w.shape
    b = w.reshape(k // P, P, n // P, P).transpose(2, 1, 0, 3)
    if order is not None:
        b = b[order]
    if ft:
        b = b.reshape(-1, ft, P, k // P, P).transpose(0, 2, 1, 3, 4)
        return np.ascontiguousarray(b.reshape(b.shape[0], P, -1))
    b = b.transpose(2, 1, 0, 3).reshape(k // P // 2, 2, P, n // P, P).transpose(0, 2, 1, 3, 4)
    return np.ascontiguousarray(b.reshape(k // P // 2, P, -1))


def wide_rows(w):
    k, n = w.shape
    return np.ascontiguousarray(w.T.reshape(n // P // 2, 2, P, k).transpose(0, 2, 1, 3).reshape(-1, P, 2 * k))


def columns(a):
    a = np.asarray(a)
    return a.reshape(-1, P).T


def constants():
    con = np.zeros((P, NC), np.float32)

    def put(name, x):
        a, w = CON[name]
        con[:, a:a + w] = x.reshape(P, w)

    put("ident", np.eye(P))
    i = np.arange(P)
    ang = 2 * np.pi * (np.outer(i, i) % P) / P
    put("dft_c", np.concatenate([np.cos(ang), np.sin(ang)], 1))
    j = np.arange(T)
    ang = 2 * np.pi * (np.outer(j, j) % T) / T
    s = 1.0 / np.sqrt(T * P)
    both = np.stack([np.cos(ang) * s, -np.sin(ang) * s])
    put("dft_l", both.reshape(2, 2, P, T).transpose(2, 1, 0, 3))
    put("blk", (i[:, None] // 64 == i[None, :] // 64).astype(np.float32))
    r = np.zeros((P, 2, 16))
    for f in range(2):
        for p in range(P):
            w = 2 ** (2 * f + p // 64 + 1)
            r[p, f] = w / np.minimum(np.arange(16) + 1, w)
    put("poolr", r)
    masks = np.zeros((P, len(LEVELS), P), np.float32)
    for n, h in enumerate(LEVELS):
        masks[:, n] = (i[:, None] // (2 * h) == i[None, :] // (2 * h)) & (i[:, None] // h != i[None, :] // h)
    return con, masks


def bias_rows(rel):
    t, s = np.arange(T)[:, None], np.arange(T)[None, :]
    full = rel[:, np.clip(t - s, -128, 128) + 128]
    full = np.where((s // 64 <= t // 64)[None], full, np.float32(-1e30)).astype(rel.dtype)
    full = full[HORDER]
    a = full[:, 0:P, 0:P].transpose(1, 0, 2).reshape(P, -1)
    b = full[:, P:T, :].transpose(1, 0, 2).reshape(P, -1)
    return np.ascontiguousarray(np.concatenate([a, b], 1).reshape(P, 8, 384))


def kernel(**inputs):
    import concourse.bacc as bacc
    from concourse.bass_utils import run_bass_kernel_spmd as run

    g = {k: np.asarray(x) for k, x in inputs.items()}
    con, masks = constants()
    dup = lambda a: np.concatenate([a.reshape(-1), a.reshape(-1)])[:, None]
    cols = {
        "norm1_g": columns(g["norm1_g"]), "ada_b": columns(g["ada_b"]), "hg_lb": columns(g["hg_lb"]),
        "onorm": columns(g["hg_onorm_g"]), "norm2_g": columns(g["norm2_g"]), "conv_b": columns(g["ffn_conv_b"]),
        "conv_w": g["ffn_conv_w"].reshape(9, 44, P).transpose(2, 1, 0).reshape(P, -1),
        "final_g": columns(g["final_g"]), "norm1_g_2": columns(g["norm1_g_2"]),
        "q_g": dup(g["q_norm_g_2"]), "k_g": dup(g["k_norm_g_2"]),
        "conv_w_2": g["conv_w_2"].reshape(3, 2, P).transpose(2, 1, 0).reshape(P, -1),
        "pool_scale": columns(g["pool_scale_2"]), "norm2_g_2": columns(g["norm2_g_2"]),
        "c2": np.stack([g["c"].reshape(KT, P), g["c_ctx"].reshape(KT, P)], 2).transpose(1, 0, 2).reshape(P, -1),
    }
    pw = np.zeros((P, 2, P), np.float32)
    for n in range(4):
        a = 64 * (n % 2)
        pw[a:a + 64, n // 2, a:a + 64] = g["pool_w_2"][0, n]
    w_in = g["w_in"][0]
    arrays = {
        "vec": np.ascontiguousarray(np.concatenate([cols[n] for n in VEC], 1)),
        "con": con, "masks": masks,
        "xT": np.ascontiguousarray(g["x"][0].T.reshape(KT, P, T).transpose(1, 0, 2)),
        "ctxT": np.ascontiguousarray(g["ctx"][0].T.reshape(KT, P, T).transpose(1, 0, 2)),
        "c_row": np.ascontiguousarray(g["c"].reshape(1, D)),
        "bias": bias_rows(g["rel_bias_2"][0]), "pool_w": pw,
        "c_ctx_row": np.ascontiguousarray(g["c_ctx"].reshape(1, D)),
        "ada_p": tiles(g["ada_w"][0][:, :1024], 2), "ada_s": wide_rows(g["ada_w"][0][:, 1024:2048]),
        "ada_hi": wide_rows(g["ada_w"][0][:, 2048:]),
        "w_in": tiles(w_in, 2, [*range(4, 20), *range(0, 4), *range(20, 40)]),
        "w_a": tiles(g["w_a"][0], 4), "w_b": tiles(g["w_b"][0], 4), "w_out": tiles(g["w_out"][0], 2),
        "ffn_up": tiles(g["ffn_up"][0], 2, [f for i in range(22) for f in (i, i + 22)]),
        "ffn_down": tiles(g["ffn_down"][0], 0),
        "w_in_2": tiles(g["w_in_2"][0], 2, [*range(12), 18, 19, *range(12, 18)]), "w_out_2": tiles(g["w_out_2"][0], 2),
        "w_mlp1": tiles(g["w_mlp1_2"][0], 2), "w_mlp2": tiles(g["w_mlp2_2"][0], 0),
    }
    nc = bacc.Bacc("TRN2", target_bir_lowering=False, num_devices=1)
    io, feed = {}, {}
    for name, a in arrays.items():
        feed[f"in_{name}"] = a
        io[name] = nc.dram_tensor(f"in_{name}", a.shape, mybir.dt.from_np(a.dtype), kind="ExternalInput").ap()
    io["out"] = nc.dram_tensor("out_x", (P, KT, T), F32, kind="ExternalOutput").ap()
    build(nc, io)
    r = run(nc, [feed], core_ids=[0])
    got = r.results[0]["out_x"]
    return np.ascontiguousarray(got.transpose(2, 1, 0).reshape(1, T, D))
```

```python
import numpy as np

import concourse.bass as bass
from concourse import mybir

F32 = mybir.dt.float32
F32R = mybir.dt.float32r
U8 = mybir.dt.uint8
ALU = mybir.AluOpType
ACT = mybir.ActivationFunctionType
AX = mybir.AxisListType

P = 128
T = 256
D = 1024
KT = D // P
NH = 4
CH = 2048
NRAW, NHI = 4, 3
EPS = 1e-6
LEVELS = [1, 2, 4, 8, 16, 32, 64]
HORDER = [0, 2, 4, 6, 1, 3, 5, 7]

VEC = {}
_at = 0
for _n, _w in [("norm1_g", 8), ("ada_b", 48), ("hg_lb", 8), ("onorm", 4), ("norm2_g", 8), ("conv_b", 44),
               ("conv_w", 44 * 9), ("final_g", 8), ("norm1_g_2", 8), ("q_g", 1), ("k_g", 1), ("conv_w_2", 6),
               ("pool_scale", 2), ("norm2_g_2", 8), ("c2", 16)]:
    VEC[_n] = (_at, _w)
    _at += _w
NV = _at

CON = {}
_at = 0
for _n, _w in [("ident", 128), ("dft_c", 256), ("dft_l", 1024), ("blk", 128), ("poolr", 32)]:
    CON[_n] = (_at, _w)
    _at += _w
NC = _at


class Queue:

    def __init__(self, sem):
        self.sem, self.count, self.ops, self.seen = sem, 0, [], {}

    def wait(self, *marks):
        for sem, value in marks:
            if self.seen.get(sem.name, 0) < value:
                self.seen[sem.name] = value
                self.ops.append(lambda e, s=sem, v=value: e.wait_ge(s, v))

    def do(self, fn):
        self.count += 1
        self.ops.append(lambda e, f=fn: f(e).then_inc(self.sem, 1))
        return self.sem, self.count

    def go(self, fn):
        self.ops.append(fn)

    def replay(self, e):
        for op in self.ops:
            op(e)


def chunk_plan():
    plan = []
    for name, i in (("ada_s", 0), ("ada_s", 1), ("ada_p", 0), ("ada_s", 2), ("ada_p", 1), ("ada_s", 3), ("ada_p", 2),
                    ("ada_s", 4), ("w_in", 0)):
        plan.append((name, i, 2048))
    for i in range(20):
        if i:
            plan.append(("w_in", i, 2048))
        if 2 <= i < 10:
            plan += [("ada_hi", 2 * (i - 2), 2048), ("ada_hi", 2 * (i - 2) + 1, 2048)]
    for name, n in (("w_a", 2), ("w_b", 2), ("w_out", 4)):
        plan += [(name, i, 2048) for i in range(n)]
    for i in range(22):
        plan.append(("ffn_up", i, 2048))
        if i >= 5 and i % 2:
            plan.append(("ffn_down", (i - 5) // 2, 2048))
    plan += [("ffn_down", 9, 2048), ("ffn_down", 10, 2048)]
    for name, n in (("w_in_2", 10), ("w_out_2", 4)):
        plan += [(name, i, 2048) for i in range(n)]
    for i in range(16):
        plan.append(("w_mlp1", i, 2048))
        if i >= 2:
            plan.append(("w_mlp2", i - 2, 2048))
    return plan + [("w_mlp2", 14, 2048), ("w_mlp2", 15, 2048)]


def build(nc, io):
    sems = []

    def sem(name):
        s = nc.alloc_semaphore(name)
        sems.append(s)
        return s

    PE, SC, VE, PO, SY = (Queue(sem(n)) for n in ("pe_done", "act_done", "dve_done", "pool_done", "sp_done"))

    start = 16512
    cursor = [start]

    def place(name, shape, dt, offset):
        return nc.alloc_sbuf_tensor_at(name, shape, dt, offset=offset)

    def keep(name, shape, dt=F32):
        size = int(np.prod(shape[1:])) * (1 if dt == U8 else 4)
        t = place(name, shape, dt, cursor[0])
        cursor[0] += (size + 31) // 32 * 32
        return t

    raw = [keep(f"raw{i}", [P, CH]) for i in range(NRAW)]
    whi = [keep(f"whi{i}", [P, CH], F32R) for i in range(NHI)]
    wlo = [keep(f"wlo{i}", [P, CH], F32R) for i in range(NHI)]
    XR = keep("XR", [P, KT, T])
    con = keep("con", [P, NC])
    masks = keep("masks", [P, len(LEVELS), P], U8)
    vec = keep("vec", [P, NV])
    CB = keep("CB", [P, D])
    RC = keep("RC", [P, 64])
    ones = keep("ones", [P, T])
    eps = keep("eps", [P, 1])
    C2 = keep("C2", [P, KT, 2])
    MOD = keep("MOD", [P, 16, 2])
    warmed = keep("warmed", [P, 1])
    A1 = keep("A1", [P, KT, 2])
    MODX = keep("MODX", [P, 32])
    A2 = keep("A2", [P, KT])
    LBE = keep("LBE", [P, 8])
    LBM = keep("LBM", [P, 4])
    LB = keep("LB", [P, 4])
    LB1 = keep("LB1", [P, 4])
    MX = keep("MX", [P, 16])
    SM = keep("SM", [P, 16])
    GG = keep("GG", [P, KT])
    G2 = keep("G2", [P, KT, 2])
    base = cursor[0]

    def area(name, shape, kb, dt=F32):
        return place(name, shape, dt, base + int(kb * 1024))

    def v(name, i=0, n=None):
        a, w = VEC[name]
        return vec[:, a + i:a + i + (w if n is None else n)]

    def c(name):
        a, w = CON[name]
        return con[:, a:a + w]

    ident = c("ident")
    bank = [nc.alloc_psum_tensor(f"bank{i}", [P, 512], F32) for i in range(8)]
    freed = {i: [] for i in range(8)}
    ring = {"g": [0, 1, 2], "m": [3, 4, 5, 6, 7]}
    turn = {"g": 0, "m": 0}

    def claim(b):
        PE.wait(*freed[b])
        freed[b] = []
        return b

    def take(kind):
        turn[kind] += 1
        return claim(ring[kind][turn[kind] % len(ring[kind])])

    def load(eng, name, dst, src):
        s = sem(f"in_{name}")
        eng.go(lambda e: e.dma_start(dst, src).then_inc(s, 16))
        return s, 16

    CX = area("CX", [P, KT, T], 32)
    MASKF = area("MASKF", [P, len(LEVELS), P], 40)
    CBX = area("CBX", [P, D], 44)
    c_in = [load(SC, "c", CB[:, :], io["c_row"].to_broadcast([P, D])),
            load(SC, "c_ctx", CBX[:, :], io["c_ctx_row"].to_broadcast([P, D]))]
    vec_in = load(SY, "vec", vec[:, :], io["vec"])
    x_in = load(SC, "x", XR[:, :, :], io["xT"])
    ctx_in = load(SC, "ctx", CX[:, :, :], io["ctxT"])
    ident_in = load(SC, "ident", ident, io["con"][:, 0:P])

    plan = chunk_plan()
    s_raw = [sem(f"raw{i}") for i in range(NRAW)]
    n_raw = [0] * NRAW
    arrived, raw_free = {}, {}
    split = {}
    hi_free = {}
    order = {}
    for n, (name, i, cols) in enumerate(plan):
        order[(name, i)] = n
    slot_of = {}
    nsplit = [0]
    issued = [0]
    prepped = [0]

    def issue_loads(upto):
        while issued[0] < min(upto, len(plan)):
            n = issued[0]
            name, i, cols = plan[n]
            s = n % NRAW
            if n >= NRAW:
                SY.wait(*raw_free[n - NRAW])
            SY.go(lambda e, s=s, name=name, i=i, cols=cols:
                  e.dma_start(raw[s][:, 0:cols], io[name][i]).then_inc(s_raw[s], 16))
            n_raw[s] += 16
            arrived[n] = (s_raw[s], n_raw[s])
            issued[0] += 1

    def lo_engine(name, i):
        return PO if name in ("w_in", "w_a", "w_b", "w_out", "ffn_up", "ffn_down", "w_in_2", "w_out_2") else VE

    def prep(n):
        name, i, cols = plan[n]
        r = raw[n % NRAW]
        if name == "ada_hi":
            VE.wait(arrived[n], c_rows[0])
            for j in range(2):
                f = 2 * i + j
                m = VE.do(lambda e, j=j, f=f: e.tensor_tensor_reduce(
                    out=r[:, j * D:(j + 1) * D], in0=r[:, j * D:(j + 1) * D], in1=CB[:, :], scale=1.0, scalar=0.0,
                    op0=ALU.mult, op1=ALU.add, accum_out=MODX[:, f:f + 1]))
            side_done[i] = m
            raw_free[n] = [m]
            issue_loads(n + NRAW + 1)
            return
        s = nsplit[0] % NHI
        nsplit[0] += 1
        slot_of[n] = s
        h, l = whi[s], wlo[s]
        prev = hi_free.get(s, [])
        SC.wait(arrived[n], *prev)
        a = SC.do(lambda e: e.activation(h[:, 0:cols], r[:, 0:cols], ACT.Copy))
        L = lo_engine(name, i)
        L.wait(arrived[n], a, *prev)
        half = cols // 2 if (name, i) == ("w_in", 0) else 0
        b = [L.do(lambda e: e.tensor_tensor(l[:, half:cols], r[:, half:cols], h[:, half:cols].bitcast(F32),
                                            ALU.subtract))]
        if half:
            VE.wait(a, *prev)
            b.append(VE.do(lambda e: e.tensor_tensor(l[:, 0:half], r[:, 0:half], h[:, 0:half].bitcast(F32),
                                                     ALU.subtract)))
        split[n] = [a, *b]
        raw_free[n] = split[n]
        issue_loads(n + NRAW + 1)

    def prep_upto(n):
        while prepped[0] <= min(n, len(plan) - 1):
            prep(prepped[0])
            prepped[0] += 1

    side_done = {}

    def chunk(name, i):
        n = order[(name, i)]
        look, more = n, NHI - 1
        while more and look + 1 < len(plan):
            look += 1
            more -= plan[look][0] != "ada_hi"
        prep_upto(look)
        PE.wait(*split[n])
        s = slot_of[n]
        return s, whi[s], wlo[s]

    def chunk_done(s, mark):
        hi_free[s] = [mark]

    def mm3(out, h, l, col, xh, xl, first, last):
        PE.go(lambda e: e.matmul(out, h[:, col:col + P], xh, start=first, stop=False, skip_group_check=True))
        PE.go(lambda e: e.matmul(out, h[:, col:col + P], xl, start=False, stop=False, skip_group_check=True))
        op = lambda e: e.matmul(out, l[:, col:col + P], xh, start=False, stop=last, skip_group_check=True)
        return PE.do(op) if last else PE.go(op)

    m_ones = PO.do(lambda e: e.memset(ones[:, :], 1.0))
    m_eps = PO.do(lambda e: e.memset(eps[:, :], EPS))
    one128 = ones[:, 0:P]

    issue_loads(NRAW)

    HN = area("HN", [P, 2, KT, T], 72)
    H1h = area("H1h", [P, 2, KT, T], 0, F32R)
    H1l = area("H1l", [P, 2, KT, T], 16, F32R)
    SPARE = [area(f"SPARE{i}", [P, D], 48 + 4 * i) for i in range(2)]
    c_rows = []
    SC.wait(vec_in)
    c2 = SC.do(lambda e: e.activation(C2[:, :, :], v("c2").rearrange("p (k j) -> p k j", j=2), ACT.Silu))
    SC.wait(c_in[0])
    c_rows.append(SC.do(lambda e: e.activation(CB[:, :], CB[:, :], ACT.Silu)))
    SC.wait(c_in[1])
    c_rows.append(SC.do(lambda e: e.activation(CBX[:, :], CBX[:, :], ACT.Silu)))
    def column(b, i, sq, first, last):
        op = lambda e: e.matmul(bank[b][:, i:i + 1], sq, ones[:, 0:1], start=first, stop=last, skip_group_check=True)
        return PE.do(op) if last else PE.go(op)

    def rstd_columns(b, n, width, at, after):
        SC.wait(after)
        m = SC.do(lambda e: e.activation(RC[:, at:at + n], bank[b][:, 0:n], ACT.Sqrt, bias=eps[:, 0:1],
                                         scale=1.0 / width))
        freed[b].append(m)
        VE.wait(m)
        return VE.do(lambda e: e.reciprocal(RC[:, at:at + n], RC[:, at:at + n]))

    def rows(b, cols, ready, at=0):
        PE.wait(ready, ident_in)
        for i, col in enumerate(cols):
            op = lambda e, i=i, col=col: e.matmul(bank[b][:, (at + i) * P:(at + i + 1) * P], col, ident, start=True, stop=True)
            m = PE.do(op) if i == len(cols) - 1 else PE.go(op)
        return m

    def wide(i):
        return RC[:, i:i + 1].to_broadcast([P, P])

    lbr = v("hg_lb").rearrange("p (r h) -> p r h", r=2)
    LBE2 = LBE[:, :].rearrange("p (r h) -> p r h", r=2)
    VE.wait(vec_in)
    lb_max = VE.do(lambda e: e.tensor_tensor(LBM[:, :], lbr[:, 0, :], lbr[:, 1, :], ALU.max))

    def warm(func):
        SC.do(lambda e: e.activation(warmed[:, 0:1], eps[:, 0:1], func))

    def input_columns(x):
        PE.wait(sums[x], m_ones)
        b = take("m")
        for t in range(2):
            m = PE.do(lambda e, t=t: e.matmul(bank[b][:, t:t + 1], HN[:, x, 0, t * P:(t + 1) * P], ones[:, 0:1],
                                              start=t == 0, stop=True, skip_group_check=True))
        return rstd_columns(b, 2, D, 2 * x, m)

    bm = take("m")
    modp = bank[bm][:, 0:12].rearrange("p (f j) -> p f j", j=2)
    spare_free = [[], []]
    ada_tiles = [8, 10, 12, 14, 0]

    def ada_rows(i):
        n = order[("ada_s", i)]
        VE.wait(arrived[n])
        r = raw[n % NRAW]
        for f in range(2):
            VE.wait(*spare_free[f])
            for j, (row, out) in enumerate(((CB, SPARE[f][:, :]), (CBX, r[:, f * D:(f + 1) * D]))):
                VE.wait(c_rows[j])
                m = VE.do(lambda e, f=f, j=j, row=row, out=out: e.tensor_tensor_reduce(
                    out=out, in0=r[:, f * D:(f + 1) * D], in1=row[:, :], scale=1.0, scalar=0.0,
                    op0=ALU.mult, op1=ALU.add, accum_out=MOD[:, ada_tiles[i] + f, j:j + 1]))
                if j == 0:
                    spare_free[f] = [m]
        raw_free[n] = [m]
        issue_loads(n + NRAW + 1)
        return m

    def ada_columns(i):
        n = order[("ada_p", i)]
        PE.wait(arrived[n], c2)
        r = raw[n % NRAW]
        for f in range(2):
            for k in range(KT):
                op = lambda e, f=f, k=k: e.matmul(
                    modp[:, 2 * i + f, :], r[:, (f * KT + k) * P:(f * KT + k + 1) * P], C2[:, k, :],
                    start=k == 0, stop=k == KT - 1)
                m = PE.do(op) if f == 1 and k == KT - 1 else PE.go(op)
        raw_free[n] = [m]
        issue_loads(n + NRAW + 1)
        return m

    ada_rows(0)
    ada_rows(1)
    sums = []
    for x, (src, src_in) in enumerate(((XR, x_in), (CX, ctx_in))):
        SC.wait(src_in)
        m = SC.do(lambda e, x=x, src=src: e.activation(HN[:, x, :, :], src[:, :, :], ACT.Square))
        E = PO if x else VE
        for n in (4, 2, 1):
            E.wait(m)
            m = E.do(lambda e, x=x, n=n: e.tensor_tensor(HN[:, x, 0:n, :], HN[:, x, 0:n, :], HN[:, x, n:2 * n, :],
                                                         ALU.add))
        sums.append(m)

    ada_columns(0)
    VE.wait(lb_max)
    a = VE.do(lambda e: e.tensor_tensor(LBE2, lbr, LBM[:, :].unsqueeze(1).to_broadcast([P, 2, 4]), ALU.subtract))
    SC.wait(a)
    lb_exp = SC.do(lambda e: e.activation(LBE[:, :], LBE[:, :], ACT.Exp))
    SC.wait(m_eps)
    warm(ACT.Sqrt)
    ada_rows(2)
    rcs = [input_columns(0)]
    ada_columns(1)
    VE.wait(lb_exp)
    a = VE.do(lambda e: e.tensor_tensor(LBM[:, :], LBE2[:, 0, :], LBE2[:, 1, :], ALU.add))
    VE.wait(a)
    a = VE.do(lambda e: e.reciprocal(LBM[:, :], LBM[:, :]))
    VE.wait(a)
    a = VE.do(lambda e: e.tensor_tensor(LB[:, :], LBE2[:, 0, :], LBM[:, :], ALU.mult))
    VE.wait(a)
    lb_ready = VE.do(lambda e: e.tensor_scalar(LB1[:, :], LB[:, :], -1.0, 1.0, ALU.mult, ALU.add))
    ada_rows(3)
    rcs.append(input_columns(1))
    br = take("m")
    rs = [rows(br, [wide(2 * x), wide(2 * x + 1)], rcs[x], 2 * x) for x in range(2)]
    shifts = ada_columns(2)
    scale_done = ada_rows(4)
    prep(order[("w_in", 0)])
    masks_in = load(SY, "masks", MASKF[:, :, :], io["masks"])
    con_in = load(SY, "con", con[:, P:NC], io["con"][:, P:NC])
    prepped[0] = 9
    VE.wait(scale_done)
    both = lambda ap: ap.unsqueeze(2).to_broadcast([P, KT, 2])
    a = VE.do(lambda e: e.tensor_tensor(MOD[:, 8:16, :], MOD[:, 8:16, :], both(v("ada_b", 8, 8)), ALU.add))
    a0 = VE.do(lambda e: e.tensor_tensor(MOD[:, 0:2, :], MOD[:, 0:2, :],
                                         v("ada_b", 0, 2).unsqueeze(2).to_broadcast([P, 2, 2]), ALU.add))
    VE.wait(a)
    a1 = VE.do(lambda e: e.scalar_tensor_tensor(A1[:, :, :], MOD[:, 8:16, :], 1.0, both(v("norm1_g")), ALU.add,
                                                ALU.mult))
    VE.wait(shifts)
    m = VE.do(lambda e: e.tensor_tensor(MOD[:, 2:8, :], modp, v("ada_b", 2, 6).unsqueeze(2).to_broadcast([P, 6, 2]),
                                        ALU.add))
    freed[bm].append(m)
    VE.wait(m, a0, a1, *rs)
    his, h1 = [[], []], [[], []]
    for x in range(2):
        for k in range(KT + 1):
            if k < KT:
                src = (XR, CX)[x]
                m = VE.do(lambda e, k=k, x=x, src=src, br=br: e.scalar_tensor_tensor(
                    HN[:, x, k, :], src[:, k, :], A1[:, k, x:x + 1], bank[br][:, x * T:(x + 1) * T], ALU.mult, ALU.mult))
                SC.wait(m)
                his[x].append(SC.do(lambda e, k=k, x=x: e.activation(H1h[:, x, k, :], HN[:, x, k, :], ACT.Identity,
                                                                     bias=MOD[:, k, x:x + 1])))
                if x == 0 and k in (3, 7):
                    prep_upto(9 + k // 7)
            if k:
                VE.wait(his[x][k - 1])
                h1[x].append(VE.do(lambda e, k=k - 1, x=x: e.scalar_tensor_tensor(
                    H1l[:, x, k, :], HN[:, x, k, :], MOD[:, k, x:x + 1], H1h[:, x, k, :].bitcast(F32),
                    ALU.add, ALU.subtract)))
    freed[br].append(m)
    h1_all = [his[1][-1], h1[1][-1]]

    VE.wait(masks_in)
    m_masks = VE.do(lambda e: e.tensor_copy(masks[:, :, :], MASKF[:, :, :]))

    F = area("F", [P, 2, 2, NH, T], 32)
    K = area("K", [P, 2, 2, NH, T], 48)
    VT = area("VT", [P, 2, NH, T], 64)
    f_ready = {0: [], 1: []}
    vt_ready = []
    Q = area("Q", [P, NH, T], 96)
    XS = area("XS", [P, 2, NH, T], 72)
    FU = area("FU", [P, NH, T], 76)
    SG = area("SG", [P, NH, T], 88)
    GA = area("GA", [P, 2 * NH, T], 8)
    GB = area("GB", [P, 2 * NH, T], 24)
    QF = area("QF", [P, 2, NH, T], 40)
    A = area("A", [P, 2, NH, T], 56)
    VX = area("VX", [P, 2, NH, P], 68)
    KS = area("KS", [P, NH, T], 72)
    KTT = area("KTT", [P, 2, 2, NH, P], 80)
    VC = area("VC", [P, 2, NH, P], 88)
    ST = area("ST", [P, 2, NH, P], 92)
    T1 = area("T1", [P, 2, NH, T], 80)
    YFh = area("YFh", [P, NH, T], 72, F32R)
    YFl = area("YFl", [P, NH, T], 76, F32R)
    SQo = area("SQo", [P, NH, T], 80)
    RSo = area("RSo", [P, NH, T], 84)
    ON = area("ON", [P, NH, T], 64)
    YHh = area("YHh", [P, NH, T], 48, F32R)
    YHl = area("YHl", [P, NH, T], 52, F32R)
    MGh = area("MGh", [P, KT, T], 0, F32R)
    MGl = area("MGl", [P, KT, T], 16, F32R)
    kk, kc = {}, []

    def both_inputs(i):
        s, h, l = chunk("w_in", i)
        for j in range(2):
            b = take("g")
            for k in range(KT):
                PE.wait(his[1][k], h1[1][k])
                m = mm3(bank[b][:, :].rearrange("p (x t) -> p x t", x=2), h, l, (j * KT + k) * P,
                        H1h[:, :, k, :], H1l[:, :, k, :], k == 0, k == KT - 1)
            if j == 1:
                chunk_done(s, m)
            f = 2 * (i - 2) + j
            d, head = f // 4, f % 4
            src = bank[b][:, :].rearrange("p (x t) -> p x t", x=2)
            SC.wait(m, h1[1][-1], m_masks, scale_done)
            if d == 2:
                a = SC.do(lambda e, src=src, head=head: e.activation(VT[:, :, head, :], src, ACT.Copy))
                vt_ready.append(a)
            else:
                a = SC.do(lambda e, src=src, d=d, head=head: e.activation(F[:, :, d, head, :], src, ACT.Sigmoid))
                VE.wait(a, lb_ready)
                f_ready[d].append(VE.do(lambda e, d=d, head=head: e.tensor_scalar(
                    F[:, :, d, head, :], F[:, :, d, head, :], LB1[:, head:head + 1], LB[:, head:head + 1],
                    ALU.mult, ALU.add)))
            freed[b].append(a)
        return m

    def ctx_decay():
        PO.wait(*h1_all)
        m_xs = [PO.do(lambda e: e.memset(XS[:, 0, :, T - 1:T], 1.0)),
                PO.do(lambda e: e.memset(XS[:, 1, :, 0:1], 1.0))]
        for x in (1, 0):
            for d in range(2):
                VE.wait(f_ready[d][-1])
                kk[x, d] = VE.do(lambda e, x=x, d=d: e.tensor_scalar(K[:, x, d, :, :], F[:, x, d, :, :], -1.0, 1.0,
                                                                     ALU.mult, ALU.add))
        VE.wait(*m_xs, m_ones)
        for d in range(2):
            for head in range(NH):
                if d == 0:
                    o, i0 = XS[:, 0, head, T - 2::-1], F[:, 1, 0, head, T - 1:0:-1]
                else:
                    o, i0 = XS[:, 1, head, 1:T], F[:, 1, 1, head, 0:T - 1]
                m = VE.do(lambda e, o=o, i0=i0: e.tensor_tensor_scan(o, i0, ones[:, 0:T - 1], 1.0, ALU.mult,
                                                                     ALU.mult))
            VE.wait(m, kk[1, d])
            kc.append(VE.do(lambda e, d=d: e.tensor_tensor(K[:, 1, d, :, :], K[:, 1, d, :, :], XS[:, d, :, :],
                                                           ALU.mult)))

    def evict(b, m, out, func=ACT.Copy, after=()):
        SC.wait(m, *after)
        a = SC.do(lambda e: e.activation(out, bank[b][:, :], func))
        freed[b].append(a)
        return a

    def flat(ap):
        return ap.rearrange("p a b -> p (a b)")

    hx, hl = H1h[:, 0, :, :], H1l[:, 0, :, :]
    marks = {}

    def transposes(srcs, outs, after, before):
        PE.wait(*after)
        done = []
        for four, out in zip(srcs, outs):
            b = take("m")
            for n, src in enumerate(four):
                op = lambda e, b=b, n=n, src=src: e.transpose(bank[b][:, n * P:(n + 1) * P], src, ident)
                m = PE.do(op) if n == len(four) - 1 else PE.go(op)
            done.append(evict(b, m, out, after=before))
        return done

    def ctx_turn():
        srcs, outs = [], []
        for d in range(2):
            for t in range(2):
                srcs.append([K[:, 1, d, h, t * P:(t + 1) * P] for h in range(NH)])
                outs.append(flat(KTT[:, d, t, :, :]))
        marks["turned"] = transposes(srcs, outs, kc, h1_all)

    def v_turn():
        for x, name, dst in ((1, "vc", VC), (0, "vx", VX)):
            srcs = [[VT[:, x, h, t * P:(t + 1) * P] for h in range(NH)] for t in range(2)]
            marks[name] = transposes(srcs, [flat(dst[:, t, :, :]) for t in range(2)], vt_ready,
                                     marks["turned"] + marks.get("vc", []))

    def ctx_state():
        PE.wait(*marks["turned"], *marks["vc"])
        st = []
        for d in range(2):
            b = take("m")
            for h in range(NH):
                for t in range(2):
                    op = lambda e, b=b, d=d, h=h, t=t: e.matmul(
                        bank[b][:, h * P:(h + 1) * P], KTT[:, d, t, h, :], VC[:, t, h, :], start=t == 0, stop=t == 1)
                    m = PE.do(op) if (h, t) == (NH - 1, 1) else PE.go(op)
            st.append(evict(b, m, flat(ST[:, d, :, :])))
        marks["state"] = st
        marks["state_pe"] = m

    def x_start():
        VE.wait(*marks["q"], *kc)
        marks["qf"] = [VE.do(lambda e, d=d: e.tensor_tensor(QF[:, d, :, :], Q[:, :, :], F[:, 0, d, :, :], ALU.mult))
                       for d in range(2)]
        VE.wait(kk[0, 0], kk[0, 1])
        marks["ks"] = VE.do(lambda e: e.tensor_tensor(KS[:, :, :], K[:, 0, 0, :, :], K[:, 0, 1, :, :], ALU.add))

    def diagonal():
        PE.wait(marks["ks"], *marks["q"])
        marks["a"] = []
        for t in range(2):
            b = take("m")
            cols = slice(t * P, (t + 1) * P)
            for h in range(NH):
                op = lambda e, b=b, h=h, cols=cols: e.matmul(bank[b][:, h * P:(h + 1) * P], KS[:, h, cols],
                                                            Q[:, h, cols], start=True, stop=True)
                m = PE.do(op) if h == NH - 1 else PE.go(op)
            SC.wait(m, *marks["turned"])
            a = SC.do(lambda e, b=b, t=t: e.activation(A[:, t, :, t * P:(t + 1) * P],
                                                       bank[b][:, :].rearrange("p (h t) -> p h t", h=NH), ACT.Copy))
            freed[b].append(a)
            marks["a"].append(a)
        marks["diag_pe"] = m

    def halves(ap, h):
        return ap.rearrange("p (b two h) -> p b two h", two=2, h=h)

    def level(li):
        h = LEVELS[li]
        PE.wait(*marks["qf"])
        PE.wait(*marks.get("kf", []))
        got = []
        for t in range(2):
            b = take("m")
            cols = slice(t * P, (t + 1) * P)
            for hd in range(NH):
                o = halves(bank[b][:, hd * P:(hd + 1) * P], h)
                qr = halves(QF[:, 0, hd, cols], h)
                ql = halves(QF[:, 1, hd, cols], h)
                PE.go(lambda e, o=o, qr=qr, hd=hd, cols=cols: e.matmul(o[:, :, 1, :], K[:, 0, 0, hd, cols],
                                                                      qr[:, :, 1, :], start=True, stop=True))
                op = lambda e, o=o, ql=ql, hd=hd, cols=cols: e.matmul(o[:, :, 0, :], K[:, 0, 1, hd, cols],
                                                                     ql[:, :, 0, :], start=True, stop=True)
                m = PE.do(op) if hd == NH - 1 else PE.go(op)
            got.append((b, m))
        for t, (b, m) in enumerate(got):
            VE.wait(m, *marks["a"])
            a = VE.do(lambda e, b=b, t=t: e.copy_predicated(
                A[:, t, :, t * P:(t + 1) * P],
                masks[:, li, :].unsqueeze(1).to_broadcast([P, NH, P]),
                bank[b][:, :].rearrange("p (h t) -> p h t", h=NH)))
            freed[b].append(a)
            marks["ap"] = a
        grow(h, got[-1][1])

    def blocks(d, h):
        f = F[:, 0, d, :, :].rearrange("p a t -> p (a t)")
        return f.rearrange("p (b two h) -> p b two h", two=2, h=h)[:, :, :, 0]

    def grow(h, read):
        nb = NH * T // (2 * h)
        VE.wait(read)
        q0, q1 = (halves(QF[:, d, :, :].rearrange("p a t -> p (a t)"), h) for d in range(2))
        k0, k1 = (halves(K[:, 0, d, :, :].rearrange("p a t -> p (a t)"), h) for d in range(2))
        f0, f1 = blocks(0, h), blocks(1, h)

        def times(x, f):
            return VE.do(lambda e: e.tensor_tensor(x, x, f.unsqueeze(2).to_broadcast([P, nb, h]), ALU.mult))

        VE.wait(*marks.get("bp", f_ready[0] + f_ready[1]))
        marks["qf"] = [times(q0[:, :, 1, :], f0[:, :, 0]), times(q1[:, :, 0, :], f1[:, :, 1])]
        if 2 * h < T:
            marks["kf"] = [times(k0[:, :, 0, :], f0[:, :, 1]), times(k1[:, :, 1, :], f1[:, :, 0])]
            VE.wait(*marks["kf"])
            marks["bp"] = [VE.do(lambda e, f=f: e.tensor_tensor(f[:, :, 0], f[:, :, 0], f[:, :, 1], ALU.mult))
                           for f in (f0, f1)]

    def level_wide():
        PE.wait(*marks["qf"], *marks["kf"])
        marks["aw"] = []
        for d in range(2):
            b = take("m")
            ks, ts = (slice(0, P), slice(P, T)) if d == 0 else (slice(P, T), slice(0, P))
            for h in range(NH):
                op = lambda e, b=b, d=d, h=h, ks=ks, ts=ts: e.matmul(
                    bank[b][:, h * P:(h + 1) * P], K[:, 0, d, h, ks], QF[:, d, h, ts], start=True, stop=True)
                m = PE.do(op) if h == NH - 1 else PE.go(op)
            SC.wait(m, *marks["turned"])
            a = SC.do(lambda e, b=b, d=d, ts=ts: e.activation(
                A[:, d, :, ts], bank[b][:, :].rearrange("p (h t) -> p h t", h=NH), ACT.Copy))
            freed[b].append(a)
            marks["aw"].append(a)
        marks["wide_pe"] = m
        grow(P, m)

    def outputs():
        PE.wait(marks["ap"], *marks["aw"], *marks["a"], *marks["qf"], *marks["state"], *marks["vx"])
        marks["o"] = []
        for hp in range(2):
            b = take("m")
            for j in range(2):
                h = 2 * hp + j
                o = bank[b][:, j * T:(j + 1) * T]
                for t in range(2):
                    PE.go(lambda e, o=o, h=h, t=t: e.matmul(o, VX[:, t, h, :], A[:, t, h, :], start=t == 0,
                                                            stop=False))
                PE.go(lambda e, o=o, h=h: e.matmul(o, ST[:, 0, h, :], QF[:, 0, h, :], start=False, stop=False))
                op = lambda e, o=o, h=h: e.matmul(o, ST[:, 1, h, :], QF[:, 1, h, :], start=False, stop=True)
                m = PE.do(op) if j == 1 else PE.go(op)
            marks["o"].append((b, m))

    def readout_squares():
        for hp, (b, m) in enumerate(marks["o"]):
            a = evict(b, m, flat(ON[:, 2 * hp:2 * hp + 2, :]), after=marks["vx"])
            SC.wait(a, *marks["t1_free"])
            a = SC.do(lambda e, hp=hp: e.activation(SQo[:, 2 * hp:2 * hp + 2, :], ON[:, 2 * hp:2 * hp + 2, :],
                                                    ACT.Square))
            marks["sqo", hp] = a

    def readout_columns():
        b = take("m")
        for h in range(NH):
            PE.wait(marks["sqo", h // 2])
            for t in range(2):
                m = column(b, 2 * h + t, SQo[:, h, t * P:(t + 1) * P], h + t == 0, h + t == NH)
        marks["rco"] = rstd_columns(b, 8, P, 8, m)

    def readout_norm():
        for hp in range(2):
            b = take("m")
            r = rows(b, [wide(8 + 4 * hp + i) for i in range(4)], marks["rco"])
            VE.wait(r, marks["sg"])
            for j in range(2):
                h = 2 * hp + j
                g = VE.do(lambda e, h=h, b=b, j=j: e.scalar_tensor_tensor(
                    RSo[:, h, :], bank[b][:, j * T:(j + 1) * T], v("onorm", h, 1), SG[:, h, :], ALU.mult, ALU.mult))
            freed[b].append(g)
            VE.wait(g)
            y = VE.do(lambda e, hp=hp: e.tensor_tensor(ON[:, 2 * hp:2 * hp + 2, :], ON[:, 2 * hp:2 * hp + 2, :],
                                                       RSo[:, 2 * hp:2 * hp + 2, :], ALU.mult))
            SC.wait(y, marks["wide_pe"])
            yh = SC.do(lambda e, hp=hp: e.activation(YHh[:, 2 * hp:2 * hp + 2, :], ON[:, 2 * hp:2 * hp + 2, :],
                                                     ACT.Copy))
            VE.wait(yh)
            yl = VE.do(lambda e, hp=hp: e.tensor_tensor(YHl[:, 2 * hp:2 * hp + 2, :], ON[:, 2 * hp:2 * hp + 2, :],
                                                        YHh[:, 2 * hp:2 * hp + 2, :].bitcast(F32), ALU.subtract))
            marks["yh", hp] = [yh, yl]

    dft_l = c("dft_l").rearrange("p (t s n) -> p t s n", t=2, s=2)

    def fourier_1():
        PE.wait(*marks["fu"])
        marks["t1"] = []
        for t in range(2):
            for gp in range(2):
                b = take("m")
                for j in range(2):
                    op = lambda e, b=b, t=t, g=2 * gp + j, j=j: e.matmul(
                        bank[b][:, j * T:(j + 1) * T], FU[:, g, t * P:(t + 1) * P], c("dft_c"), start=True, stop=True)
                    m = PE.do(op) if j == 1 else PE.go(op)
                marks["t1"].append(evict(b, m, flat(T1[:, t, 2 * gp:2 * gp + 2, :]),
                                         after=[marks["state_pe"]]))
        marks["fu_free"] = m

    def fourier_2():
        PE.wait(*marks["t1"])
        for gp in range(2):
            b = take("m")
            for j in range(2):
                g = 2 * gp + j
                for n, (t, s) in enumerate([(0, 0), (1, 0), (0, 1), (1, 1)]):
                    op = lambda e, b=b, g=g, j=j, t=t, s=s, n=n: e.matmul(
                        bank[b][:, j * T:(j + 1) * T], T1[:, t, g, s * P:(s + 1) * P], dft_l[:, t, s, :],
                        start=n == 0, stop=n == 3)
                    m = PE.do(op) if (j, n) == (1, 3) else PE.go(op)
            a = evict(b, m, flat(YFh[:, 2 * gp:2 * gp + 2, :]), after=[marks["diag_pe"], marks["fu_free"]])
            VE.wait(a)
            y = VE.do(lambda e, b=b, gp=gp: e.tensor_tensor(
                flat(YFl[:, 2 * gp:2 * gp + 2, :]), bank[b][:, :], flat(YFh[:, 2 * gp:2 * gp + 2, :]).bitcast(F32),
                ALU.subtract))
            freed[b].append(y)
            marks["yf", gp] = [a, y]
        marks["t1_free"] = [m]

    for i in range(20):
        if 2 <= i < 8:
            m = h1c_done = both_inputs(i)
        else:
            s, h, l = chunk("w_in", i)
            b = take("g")
            for k in range(KT):
                PE.wait(his[0][k], h1[0][k])
                for j in range(2):
                    m = mm3(bank[b][:, j * T:(j + 1) * T], h, l, (j * KT + k) * P, hx[:, k, :], hl[:, k, :],
                            k + j == 0, k == KT - 1)
            chunk_done(s, m)
        if i < 2:
            marks.setdefault("q", []).append(evict(b, m, flat(Q[:, 2 * i:2 * i + 2, :]), ACT.Silu))
        elif i < 8:
            if i == 5:
                ctx_decay()
                x_start()
        elif i < 10:
            marks.setdefault("fu", []).append(
                evict(b, m, flat(FU[:, 2 * (i - 8):2 * (i - 8) + 2, :]), after=kc))
        elif i < 12:
            marks["sg"] = evict(b, m, flat(SG[:, 2 * (i - 10):2 * (i - 10) + 2, :]), ACT.Silu,
                                after=[marks["state_pe"]])
        elif i < 16:
            marks["ga"] = evict(b, m, flat(GA[:, 2 * (i - 12):2 * (i - 12) + 2, :]), ACT.Sigmoid, after=[h1c_done])
        else:
            marks["gb"] = evict(b, m, flat(GB[:, 2 * (i - 16):2 * (i - 16) + 2, :]), ACT.Sigmoid, after=[h1c_done])
        if i == 6:
            ctx_turn()
            diagonal()
            level(0)
        elif i == 7:
            level(1)
        elif i == 8:
            v_turn()
            level(2)
        elif i == 9:
            ctx_state()
            level(3)
        elif i == 10:
            fourier_1()
            level(4)
        elif i == 11:
            level(5)
        elif i == 12:
            fourier_2()
            level(6)
        elif i == 13:
            level_wide()
        elif i == 14:
            outputs()
            readout_squares()
        elif i == 15:
            readout_columns()
        elif i == 16:
            readout_norm()
    hx_done = m

    def quad(name, i, xh, xl):
        s, h, l = chunk(name, i)
        out = []
        for jp in range(2):
            b = take("g")
            for k in range(NH):
                for j in range(2):
                    m = mm3(bank[b][:, j * T:(j + 1) * T], h, l, ((2 * jp + j) * NH + k) * P, xh[:, k, :], xl[:, k, :],
                            k + j == 0, k == NH - 1)
            out.append((b, m))
        chunk_done(s, m)
        return out

    def gated(b, m, g, ready, f):
        VE.wait(m, ready)
        a = VE.do(lambda e: e.tensor_tensor(flat(g[:, f:f + 2, :]), bank[b][:, :], flat(g[:, f:f + 2, :]), ALU.mult))
        freed[b].append(a)
        return a

    PE.wait(*marks["yf", 0], *marks["yf", 1])
    ya = {}
    for i in range(2):
        for jp, (b, m) in enumerate(quad("w_a", i, YFh, YFl)):
            f = 4 * i + 2 * jp
            ya[f] = gated(b, m, GA, marks["ga"], f)
    PE.wait(*marks["yh", 0], *marks["yh", 1])
    mg = {}
    for i in range(2):
        for jp, (b, m) in enumerate(quad("w_b", i, YHh, YHl)):
            f = 4 * i + 2 * jp
            yb = gated(b, m, GB, marks["gb"], f)
            VE.wait(yb, ya[f])
            s = VE.do(lambda e, f=f: e.tensor_tensor(GA[:, f:f + 2, :], GA[:, f:f + 2, :], GB[:, f:f + 2, :],
                                                     ALU.add))
            SC.wait(s, hx_done)
            a = SC.do(lambda e, f=f: e.activation(MGh[:, f:f + 2, :], GA[:, f:f + 2, :], ACT.Copy))
            VE.wait(a)
            y = VE.do(lambda e, f=f: e.tensor_tensor(MGl[:, f:f + 2, :], GA[:, f:f + 2, :],
                                                     MGh[:, f:f + 2, :].bitcast(F32), ALU.subtract))
            mg[f] = mg[f + 1] = [a, y]

    mod_ready = {}

    def mods(a, n):
        prep_upto(max(order[("ada_hi", i)] for i in range(a // 2, (a + n) // 2)))
        VE.wait(side_done[(a + n) // 2 - 1])
        mod_ready[a] = VE.do(lambda e: e.tensor_tensor(MODX[:, a:a + n], MODX[:, a:a + n], v("ada_b", 16 + a, n),
                                                       ALU.add))

    mods(0, 32)
    VE.wait(mod_ready[0])
    g2 = [VE.do(lambda e: e.tensor_copy(G2[:, :, 0], ones[:, 0:KT])),
          VE.do(lambda e: e.tensor_tensor(G2[:, :, 1], v("final_g"), v("final_g"), ALU.mult))]
    gg = VE.do(lambda e: e.tensor_tensor(GG[:, :], v("final_g"), v("norm1_g_2"), ALU.mult))
    a2 = VE.do(lambda e: e.scalar_tensor_tensor(A2[:, :], MODX[:, 16:24], 1.0, v("norm2_g"), ALU.add, ALU.mult))

    def add_to_x(b, ready, f, gate, js=(0, 1)):
        VE.wait(ready)
        for j in js:
            g = 1.0 if gate is None else MODX[:, gate + f + j:gate + f + j + 1]
            a = VE.do(lambda e, j=j, g=g: e.scalar_tensor_tensor(
                XR[:, f + j, :], bank[b][:, j * T:(j + 1) * T], g, XR[:, f + j, :], ALU.mult, ALU.add))
        freed[b].append(a)
        return a

    def squares(sq, f, after, n=2):
        SC.wait(after)
        return SC.do(lambda e: e.activation(sq[:, f:f + n, :], XR[:, f:f + n, :], ACT.Square))

    def square_columns(b, sq, f, ready, n=2):
        PE.wait(ready)
        for k in range(f, f + n):
            for t in range(2):
                m = column(b, t, sq[:, k, t * P:(t + 1) * P], k + t == 0, k == KT - 1)
        return m

    def project(name, xh, xl, ready, ks, gate, sq):
        bs = take("m")
        warm(ACT.Sqrt)
        prev = None
        for i in range(3):
            b, m = pair_when(name, i, xh, xl, ready, ks)
            now = squares(sq, 2 * i, add_to_x(b, m, 2 * i, gate))
            if i:
                square_columns(bs, sq, 2 * i - 2, prev)
            prev = now
        ends = pair_when(name, 3, xh, xl, ready, ks, True)
        parts = [squares(sq, 6 + j, add_to_x(b, m, 6, gate, (j,)), 1) for j, (b, m) in enumerate(ends)]
        square_columns(bs, sq, 4, prev)
        for j in range(2):
            done = square_columns(bs, sq, 6 + j, parts[j], 1)
        return bs, done, ends[1][1]

    def normed(rs, b, gain, shift, tmp, xh, xl):
        out = []
        VE.wait(rs)
        hs = []
        for k in range(KT + 1):
            if k < KT:
                t = VE.do(lambda e, k=k: e.scalar_tensor_tensor(tmp[:, k, :], XR[:, k, :], gain[:, k:k + 1],
                                                                bank[b][:, 0:T], ALU.mult, ALU.mult))
                SC.wait(t)
                if shift is None:
                    hs.append(SC.do(lambda e, k=k: e.activation(xh[:, k, :], tmp[:, k, :], ACT.Copy)))
                else:
                    hs.append(SC.do(lambda e, k=k: e.activation(xh[:, k, :], tmp[:, k, :], ACT.Identity,
                                                                bias=shift[:, k:k + 1])))
                if k == KT - 1:
                    freed[b].append(t)
            if k and shift is None:
                PO.wait(hs[k - 1])
                out.append([hs[k - 1], PO.do(lambda e, k=k - 1: e.tensor_tensor(
                    xl[:, k, :], tmp[:, k, :], xh[:, k, :].bitcast(F32), ALU.subtract))])
            elif k:
                VE.wait(hs[k - 1])
                out.append([hs[k - 1], VE.do(lambda e, k=k - 1: e.scalar_tensor_tensor(
                    xl[:, k, :], tmp[:, k, :], shift[:, k:k + 1], xh[:, k, :].bitcast(F32), ALU.add, ALU.subtract))])
        return out

    def pair_when(name, i, xh, xl, ready, ks=range(KT), apart=False):
        s, h, l = chunk(name, i)
        bs = [take("g"), take("g")] if apart else [take("g")] * 2
        todo = [(n, k, j) for j in range(2) for n, k in enumerate(ks)] if apart else [
            (n, k, j) for n, k in enumerate(ks) for j in range(2)]
        marks_ = []
        for n, k, j in todo:
            PE.wait(*ready[k])
            m = mm3(bank[bs[j]][:, j * T:(j + 1) * T], h, l, (j * KT + k) * P, xh[:, k, :], xl[:, k, :],
                    n == 0 and (j == 0 or apart), n == KT - 1)
            if n == KT - 1:
                marks_.append((bs[j], m))
        chunk_done(s, m)
        return marks_ if apart else (bs[0], m)

    SQ1 = area("SQ1", [P, KT, T], 48)
    TMP1 = area("TMP1", [P, KT, T], 40)
    H2h = area("H2h", [P, KT, T], 24, F32R)
    H2l = area("H2l", [P, KT, T], 32, F32R)
    bs, m, merge_done = project("w_out", MGh, MGl, mg, range(KT), 0, SQ1)
    rc = rstd_columns(bs, 2, D, 0, m)
    warm(ACT.Silu)
    br = claim(3)
    h2 = normed(rows(br, [wide(0), wide(1)], rc), br, A2, MODX[:, 8:16], TMP1, H2h, H2l)

    BI = area("BI", [P, 8, 384], 72)
    PW = area("PW", [P, 2, P], 96)
    SY.wait(merge_done)
    bias_in = load(SY, "bias", BI[:, :, :], io["bias"])
    pw_in = load(SY, "pool_w", PW[:, :, :], io["pool_w"])
    NA = 8
    AH = area("AH", [P, NA, T], 0, F32R)
    AL = area("AL", [P, NA, T], 8, F32R)
    Y = [area(f"Y{i}", [P, 2, T], (56, 58, 64, 66)[i]) for i in range(4)]
    SI = [area(f"SI{i}", [P, T], 60 + i) for i in range(2)]
    AT = [area(f"AT{i}", [P, T], 62 + i) for i in range(2)]
    cw = v("conv_w").rearrange("p (f w) -> p f w", w=9)
    taps = [(dr, dc) for dr in (0, -1, 1) for dc in (0, -1, 1) if (dr, dc) != (0, 0)]
    ring["m"] = [3]
    acc = [claim(b) for b in (4, 5, 6, 7)]
    mids = {}
    a_done, a_read, conv_done, silu_done, ah_done = {}, {}, {}, {}, {}
    y_free = [[], [], [], []]

    def up(i):
        b, m = pair_when("ffn_up", i, H2h, H2l, h2)
        y = Y[i % 4]
        SC.wait(m, *y_free[i % 4])
        for s in range(2):
            f = i + 22 * s
            mid = SC.do(lambda e, s=s, f=f: e.activation(
                y[:, s, :], bank[b][:, s * T:(s + 1) * T], ACT.Identity, bias=v("conv_b", f, 1), scale=cw[:, f, 4:5]))
        mids[i] = b, mid

    def convolve(i):
        y = Y[i % 4]
        b, mid = mids[i]
        VE.wait(mid)
        prev = [mid, mid]
        for dr, dc in taps:
            for s in range(2):
                f = i + 22 * s
                z = bank[b][:, s * T:(s + 1) * T].rearrange("p (r c) -> p r c", c=64)
                o = y[:, s, :].rearrange("p (r c) -> p r c", c=64)
                r0, r1, c0, c1 = max(0, -dr), min(4, 4 - dr), max(0, -dc), min(64, 64 - dc)
                w = cw[:, f, 3 * (dr + 1) + dc + 1:3 * (dr + 1) + dc + 2]
                VE.wait(prev[s])
                prev[s] = VE.do(lambda e, o=o[:, r0:r1, c0:c1], z=z[:, r0 + dr:r1 + dr, c0 + dc:c1 + dc], w=w:
                                e.scalar_tensor_tensor(o, z, w, o, ALU.mult, ALU.add))
        freed[b].append(prev[1])
        conv_done[i] = prev

    def gate(i):
        SC.wait(conv_done[i][0])
        silu_done[i] = SC.do(lambda e: e.activation(SI[i % 2][:, :], Y[i % 4][:, 0, :], ACT.Silu))

    def gated_high(i):
        at = AT[i % 2]
        VE.wait(silu_done[i], conv_done[i][1])
        m = VE.do(lambda e: e.tensor_tensor(at[:, :], SI[i % 2][:, :], Y[i % 4][:, 1, :], ALU.mult))
        y_free[i % 4] = [m]
        SC.wait(m, merge_done, *a_read.get(i - NA, []))
        ah_done[i] = SC.do(lambda e: e.activation(AH[:, i % NA, :], at[:, :], ACT.Copy))

    def gated_low(i):
        at = AT[i % 2]
        VE.wait(ah_done[i], *a_read.get(i - NA, []))
        a_done[i] = [ah_done[i], VE.do(lambda e: e.tensor_tensor(
            AL[:, i % NA, :], at[:, :], AH[:, i % NA, :].bitcast(F32), ALU.subtract))]

    def contract(name, j, xh, xl, slots, ready, last, tell):
        s, h, l = chunk(name, j)
        ends = last == 2 * j + 1
        blocks_ = [(kk_, f) for kk_ in range(2) for f in range(KT)]
        if ends:
            blocks_ = [(kk_, f) for fp in range(4) for kk_ in range(2) for f in (2 * fp, 2 * fp + 1)]
        for n, (kk_, f) in enumerate(blocks_):
            k = 2 * j + kk_
            PE.wait(*ready[k])
            m = mm3(bank[acc[f // 2]][:, f % 2 * T:(f % 2 + 1) * T], h, l, (kk_ * KT + f) * P,
                    xh[:, k % slots, :], xl[:, k % slots, :], k == 0 and f % 2 == 0, ends and n % 4 == 3 or n == 15)
            if ends and n % 4 == 3:
                tell(n // 4, m)
        chunk_done(s, m)
        return m

    def down(j):
        m = contract("ffn_down", j, AH, AL, NA, a_done, 21, residual)
        a_read[2 * j] = a_read[2 * j + 1] = [m]

    SQ2 = area("SQ2", [P, KT, T], 48)
    rb = 3
    sqs = {}

    def residual(i, m):
        sqs[i] = squares(SQ2, 2 * i, add_to_x(acc[i], m, 2 * i, 24))
        if i == 0:
            claim(rb)
        if i >= 2:
            residual_columns(i - 2)

    def residual_columns(i):
        PE.wait(sqs[i], *g2)
        for k in (2 * i, 2 * i + 1):
            for t in range(2):
                op = lambda e, k=k, t=t: e.matmul(
                    bank[rb][:, 2 * t:2 * t + 2], SQ2[:, k, t * P:(t + 1) * P], G2[:, k, :],
                    start=k == 0 and t == 0, stop=k == KT - 1, skip_group_check=True)
                m = PE.do(op) if (k, t) == (KT - 1, 1) else PE.go(op)
        return m

    for i in range(24):
        if i < 22:
            up(i)
        if i >= 2:
            gated_high(i - 2)
        if i < 22:
            convolve(i)
        if i >= 2:
            gated_low(i - 2)
        if 1 <= i < 23:
            gate(i - 1)
        if i == 22:
            warm(ACT.Sqrt)
        if i >= 5 and i % 2:
            down((i - 5) // 2)
    down(10)
    residual_columns(2)
    m = residual_columns(3)
    down_done = m
    ring["m"] = [3, 4, 5, 6, 7]
    VE.wait(m)
    t = [VE.do(lambda e: e.tensor_scalar(RC[:, 0:2], bank[rb][:, 0:4:2], 1.0 / D, EPS, ALU.mult, ALU.add)),
         VE.do(lambda e: e.tensor_scalar(RC[:, 2:4], bank[rb][:, 1:4:2], 1.0 / D, None, ALU.mult))]
    freed[rb] += t
    VE.wait(*t)
    t = VE.do(lambda e: e.scalar_tensor_tensor(RC[:, 2:4], RC[:, 0:2], EPS, RC[:, 2:4], ALU.mult, ALU.add))
    SC.wait(t)
    t = SC.do(lambda e: e.activation(RC[:, 0:4], RC[:, 0:4], ACT.Sqrt))
    VE.wait(t)
    r12 = VE.do(lambda e: e.reciprocal(RC[:, 0:4], RC[:, 0:4]))
    b2 = take("m")
    rs2 = rows(b2, [wide(2), wide(3)], r12)
    b1 = take("m")
    rs1 = rows(b1, [wide(0), wide(1)], r12)

    H3h = area("H3h", [P, KT, T], 24, F32R)
    H3l = area("H3l", [P, KT, T], 32, F32R)
    TMP2 = area("TMP2", [P, KT, T], 40)
    VE.wait(gg)
    h3 = normed(rs2, b2, GG, None, TMP2, H3h, H3l)
    VE.wait(rs1)
    for f in range(KT):
        x = VE.do(lambda e, f=f: e.scalar_tensor_tensor(XR[:, f, :], XR[:, f, :], v("final_g", f, 1),
                                                        bank[b1][:, 0:T], ALU.mult, ALU.mult))
    freed[b1].append(x)
    VE.wait(x)
    PP = area("PP", [P, 20, T], 0)
    SQq = [area(f"SQq{i}", [P, 2, T], 20 + 2 * i) for i in range(2)]
    PT = area("PT", [P, 3, 8, P], 56)
    VV = area("VV", [P, 2, NH, P], 68)
    SCR = area("SCR", [P, 8 * 384], 84)
    S0 = SCR[:, 0:8 * P].rearrange("p (h s) -> p h s", h=8)
    S1 = SCR[:, 8 * P:8 * 384].rearrange("p (h s) -> p h s", h=8)
    MXh = area("MXh", [P, KT, T], 40, F32R)
    MXl = area("MXl", [P, KT, T], 48, F32R)
    Z = area("Z", [P, 2, T], 72)
    YC = area("YC", [P, 2, T], 74)
    M2 = area("M2", [P, 2, T], 76)
    M4 = area("M4", [P, 2, T], 78)
    M8 = area("M8", [P, T], 80)
    M16 = area("M16", [P, T], 81)
    PM = area("PM", [P, 2, T], 82)
    UP = area("UP", [P, 2, T], 97)
    pp, qk, qk_sq, qk_rc, qk_cols = {}, {}, {}, {}, {}
    halves2 = c("blk")[:, 0:P:64]

    def qk_columns(i):
        PE.wait(qk_sq[i], con_in)
        b = take("m")
        for j in range(2):
            for t in range(2):
                o = 2 * (2 * j + t)
                op = lambda e, j=j, t=t, o=o: e.matmul(bank[b][:, o:o + 2], SQq[i % 2][:, j, t * P:(t + 1) * P],
                                                       halves2, start=True, stop=True)
                m = PE.do(op) if j + t == 2 else PE.go(op)
        qk_cols[i] = m
        qk_rc[i] = rstd_columns(b, 8, 64, 16 + 8 * i, m)

    def qk_norm(i):
        b = take("m")
        at = 16 + 8 * i
        PE.wait(qk_rc[i], con_in)
        for n in range(8):
            half = slice(64 * (n % 2), 64 * (n % 2) + 64)
            col = RC[:, at + n:at + n + 1].to_broadcast([P, 64])
            op = lambda e, n=n, half=half, col=col: e.matmul(bank[b][half, n // 2 * P:(n // 2 + 1) * P], col, ident,
                                                            start=True, stop=True)
            r = PE.do(op) if n == 7 else PE.go(op)
        g = v("q_g") if i < 2 else v("k_g")
        VE.wait(r, pp[i])
        x = PP[:, 2 * i:2 * i + 2, :].rearrange("p a b -> p (a b)")
        qk[i] = VE.do(lambda e: e.scalar_tensor_tensor(x, x, g, bank[b][:, :], ALU.mult, ALU.mult))
        freed[b].append(qk[i])

    S = [S0, S1]
    probs = {}

    def scores(g):
        PE.wait(*qk.values())
        VE.wait(bias_in)
        bi = BI[:, :, :].rearrange("p a b -> p (a b)")
        ready = []
        for t, n0, per in ((0, 4 * g, 4), (1, 4 * g, 2), (1, 4 * g + 2, 2)):
            ns = P * (t + 1)
            b = take("m")
            for n in range(per):
                h = HORDER[n0 + n]
                lo_p, tile = 64 * (h % 2), h // 2
                op = lambda e, b=b, n=n, ns=ns, lo_p=lo_p, tile=tile, t=t: e.matmul(
                    bank[b][:, n * ns:(n + 1) * ns], PP[lo_p:lo_p + 64, tile, t * P:(t + 1) * P],
                    PP[lo_p:lo_p + 64, 4 + tile, 0:ns], start=True, stop=True)
                m = PE.do(op) if n == per - 1 else PE.go(op)
            VE.wait(m)
            dst = S[t][:, n0:n0 + per, :].rearrange("p a b -> p (a b)")
            off = 8 * P * t + n0 * ns
            a = VE.do(lambda e, b=b, dst=dst, off=off: e.scalar_tensor_tensor(
                dst, bank[b][:, :], 0.125, bi[:, off:off + 512], ALU.mult, ALU.add))
            freed[b].append(a)
            ready.append(a)
        VE.wait(*ready)
        mx = [VE.do(lambda e, t=t, g=g: e.tensor_reduce(MX[:, 8 * t + 4 * g:8 * t + 4 * g + 4],
                                                       S[t][:, 4 * g:4 * g + 4, :], AX.X, ALU.max, negate=True))
              for t in range(2)]
        SC.wait(*mx)
        for t in range(2):
            for n in range(4 * g, 4 * g + 4):
                ex = SC.do(lambda e, t=t, n=n, g=g: e.activation(
                    S[t][:, n, :], S[t][:, n, :], ACT.Exp, bias=MX[:, 8 * t + n:8 * t + n + 1],
                    accum_out=SM[:, 8 * g + 4 * t + n % 4:8 * g + 4 * t + n % 4 + 1]))
        probs[g] = ex

    def probabilities(g):
        VE.wait(probs[g])
        rc = VE.do(lambda e: e.reciprocal(SM[:, 8 * g:8 * g + 8], SM[:, 8 * g:8 * g + 8]))
        VE.wait(rc)
        probs["n", g] = [VE.do(lambda e, t=t: e.tensor_tensor(
            S[t][:, 4 * g:4 * g + 4, :], S[t][:, 4 * g:4 * g + 4, :],
            SM[:, 8 * g + 4 * t:8 * g + 4 * t + 4].unsqueeze(2).to_broadcast([P, 4, P * (t + 1)]), ALU.mult))
            for t in range(2)]

    def turn_probabilities(g):
        srcs = [[S[t][:, 4 * g + n, s:s + P] for n in range(4)] for t, s in ((0, 0), (1, 0), (1, P))]
        outs = [PT[:, blk, 4 * g:4 * g + 4, :].rearrange("p a b -> p (a b)") for blk in range(3)]
        probs["t", g] = transposes(srcs, outs, probs["n", g], [down_done])

    pool_m = {}

    def pooling():
        U = PP[:, 12:14, :]
        VE.wait(pp[6])

        def shifted(dst, src, w):
            a = VE.do(lambda e: e.tensor_copy(dst[..., 0:w], src[..., 0:w]))
            return [a, VE.do(lambda e: e.tensor_tensor(dst[..., w:T], src[..., w:T], src[..., 0:T - w], ALU.add))]

        VE.wait(*shifted(M2[:, :, :], U, 1))
        VE.wait(*shifted(M4[:, :, :], M2[:, :, :], 2))
        VE.wait(*shifted(M8[:, :], M4[:, 1, :], 4))
        VE.wait(*shifted(M16[:, :], M8[:, :], 8))
        pr = c("poolr").rearrange("p (f n) -> p f n", f=2)
        groups = [(0, M2[0:64, 0, :], 2), (0, M4[64:128, 0, :], 4), (1, M8[0:64, :], 8), (1, M16[64:128, :], 16)]
        for n, (f, src, w) in enumerate(groups):
            lo_p = 64 * (n % 2)
            y = VE.do(lambda e, f=f, src=src, w=w, lo_p=lo_p: e.tensor_scalar(
                PM[lo_p:lo_p + 64, f, :], src, 1.0 / w, None, ALU.mult))
        VE.wait(y)
        y = VE.do(lambda e: e.tensor_tensor(PM[:, :, 0:16], PM[:, :, 0:16], pr, ALU.mult))
        VE.wait(y)
        pool_m["m"] = VE.do(lambda e: e.tensor_tensor(PM[:, :, :], PM[:, :, :], U, ALU.subtract))

    def pool_product():
        PE.wait(pool_m["m"], pw_in)
        b = take("m")
        for f in range(2):
            m = PE.do(lambda e, f=f: e.matmul(bank[b][:, f * T:(f + 1) * T], PW[:, f, :], PM[:, f, :], start=True,
                                              stop=True))
        VE.wait(m)
        for f in range(2):
            y = VE.do(lambda e, f=f: e.tensor_scalar(UP[:, f, :], bank[b][:, f * T:(f + 1) * T],
                                                     v("pool_scale", f, 1), None, ALU.mult))
        freed[b].append(y)
        mix[6] = mix[7] = to_mix(UP[:, :, :], 6, 2, y)

    def short_conv():
        VE.wait(pp[7], pp[8])
        z = VE.do(lambda e: e.tensor_tensor(Z[:, :, :], PP[:, 14:16, :], PP[:, 16:18, :], ALU.mult))
        VE.wait(z)
        cw2 = v("conv_w_2").rearrange("p (f w) -> p f w", w=3)
        for f in range(2):
            y = VE.do(lambda e, f=f: e.tensor_scalar(YC[:, f, :], Z[:, f, :], cw2[:, f, 2:3], None, ALU.mult))
        for s in (1, 2):
            VE.wait(y)
            for f in range(2):
                y = VE.do(lambda e, f=f, s=s: e.scalar_tensor_tensor(
                    YC[:, f, s:T], Z[:, f, 0:T - s], cw2[:, f, 2 - s:3 - s], YC[:, f, s:T], ALU.mult, ALU.add))
        pool_m["conv"] = y

    def short_conv_gate():
        VE.wait(pool_m["conv"], pp[9])
        y = VE.do(lambda e: e.tensor_tensor(YC[:, :, :], YC[:, :, :], PP[:, 18:20, :], ALU.mult))
        mix[4] = mix[5] = to_mix(YC[:, :, :], 4, 2, y)

    mix = {}

    def to_mix(src, k, n, after):
        SC.wait(after, *h3[-1])
        a = SC.do(lambda e: e.activation(MXh[:, k:k + n, :], src, ACT.Copy))
        VE.wait(a)
        return [a, VE.do(lambda e: e.tensor_tensor(MXl[:, k:k + n, :], src, MXh[:, k:k + n, :].bitcast(F32),
                                                   ALU.subtract))]

    for i in range(10):
        b, m = pair_when("w_in_2", i, H3h, H3l, h3)
        pp[i] = evict(b, m, flat(PP[:, 2 * i:2 * i + 2, :]), after=[down_done])
        if i < 4:
            SC.wait(pp[i], *([qk_cols[i - 2]] if i >= 2 else []))
            qk_sq[i] = SC.do(lambda e, i=i: e.activation(SQq[i % 2][:, :, :], PP[:, 2 * i:2 * i + 2, :], ACT.Square))
        if 2 <= i < 6:
            qk_norm(i - 2)
        if 1 <= i < 5:
            qk_columns(i - 1)
        if i == 6:
            srcs = [[PP[:, 8 + n, t * P:(t + 1) * P] for n in range(4)] for t in range(2)]
            vv = transposes(srcs, [flat(VV[:, t, :, :]) for t in range(2)], [pp[4], pp[5]], [down_done, x])
            scores(0)
        if i == 7:
            scores(1)
            probabilities(0)
            pooling()
            probabilities(1)
        if i == 8:
            turn_probabilities(0)
            short_conv()
    turn_probabilities(1)
    pool_product()
    short_conv_gate()
    PE.wait(*probs["t", 0], *probs["t", 1], *vv)
    for tp in range(2):
        b = take("m")
        for j in range(2):
            for par in range(2):
                h = 2 * (2 * tp + j) + par
                n = HORDER.index(h)
                o = bank[b][64 * par:64 * par + 64, j * T:(j + 1) * T]
                w = [VV[:, t, h // 2, 64 * par:64 * par + 64] for t in range(2)]
                PE.go(lambda e, o=o, w=w, n=n: e.matmul(o[:, 0:P], w[0], PT[:, 0, n, :], start=True, stop=True))
                PE.go(lambda e, o=o, w=w, n=n: e.matmul(o[:, P:T], w[0], PT[:, 1, n, :], start=True, stop=False))
                m = PE.do(lambda e, o=o, w=w, n=n: e.matmul(o[:, P:T], w[1], PT[:, 2, n, :], start=False, stop=True))
        src = bank[b][:, :].rearrange("p (a t) -> p a t", a=2)
        mix[2 * tp] = mix[2 * tp + 1] = to_mix(src, 2 * tp, 2, m)
        freed[b].append(mix[2 * tp][1])

    SQ3 = area("SQ3", [P, KT, T], 72)
    TMP3 = area("TMP3", [P, KT, T], 0)
    H4h = area("H4h", [P, KT, T], 8, F32R)
    H4l = area("H4l", [P, KT, T], 16, F32R)
    ready = [mix[k] for k in range(KT)]
    bs, m, out2_done = project("w_out_2", MXh, MXl, ready, [6, 7, 4, 5, 0, 1, 2, 3], None, SQ3)
    rc = rstd_columns(bs, 2, D, 0, m)
    br = claim(3)
    h4 = normed(rows(br, [wide(0), wide(1)], rc), br, v("norm2_g_2"), None, TMP3, H4h, H4l)

    NF = 8
    FH = area("FH", [P, NF, T], 24, F32R)
    FL = area("FL", [P, NF, T], 32, F32R)
    FR = [area(f"FR{i}", [P, 2, T], 88 + 2 * i) for i in range(2)]
    FQ = [area(f"FQ{i}", [P, 2, T], 92 + 2 * i) for i in range(2)]
    f_done, f_read = {}, {}
    fr_free = [[], []]
    ring["m"] = [3]
    acc = [claim(b) for b in (4, 5, 6, 7)]
    s_out = sem("stores")

    def mlp_out(i, m):
        x = add_to_x(acc[i], m, 2 * i, None)
        SY.wait(x)
        SY.go(lambda e: e.dma_start(io["out"][:, 2 * i:2 * i + 2, :], XR[:, 2 * i:2 * i + 2, :]).then_inc(s_out, 16))

    def mlp_up(i):
        b, m = pair_when("w_mlp1", i, H4h, H4l, h4)
        fr, fq = FR[i % 2], FQ[i % 2]
        at = 2 * i % NF
        SC.wait(m, *fr_free[i % 2])
        r = SC.do(lambda e: e.activation(flat(fr[:, :, :]), bank[b][:, :], ACT.Relu))
        freed[b].append(r)
        VE.wait(r)
        q = VE.do(lambda e: e.tensor_tensor(fq[:, :, :], fr[:, :, :], fr[:, :, :], ALU.mult))
        SC.wait(q, out2_done, *f_read.get(i - NF // 2, []))
        a = SC.do(lambda e: e.activation(FH[:, at:at + 2, :], fq[:, :, :], ACT.Copy))
        VE.wait(a, *f_read.get(i - NF // 2, []))
        l = VE.do(lambda e: e.tensor_tensor(FL[:, at:at + 2, :], fq[:, :, :], FH[:, at:at + 2, :].bitcast(F32),
                                            ALU.subtract))
        fr_free[i % 2] = [l]
        f_done[2 * i] = f_done[2 * i + 1] = [a, l]

    for i in range(18):
        if i < 16:
            mlp_up(i)
        if i >= 2:
            f_read[i - 2] = [contract("w_mlp2", i - 2, FH, FL, NF, f_done, 31, mlp_out)]
    SY.wait((s_out, 64))

    with nc.Block() as block:
        block.sync(SY.replay)
        block.scalar(SC.replay)
        block.vector(VE.replay)
        block.gpsimd(PO.replay)
        block.tensor(PE.replay)


def tiles(w, ft, order=None):
    k, n = w.shape
    b = w.reshape(k // P, P, n // P, P).transpose(2, 1, 0, 3)
    if order is not None:
        b = b[order]
    if ft:
        b = b.reshape(-1, ft, P, k // P, P).transpose(0, 2, 1, 3, 4)
        return np.ascontiguousarray(b.reshape(b.shape[0], P, -1))
    b = b.transpose(2, 1, 0, 3).reshape(k // P // 2, 2, P, n // P, P).transpose(0, 2, 1, 3, 4)
    return np.ascontiguousarray(b.reshape(k // P // 2, P, -1))


def wide_rows(w):
    k, n = w.shape
    return np.ascontiguousarray(w.T.reshape(n // P // 2, 2, P, k).transpose(0, 2, 1, 3).reshape(-1, P, 2 * k))


def columns(a):
    a = np.asarray(a)
    return a.reshape(-1, P).T


def constants():
    con = np.zeros((P, NC), np.float32)

    def put(name, x):
        a, w = CON[name]
        con[:, a:a + w] = x.reshape(P, w)

    put("ident", np.eye(P))
    i = np.arange(P)
    ang = 2 * np.pi * (np.outer(i, i) % P) / P
    put("dft_c", np.concatenate([np.cos(ang), np.sin(ang)], 1))
    j = np.arange(T)
    ang = 2 * np.pi * (np.outer(j, j) % T) / T
    s = 1.0 / np.sqrt(T * P)
    both = np.stack([np.cos(ang) * s, -np.sin(ang) * s])
    put("dft_l", both.reshape(2, 2, P, T).transpose(2, 1, 0, 3))
    put("blk", (i[:, None] // 64 == i[None, :] // 64).astype(np.float32))
    r = np.zeros((P, 2, 16))
    for f in range(2):
        for p in range(P):
            w = 2 ** (2 * f + p // 64 + 1)
            r[p, f] = w / np.minimum(np.arange(16) + 1, w)
    put("poolr", r)
    masks = np.zeros((P, len(LEVELS), P), np.float32)
    for n, h in enumerate(LEVELS):
        masks[:, n] = (i[:, None] // (2 * h) == i[None, :] // (2 * h)) & (i[:, None] // h != i[None, :] // h)
    return con, masks


def bias_rows(rel):
    t, s = np.arange(T)[:, None], np.arange(T)[None, :]
    full = rel[:, np.clip(t - s, -128, 128) + 128]
    full = np.where((s // 64 <= t // 64)[None], full, np.float32(-1e30)).astype(rel.dtype)
    full = full[HORDER]
    a = full[:, 0:P, 0:P].transpose(1, 0, 2).reshape(P, -1)
    b = full[:, P:T, :].transpose(1, 0, 2).reshape(P, -1)
    return np.ascontiguousarray(np.concatenate([a, b], 1).reshape(P, 8, 384))


def kernel(**inputs):
    import concourse.bacc as bacc
    from concourse.bass_utils import run_bass_kernel_spmd as run

    g = {k: np.asarray(x) for k, x in inputs.items()}
    con, masks = constants()
    dup = lambda a: np.concatenate([a.reshape(-1), a.reshape(-1)])[:, None]
    cols = {
        "norm1_g": columns(g["norm1_g"]), "ada_b": columns(g["ada_b"]), "hg_lb": columns(g["hg_lb"]),
        "onorm": columns(g["hg_onorm_g"]), "norm2_g": columns(g["norm2_g"]), "conv_b": columns(g["ffn_conv_b"]),
        "conv_w": g["ffn_conv_w"].reshape(9, 44, P).transpose(2, 1, 0).reshape(P, -1),
        "final_g": columns(g["final_g"]), "norm1_g_2": columns(g["norm1_g_2"]),
        "q_g": dup(g["q_norm_g_2"]), "k_g": dup(g["k_norm_g_2"]),
        "conv_w_2": g["conv_w_2"].reshape(3, 2, P).transpose(2, 1, 0).reshape(P, -1),
        "pool_scale": columns(g["pool_scale_2"]), "norm2_g_2": columns(g["norm2_g_2"]),
        "c2": np.stack([g["c"].reshape(KT, P), g["c_ctx"].reshape(KT, P)], 2).transpose(1, 0, 2).reshape(P, -1),
    }
    pw = np.zeros((P, 2, P), np.float32)
    for n in range(4):
        a = 64 * (n % 2)
        pw[a:a + 64, n // 2, a:a + 64] = g["pool_w_2"][0, n]
    w_in = g["w_in"][0]
    arrays = {
        "vec": np.ascontiguousarray(np.concatenate([cols[n] for n in VEC], 1)),
        "con": con, "masks": masks,
        "xT": np.ascontiguousarray(g["x"][0].T.reshape(KT, P, T).transpose(1, 0, 2)),
        "ctxT": np.ascontiguousarray(g["ctx"][0].T.reshape(KT, P, T).transpose(1, 0, 2)),
        "c_row": np.ascontiguousarray(g["c"].reshape(1, D)),
        "bias": bias_rows(g["rel_bias_2"][0]), "pool_w": pw,
        "c_ctx_row": np.ascontiguousarray(g["c_ctx"].reshape(1, D)),
        "ada_p": tiles(g["ada_w"][0][:, 256:1024], 2),
        "ada_s": wide_rows(np.concatenate([g["ada_w"][0][:, 1024:2048], g["ada_w"][0][:, 0:256]], 1)),
        "ada_hi": wide_rows(g["ada_w"][0][:, 2048:]),
        "w_in": tiles(w_in, 2, [*range(4, 20), *range(0, 4), *range(20, 40)]),
        "w_a": tiles(g["w_a"][0], 4), "w_b": tiles(g["w_b"][0], 4), "w_out": tiles(g["w_out"][0], 2),
        "ffn_up": tiles(g["ffn_up"][0], 2, [f for i in range(22) for f in (i, i + 22)]),
        "ffn_down": tiles(g["ffn_down"][0], 0),
        "w_in_2": tiles(g["w_in_2"][0], 2, [*range(12), 18, 19, *range(14, 18), 12, 13]), "w_out_2": tiles(g["w_out_2"][0], 2),
        "w_mlp1": tiles(g["w_mlp1_2"][0], 2), "w_mlp2": tiles(g["w_mlp2_2"][0], 0),
    }
    nc = bacc.Bacc("TRN2", target_bir_lowering=False, num_devices=1)
    io, feed = {}, {}
    for name, a in arrays.items():
        feed[f"in_{name}"] = a
        io[name] = nc.dram_tensor(f"in_{name}", a.shape, mybir.dt.from_np(a.dtype), kind="ExternalInput").ap()
    io["out"] = nc.dram_tensor("out_x", (P, KT, T), F32, kind="ExternalOutput").ap()
    build(nc, io)
    r = run(nc, [feed], core_ids=[0])
    got = r.results[0]["out_x"]
    return np.ascontiguousarray(got.transpose(2, 1, 0).reshape(1, T, D))
```

```python
import numpy as np

import concourse.bass as bass
from concourse import mybir

F32 = mybir.dt.float32
F32R = mybir.dt.float32r
U8 = mybir.dt.uint8
ALU = mybir.AluOpType
ACT = mybir.ActivationFunctionType
AX = mybir.AxisListType

P = 128
T = 256
D = 1024
KT = D // P
NH = 4
CH = 2048
NRAW, NHI = 4, 3
EPS = 1e-6
SIDE = {3: 1, 4: 2, 5: 2, 6: 2, 7: 2, **{i: 1 for i in range(8, 15)}}
LEVELS = [1, 2, 4, 8, 16, 32, 64]
HORDER = [0, 2, 4, 6, 1, 3, 5, 7]

VEC = {}
_at = 0
for _n, _w in [("norm1_g", 8), ("ada_b", 48), ("hg_lb", 8), ("onorm", 4), ("norm2_g", 8), ("conv_b", 44),
               ("conv_w", 44 * 9), ("final_g", 8), ("norm1_g_2", 8), ("q_g", 1), ("k_g", 1), ("conv_w_2", 6),
               ("pool_scale", 2), ("norm2_g_2", 8), ("c2", 16)]:
    VEC[_n] = (_at, _w)
    _at += _w
NV = _at

CON = {}
_at = 0
for _n, _w in [("ident", 128), ("dft_c", P), ("dft_l", 1024), ("blk", 128), ("poolr", 32)]:
    CON[_n] = (_at, _w)
    _at += _w
NC = _at


class Queue:

    def __init__(self, sem):
        self.sem, self.count, self.ops, self.seen = sem, 0, [], {}

    def wait(self, *marks):
        for sem, value in marks:
            if self.seen.get(sem.name, 0) < value:
                self.seen[sem.name] = value
                self.ops.append(lambda e, s=sem, v=value: e.wait_ge(s, v))

    def do(self, fn):
        self.count += 1
        self.ops.append(lambda e, f=fn: f(e).then_inc(self.sem, 1))
        return self.sem, self.count

    def go(self, fn):
        self.ops.append(fn)

    def replay(self, e):
        for op in self.ops:
            op(e)


def chunk_plan():
    plan = [("ada_p", 3, 2048), ("w_in", 0, 2048), ("w_in", 1, 2048)]
    side = 0
    for i in range(20):
        if i >= 2:
            plan.append(("w_in", i, 2048))
        for _ in range(SIDE.get(i, 0)):
            plan.append(("ada_hi", side, 2048))
            side += 1
    for name, n in (("w_a", 2), ("w_b", 2), ("w_out", 4)):
        plan += [(name, i, 2048) for i in range(n)]
    for i in range(22):
        plan.append(("ffn_up", i, 2048))
        if i >= 5 and i % 2:
            plan.append(("ffn_down", (i - 5) // 2, 2048))
    plan += [("ffn_down", 9, 2048), ("ffn_down", 10, 2048)]
    for name, n in (("w_in_2", 10), ("w_out_2", 4)):
        plan += [(name, i, 2048) for i in range(n)]
    for i in range(16):
        plan.append(("w_mlp1", i, 2048))
        if i >= 2:
            plan.append(("w_mlp2", i - 2, 2048))
    return plan + [("w_mlp2", 14, 2048), ("w_mlp2", 15, 2048)]


def build(nc, io):
    sems = []

    def sem(name):
        s = nc.alloc_semaphore(name)
        sems.append(s)
        return s

    PE, SC, VE, PO, SY = (Queue(sem(n)) for n in ("pe_done", "act_done", "dve_done", "pool_done", "sp_done"))

    start = 16512
    cursor = [start]

    def place(name, shape, dt, offset):
        return nc.alloc_sbuf_tensor_at(name, shape, dt, offset=offset)

    def keep(name, shape, dt=F32):
        size = int(np.prod(shape[1:])) * (1 if dt == U8 else 4)
        t = place(name, shape, dt, cursor[0])
        cursor[0] += (size + 31) // 32 * 32
        return t

    raw = [keep(f"raw{i}", [P, CH]) for i in range(NRAW)]
    whi = [keep(f"whi{i}", [P, CH], F32R) for i in range(NHI)]
    wlo = [keep(f"wlo{i}", [P, CH], F32R) for i in range(NHI)]
    XR = keep("XR", [P, KT, T])
    con = keep("con", [P, NC])
    masks = keep("masks", [P, len(LEVELS), P], U8)
    vec = keep("vec", [P, NV])
    CB = keep("CB", [P, D])
    RC = keep("RC", [P, 64])
    ones = keep("ones", [P, T])
    eps = keep("eps", [P, 1])
    C2 = keep("C2", [P, KT, 2])
    MOD = keep("MOD", [P, 16, 2])
    warmed = keep("warmed", [P, 1])
    A1 = keep("A1", [P, KT, 2])
    MODX = keep("MODX", [P, 32])
    A2 = keep("A2", [P, KT])
    LBE = keep("LBE", [P, 8])
    LBM = keep("LBM", [P, 4])
    LB = keep("LB", [P, 4])
    LB1 = keep("LB1", [P, 4])
    MX = keep("MX", [P, 16])
    SM = keep("SM", [P, 16])
    RR = keep("RR", [P, T])
    RR1 = keep("RR1", [P, T])
    GG = keep("GG", [P, KT])
    G2 = keep("G2", [P, KT, 2])
    base = cursor[0]

    def area(name, shape, kb, dt=F32):
        return place(name, shape, dt, base + int(kb * 1024))

    def v(name, i=0, n=None):
        a, w = VEC[name]
        return vec[:, a + i:a + i + (w if n is None else n)]

    def c(name):
        a, w = CON[name]
        return con[:, a:a + w]

    ident = c("ident")
    bank = [nc.alloc_psum_tensor(f"bank{i}", [P, 512], F32) for i in range(8)]
    freed = {i: [] for i in range(8)}
    ring = {"g": [0, 1, 2], "m": [3, 4, 5, 6, 7]}
    turn = {"g": 0, "m": 0}

    def claim(b):
        PE.wait(*freed[b])
        freed[b] = []
        return b

    def take(kind):
        turn[kind] += 1
        return claim(ring[kind][turn[kind] % len(ring[kind])])

    def load(eng, name, dst, src):
        s = sem(f"in_{name}")
        eng.go(lambda e: e.dma_start(dst, src).then_inc(s, 16))
        return s, 16

    CX = area("CX", [P, KT, T], 32)
    MASKF = area("MASKF", [P, len(LEVELS), P], 40)
    CBX = area("CBX", [P, D], 44)
    def at(t):
        return (start + [*raw, *whi, *wlo].index(t) * CH * 4 - base) / 1024

    ada_buf = {}
    for name, i, kb in (("ada_s", 0, at(whi[1])), ("ada_p", 0, at(wlo[1])), ("ada_s", 1, 64), ("ada_p", 1, 88),
                        ("ada_s", 2, 56), ("ada_p", 2, at(whi[2])), ("ada_s", 3, at(wlo[2]))):
        ada_buf[name, i] = area(f"{name}{i}", [P, CH], kb)
    CROW = area("CROW", [1, 2 * D], at(wlo[0]))
    MR = area("MR", [2, 4, 2 * P], 96)
    ada_in = {}

    def load_ada(i, names=("ada_s", "ada_p")):
        for name in names:
            ada_in[name, i] = load(SY, f"{name}{i}", ada_buf[name, i][:, :], io[name][i])

    vec_in = load(SY, "vec", vec[:, :], io["vec"])
    c_in = load(SC, "c", CROW[:, 0:D], io["c_row"])
    load_ada(0)
    c_ctx_in = load(SC, "c_ctx", CROW[:, D:2 * D], io["c_ctx_row"])
    ident_in = load(SC, "ident", ident, io["con"][:, 0:P])
    x_in = load(SY, "x", XR[:, :, :], io["xT"])
    load_ada(1)

    plan = chunk_plan()
    s_raw = [sem(f"raw{i}") for i in range(NRAW)]
    n_raw = [0] * NRAW
    arrived, raw_free = {}, {}
    split = {}
    hi_free, lo_free = {}, {}
    order = {}
    for n, (name, i, cols) in enumerate(plan):
        order[(name, i)] = n
    slot_of = {}
    nsplit = [0]
    issued = [0]
    prepped = [0]

    def issue_loads(upto):
        while issued[0] < min(upto, len(plan)):
            n = issued[0]
            name, i, cols = plan[n]
            s = n % NRAW
            if n >= NRAW:
                if n - NRAW not in raw_free:
                    break
                SY.wait(*raw_free[n - NRAW])
            SY.go(lambda e, s=s, name=name, i=i, cols=cols:
                  e.dma_start(raw[s][:, 0:cols], io[name][i]).then_inc(s_raw[s], 16))
            n_raw[s] += 16
            arrived[n] = (s_raw[s], n_raw[s])
            issued[0] += 1

    def lo_engine(name, i):
        return PO if name == "w_mlp1" and i < 4 or name in ("w_in", "w_a", "w_b", "w_out", "ffn_up", "ffn_down", "w_in_2", "w_out_2") else VE

    def prep(n):
        name, i, cols = plan[n]
        r = raw[n % NRAW]
        if name == "ada_hi":
            VE.wait(arrived[n], c_rows[0])
            for j in range(2):
                f = 2 * i + j
                m = VE.do(lambda e, j=j, f=f: e.tensor_tensor_reduce(
                    out=r[:, j * D:(j + 1) * D], in0=r[:, j * D:(j + 1) * D], in1=CB[:, :], scale=1.0, scalar=0.0,
                    op0=ALU.mult, op1=ALU.add, accum_out=MODX[:, f:f + 1]))
            side_done[i] = m
            raw_free[n] = [m]
            issue_loads(n + NRAW + 1)
            return
        s = nsplit[0] % NHI
        nsplit[0] += 1
        slot_of[n] = s
        h, l = whi[s], wlo[s]
        prev = hi_free.get(s, [])
        SC.wait(arrived[n], *prev)
        a = SC.do(lambda e: e.activation(h[:, 0:cols], r[:, 0:cols], ACT.Copy))
        L = lo_engine(name, i)
        prev = prev + lo_free.pop(s, [])
        L.wait(arrived[n], a, *prev)
        half = cols // 2 if (name, i) in (("w_in", 0), ("w_in", 1), ("w_in", 2), ("w_in", 3), ("w_in_2", 0)) else 0
        b = [L.do(lambda e: e.tensor_tensor(l[:, half:cols], r[:, half:cols], h[:, half:cols].bitcast(F32),
                                            ALU.subtract))]
        if half:
            VE.wait(a, *prev)
            b.append(VE.do(lambda e: e.tensor_tensor(l[:, 0:half], r[:, 0:half], h[:, 0:half].bitcast(F32),
                                                     ALU.subtract)))
        split[n] = [a, *b]
        raw_free[n] = split[n]
        issue_loads(n + NRAW + 1)

    def prep_upto(n):
        while prepped[0] <= min(n, len(plan) - 1):
            prep(prepped[0])
            prepped[0] += 1

    side_done = {}

    def prep_ahead(n):
        look, more = n, NHI - 1
        while more and look + 1 < len(plan):
            look += 1
            more -= plan[look][0] != "ada_hi"
        prep_upto(look)

    def chunk(name, i):
        n = order[(name, i)]
        prep_ahead(n)
        PE.wait(*split[n])
        s = slot_of[n]
        return s, whi[s], wlo[s]

    def chunk_done(s, mark):
        hi_free[s] = [mark]

    def mm3(out, h, l, col, xh, xl, first, last):
        PE.go(lambda e: e.matmul(out, h[:, col:col + P], xh, start=first, stop=False, skip_group_check=True))
        PE.go(lambda e: e.matmul(out, h[:, col:col + P], xl, start=False, stop=False, skip_group_check=True))
        op = lambda e: e.matmul(out, l[:, col:col + P], xh, start=False, stop=last, skip_group_check=True)
        return PE.do(op) if last else PE.go(op)

    m_ones = PO.do(lambda e: e.memset(ones[:, :], 1.0))
    m_eps = PO.do(lambda e: e.memset(eps[:, :], EPS))

    load_ada(2)
    issue_loads(2)
    load_ada(3, ["ada_s"])
    issue_loads(3)
    ctx_in = load(SY, "ctx", CX[:, :, :], io["ctxT"])
    issue_loads(NRAW)

    HN = area("HN", [P, 2, KT, T], 72)
    H1h = area("H1h", [P, 2, KT, T], 0, F32R)
    H1l = area("H1l", [P, 2, KT, T], 16, F32R)
    SPARE = [area(f"SPARE{i}", [P, D], 48 + 4 * i) for i in range(2)]
    c_rows = []
    SC.wait(vec_in)
    c2 = SC.do(lambda e: e.activation(C2[:, :, :], v("c2").rearrange("p (k j) -> p k j", j=2), ACT.Silu))
    def column(b, i, sq, first, last):
        op = lambda e: e.matmul(bank[b][:, i:i + 1], sq, ones[:, 0:1], start=first, stop=last, skip_group_check=True)
        return PE.do(op) if last else PE.go(op)

    def rstd_columns(b, n, width, at, after):
        SC.wait(after)
        m = SC.do(lambda e: e.activation(RC[:, at:at + n], bank[b][:, 0:n], ACT.Sqrt, bias=eps[:, 0:1],
                                         scale=1.0 / width))
        freed[b].append(m)
        VE.wait(m)
        return VE.do(lambda e: e.reciprocal(RC[:, at:at + n], RC[:, at:at + n]))

    def rows(b, cols, ready):
        PE.wait(ready, ident_in)
        for i, col in enumerate(cols):
            op = lambda e, i=i, col=col: e.matmul(bank[b][:, i * P:(i + 1) * P], col, ident, start=True, stop=True)
            m = PE.do(op) if i == len(cols) - 1 else PE.go(op)
        return m

    def wide(i):
        return RC[:, i:i + 1].to_broadcast([P, P])

    lbr = v("hg_lb").rearrange("p (r h) -> p r h", r=2)
    LBE2 = LBE[:, :].rearrange("p (r h) -> p r h", r=2)
    VE.wait(vec_in)
    lb_max = VE.do(lambda e: e.tensor_tensor(LBM[:, :], lbr[:, 0, :], lbr[:, 1, :], ALU.max))
    VE.wait(lb_max)
    a = VE.do(lambda e: e.tensor_tensor(LBE2, lbr, LBM[:, :].unsqueeze(1).to_broadcast([P, 2, 4]), ALU.subtract))
    SC.wait(a)
    lb_exp = SC.do(lambda e: e.activation(LBE[:, :], LBE[:, :], ACT.Exp))
    VE.wait(lb_exp)
    a = VE.do(lambda e: e.tensor_tensor(LBM[:, :], LBE2[:, 0, :], LBE2[:, 1, :], ALU.add))
    VE.wait(a)
    a = VE.do(lambda e: e.reciprocal(LBM[:, :], LBM[:, :]))
    VE.wait(a)
    a = VE.do(lambda e: e.tensor_tensor(LB[:, :], LBE2[:, 0, :], LBM[:, :], ALU.mult))
    VE.wait(a)
    lb_ready = VE.do(lambda e: e.tensor_scalar(LB1[:, :], LB[:, :], -1.0, 1.0, ALU.mult, ALU.add))

    PE.wait(m_ones)
    for j, (arrival, row) in enumerate(((c_in, CB), (c_ctx_in, CBX))):
        PE.wait(arrival)
        for half in range(2):
            b = take("m")
            cols = slice(half * 512, half * 512 + 512)
            m = c_read = PE.do(lambda e, b=b, j=j, half=half: e.matmul(
                bank[b][:, :], ones[0:1, 0:P], CROW[:, j * D + half * 512:j * D + half * 512 + 512], start=True, stop=True))
            SC.wait(m)
            m = SC.do(lambda e, b=b, cols=cols, row=row: e.activation(row[:, cols], bank[b][:, :], ACT.Silu))
            freed[b].append(m)
        c_rows.append(m)

    def warm(func):
        SC.do(lambda e: e.activation(warmed[:, 0:1], eps[:, 0:1], func))

    def input_columns(x):
        PE.wait(sums[x], m_ones)
        b = take("m")
        for t in range(2):
            m = PE.do(lambda e, t=t: e.matmul(bank[b][:, t:t + 1], HN[:, x, 0, t * P:(t + 1) * P], ones[:, 0:1],
                                              start=t == 0, stop=True, skip_group_check=True))
        return rstd_columns(b, 2, D, 2 * x, m)

    spare_free = [[], []]

    def ada_rows(i, j):
        VE.wait(ada_in["ada_s", i], c_rows[j])
        r = ada_buf["ada_s", i]
        for f in range(2):
            out = r[:, f * D:(f + 1) * D] if j else SPARE[f][:, :]
            VE.wait(*spare_free[f])
            m = VE.do(lambda e, f=f, out=out: e.tensor_tensor_reduce(
                out=out, in0=r[:, f * D:(f + 1) * D], in1=(CBX if j else CB)[:, :], scale=1.0, scalar=0.0,
                op0=ALU.mult, op1=ALU.add, accum_out=MOD[:, 8 + 2 * i + f, j:j + 1]))
            if not j:
                spare_free[f] = [m]
        return m

    def ada_columns(i):
        n = order.get(("ada_p", i))
        PE.wait(ada_in["ada_p", i] if n is None else arrived[n], c2)
        r = (ada_buf["ada_p", i] if n is None else raw[n % NRAW])[:, :].rearrange("p (f k c) -> p f k c", f=2, k=KT)
        b = take("m")
        out = bank[b][0:2, 0:2 * P].rearrange("p (f c) -> p f c", f=2)
        for k in range(KT):
            op = lambda e, k=k: e.matmul(out, C2[:, k, :], r[:, :, k, :], start=k == 0, stop=k == KT - 1)
            m = PE.do(op) if k == KT - 1 else PE.go(op)
        ada_read[i] = m
        if n is not None:
            raw_free[n] = [m]
        shift_bank[i] = b, m

    def shift_copy(i):
        b, m = shift_bank[i]
        SC.wait(m)
        shift_rows[i] = SC.do(lambda e: e.activation(MR[:, i, :], bank[b][0:2, 0:2 * P], ACT.Copy))
        freed[b].append(shift_rows[i])

    def scales(t, j, ready):
        n = t.stop - t.start
        at = slice(8 + t.start, 8 + t.stop)
        wide2 = lambda ap: ap.unsqueeze(2)
        VE.wait(ready)
        a = VE.do(lambda e: e.tensor_tensor(MOD[:, at, j], MOD[:, at, j], wide2(v("ada_b", at.start, n)), ALU.add))
        VE.wait(a)
        a = VE.do(lambda e: e.scalar_tensor_tensor(A1[:, t, j], MOD[:, at, j], 1.0, wide2(v("norm1_g", t.start, n)),
                                                   ALU.add, ALU.mult))
        VE.wait(a)

    def modulation(i):
        b = take("m")
        PE.wait(shift_rows[i], ident_in)
        for f in range(2):
            m = PE.do(lambda e, f=f: e.matmul(bank[b][:, 2 * f:2 * f + 2], MR[:, i, f * P:(f + 1) * P], ident[0:2, 0:2],
                                              start=True, stop=True))
        two = slice(2 * i, 2 * i + 2)
        scales(two, slice(0, 1), scale_done[i])
        VE.wait(m)
        m = VE.do(lambda e: e.tensor_tensor(MOD[:, two, :], bank[b][:, 0:4].rearrange("p (f j) -> p f j", j=2),
                                            v("ada_b", 2 * i, 2).unsqueeze(2).to_broadcast([P, 2, 2]), ALU.add))
        freed[b].append(m)
        VE.wait(m)

    def input_sums(x, src, src_in, E):
        SC.wait(src_in)
        m = SC.do(lambda e: e.activation(HN[:, x, :, :], src[:, :, :], ACT.Square))
        for n in (4, 2, 1):
            E.wait(m)
            m = E.do(lambda e, n=n: e.tensor_tensor(HN[:, x, 0:n, :], HN[:, x, 0:n, :], HN[:, x, n:2 * n, :], ALU.add))
        return m

    his, h1 = [[], []], [[], []]

    def input_tiles(x, src, row, ks):
        VE.wait(rs[x])
        for k in [*ks, None]:
            if k is not None:
                m = VE.do(lambda e, k=k: e.scalar_tensor_tensor(
                    HN[:, x, k, :], src[:, k, :], A1[:, k, x:x + 1], bank[row][:, 0:T], ALU.mult, ALU.mult))
                SC.wait(m)
                his[x].append(SC.do(lambda e, k=k: e.activation(H1h[:, x, k, :], HN[:, x, k, :], ACT.Identity,
                                                                bias=MOD[:, k, x:x + 1])))
            if k != ks[0]:
                q = len(h1[x])
                VE.wait(his[x][q])
                h1[x].append(VE.do(lambda e, k=q: e.scalar_tensor_tensor(
                    H1l[:, x, k, :], HN[:, x, k, :], MOD[:, k, x:x + 1], H1h[:, x, k, :].bitcast(F32),
                    ALU.add, ALU.subtract)))
        freed[row].append(m)

    opened = {}

    def first(i, ks):
        n = order["w_in", i]
        if i not in opened:
            opened[i] = take("g")
        b, s = opened[i], slot_of[n]
        h, l = whi[s], wlo[s]
        PE.wait(*split[n])
        for k in ks:
            PE.wait(his[0][k], h1[0][k])
            for j in range(2):
                m = mm3(bank[b][:, j * T:(j + 1) * T], h, l, (j * KT + k) * P, H1h[:, 0, k, :], H1l[:, 0, k, :],
                        k + j == 0, k == KT - 1)
        if ks[-1] == KT - 1:
            chunk_done(s, m)
        return b, m

    shift_rows, shift_bank, scale_done, ada_read = {}, {}, {}, {}
    prepped[0] = 4
    scale_done[0] = ada_rows(0, 0)
    row_read = ada_rows(0, 1)
    ada_columns(0)
    hi_free[1] = [row_read, ada_read[0]]
    sums = [input_sums(0, XR, x_in, VE)]
    SC.wait(m_eps)
    warm(ACT.Sqrt)
    shift_copy(0)
    rcs = [input_columns(0)]
    br = [claim(ring["g"][(turn["g"] + 3) % 3])]
    rs = [rows(br[0], [wide(0), wide(1)], rcs[0])]
    scale_done[1] = ada_rows(1, 0)
    ada_rows(1, 1)
    ada_columns(1)
    shift_copy(1)
    modulation(0)
    input_tiles(0, XR, br[0], [0, 1])
    modulation(1)
    input_tiles(0, XR, br[0], [2, 3])
    scale_done[2] = ada_rows(2, 0)
    ada_rows(2, 1)
    hi_free[0] = [c_read]
    prep(1)
    ada_columns(2)
    shift_copy(2)
    ada_columns(3)
    modulation(2)
    input_tiles(0, XR, br[0], [4, 5])
    shift_copy(3)
    first(0, range(0, 6))
    scale_done[3] = ada_rows(3, 0)
    prep(2)
    sums.append(input_sums(1, CX, ctx_in, PO))
    modulation(3)
    input_tiles(0, XR, br[0], [6, 7])
    row_read = ada_rows(3, 1)
    hi_free[2], lo_free[2] = [ada_read[2]], [row_read]
    prep(3)
    first(1, range(0, 6))
    opened_all = first(0, range(6, 8))
    scales(slice(0, KT), slice(1, 2), row_read)
    rcs.append(input_columns(1))
    masks_in = load(SY, "masks", MASKF[:, :, :], io["masks"])
    con_in = load(SY, "con", con[:, P:NC], io["con"][:, P:NC])
    F = area("F", [P, 2, 2, NH, T], 32)
    K = area("K", [P, 2, 2, NH, T], 48)
    f_ready = {0: [], 1: []}
    Q = area("Q", [P, NH, T], 96)
    XS = area("XS", [P, 2, NH, T], 72)
    FU = area("FU", [P, NH, T], 76)
    SG = area("SG", [P, NH, T], 88)
    GA = area("GA", [P, 2 * NH, T], 8)
    GB = area("GB", [P, 2 * NH, T], 24)
    QFP = area("QF", [P, 2 * (NH * T + LEVELS[-1])], 40)
    QF = QFP[:, 0:2 * NH * T].rearrange("p (d a t) -> p d a t", d=2, a=NH)
    A = area("A", [P, 2, NH, T], 56)
    VX = area("VX", [P, 2, NH, P], 68)
    KS = area("KS", [P, NH, T], 72)
    KTT = area("KTT", [P, 2, 2, NH, P], 80)
    VC = area("VC", [P, 2, NH, P], 88)
    ST = area("ST", [P, 2, NH, P], 92)
    T1 = area("T1", [P, 2, NH, T], 80)
    YFh = area("YFh", [P, NH, T], 72, F32R)
    YFl = area("YFl", [P, NH, T], 76, F32R)
    YF = area("YF", [P, NH, T], 64)
    SQo = area("SQo", [P, NH, T], 80)
    RSo = area("RSo", [P, NH, T], 84)
    ON = area("ON", [P, NH, T], 64)
    YHh = area("YHh", [P, NH, T], 48, F32R)
    YHl = area("YHl", [P, NH, T], 52, F32R)
    MGh = area("MGh", [P, KT, T], 0, F32R)
    MGl = area("MGl", [P, KT, T], 16, F32R)
    kk, kc = {}, []

    def both_inputs(i):
        s, h, l = chunk("w_in", i)
        for j in range(2):
            b = take("g")
            for k in range(KT):
                PE.wait(his[1][k], h1[1][k])
                m = mm3(bank[b][:, :].rearrange("p (x t) -> p x t", x=2), h, l, (j * KT + k) * P,
                        H1h[:, :, k, :], H1l[:, :, k, :], k == 0, k == KT - 1)
            if j == 1:
                chunk_done(s, m)
            f = 2 * (i - 2) + j
            d, head = f // 4, f % 4
            src = bank[b][:, :].rearrange("p (x t) -> p x t", x=2)
            SC.wait(m, h1[1][-1], m_masks)
            a = SC.do(lambda e, src=src, d=d, head=head: e.activation(F[:, :, d, head, :], src, ACT.Sigmoid))
            VE.wait(a, lb_ready)
            f_ready[d].append(VE.do(lambda e, d=d, head=head: e.tensor_scalar(
                F[:, :, d, head, :], F[:, :, d, head, :], LB1[:, head:head + 1], LB[:, head:head + 1],
                ALU.mult, ALU.add)))
            freed[b].append(a)
        return m

    def by_tokens(b, s, xh, xl, ready=None):
        wide = lambda w, k: w[:, 0:2 * KT * P].rearrange("p (f k c) -> p f k c", f=2, k=KT)[:, :, k, :]
        for k in range(KT):
            if ready is not None:
                PE.wait(*ready[k])
            h, l = wide(whi[s], k), wide(wlo[s], k)
            for t in range(2):
                out = bank[b][:, t * T:(t + 1) * T].rearrange("p (f c) -> p f c", f=2)
                th, tl = xh[:, k, t * P:(t + 1) * P], xl[:, k, t * P:(t + 1) * P]
                for n, (x, w) in enumerate(((th, h), (tl, h), (th, l))):
                    op = lambda e, out=out, x=x, w=w, n=n, k=k, t=t: e.matmul(
                        out, x, w, start=k + t + n == 0, stop=(k, n) == (KT - 1, 2), skip_group_check=True)
                    m = PE.do(op) if (k, t, n) == (KT - 1, 1, 2) else PE.go(op)
        return m

    def values(i):
        s, _, _ = chunk("w_in", i)
        two = slice(2 * (i - 6), 2 * (i - 6) + 2)
        for x, name, dst in ((1, "vc", VC), (0, "vx", VX)):
            b = take("g")
            m = by_tokens(b, s, H1h[:, x, :, :], H1l[:, x, :, :])
            SC.wait(m, *h1_all)
            a = SC.do(lambda e, b=b, dst=dst: e.activation(
                dst[:, :, two, :], bank[b][:, :].rearrange("p (t f c) -> p t f c", t=2, f=2), ACT.Copy))
            freed[b].append(a)
            marks.setdefault(name, []).append(a)
        chunk_done(s, m)
        return m

    def ctx_decay():
        PO.wait(*h1_all)
        m_xs = [PO.do(lambda e: e.memset(XS[:, 0, :, T - 1:T], 1.0)),
                PO.do(lambda e: e.memset(XS[:, 1, :, 0:1], 1.0))]
        for x in (1, 0):
            for d in range(2):
                VE.wait(f_ready[d][-1])
                kk[x, d] = VE.do(lambda e, x=x, d=d: e.tensor_scalar(K[:, x, d, :, :], F[:, x, d, :, :], -1.0, 1.0,
                                                                     ALU.mult, ALU.add))
        VE.wait(*m_xs, m_ones)
        for d in range(2):
            for head in range(NH):
                if d == 0:
                    o, i0 = XS[:, 0, head, T - 2::-1], F[:, 1, 0, head, T - 1:0:-1]
                else:
                    o, i0 = XS[:, 1, head, 1:T], F[:, 1, 1, head, 0:T - 1]
                m = VE.do(lambda e, o=o, i0=i0: e.tensor_tensor_scan(o, i0, ones[:, 0:T - 1], 1.0, ALU.mult,
                                                                     ALU.mult))
            VE.wait(m, kk[1, d])
            kc.append(VE.do(lambda e, d=d: e.tensor_tensor(K[:, 1, d, :, :], K[:, 1, d, :, :], XS[:, d, :, :],
                                                           ALU.mult)))

    def evict(b, m, out, func=ACT.Copy, after=(), src=None):
        SC.wait(m, *after)
        a = SC.do(lambda e: e.activation(out, bank[b][:, :] if src is None else src, func))
        freed[b].append(a)
        return a

    def flat(ap):
        return ap.rearrange("p a b -> p (a b)")

    hx, hl = H1h[:, 0, :, :], H1l[:, 0, :, :]
    marks = {}

    def transposes(srcs, outs, after, before):
        PE.wait(*after)
        done = []
        for four, out in zip(srcs, outs):
            b = take("m")
            for n, src in enumerate(four):
                op = lambda e, b=b, n=n, src=src: e.transpose(bank[b][:, n * P:(n + 1) * P], src, ident)
                m = PE.do(op) if n == len(four) - 1 else PE.go(op)
            done.append(evict(b, m, out, after=before))
        return done

    def ctx_turn():
        srcs, outs = [], []
        for d in range(2):
            for t in range(2):
                srcs.append([K[:, 1, d, h, t * P:(t + 1) * P] for h in range(NH)])
                outs.append(flat(KTT[:, d, t, :, :]))
        marks["turned"] = transposes(srcs, outs, kc, h1_all)

    def ctx_state():
        PE.wait(*marks["turned"], *marks["vc"])
        st = []
        for d in range(2):
            b = take("m")
            for h in range(NH):
                for t in range(2):
                    op = lambda e, b=b, d=d, h=h, t=t: e.matmul(
                        bank[b][:, h * P:(h + 1) * P], KTT[:, d, t, h, :], VC[:, t, h, :], start=t == 0, stop=t == 1)
                    m = PE.do(op) if (h, t) == (NH - 1, 1) else PE.go(op)
            st.append(evict(b, m, flat(ST[:, d, :, :])))
        marks["state"] = st
        marks["state_pe"] = m

    def x_start():
        VE.wait(*marks["q"], *kc)
        marks["qf"] = [VE.do(lambda e, d=d: e.tensor_tensor(QF[:, 1 - d, :, :], Q[:, :, :], F[:, 0, d, :, :], ALU.mult))
                       for d in range(2)]
        VE.wait(kk[0, 0], kk[0, 1])
        marks["ks"] = VE.do(lambda e: e.tensor_tensor(KS[:, :, :], K[:, 0, 0, :, :], K[:, 0, 1, :, :], ALU.add))

    def diagonal():
        PE.wait(marks["ks"], *marks["q"])
        marks["a"] = []
        for t in range(2):
            b = take("m")
            cols = slice(t * P, (t + 1) * P)
            for h in range(NH):
                op = lambda e, b=b, h=h, cols=cols: e.matmul(bank[b][:, h * P:(h + 1) * P], KS[:, h, cols],
                                                            Q[:, h, cols], start=True, stop=True)
                m = PE.do(op) if h == NH - 1 else PE.go(op)
            SC.wait(m, *marks["turned"])
            a = SC.do(lambda e, b=b, t=t: e.activation(A[:, t, :, t * P:(t + 1) * P],
                                                       bank[b][:, :].rearrange("p (h t) -> p h t", h=NH), ACT.Copy))
            freed[b].append(a)
            marks["a"].append(a)
        marks["diag_pe"] = m

    def halves(ap, h):
        return ap.rearrange("p (b two h) -> p b two h", two=2, h=h)

    QB = {h: QFP[:, 0:2 * (NH * T + h)].rearrange("p (two x) -> p two x", two=2) for h in LEVELS}
    KM = area("KM", [P, NH, T], 96)

    def merge_keys(li):
        h = LEVELS[li]
        SC.wait(kk[0, 0], kk[0, 1], *marks.get("kf", []), marks["diag_pe"], *marks.get("level_pe", []))
        marks["km"] = [SC.do(lambda e, d=d: e.activation(
            halves(flat(KM[:, :, :]), h)[:, :, d, :], halves(flat(K[:, 0, d, :, :]), h)[:, :, d, :], ACT.Copy))
            for d in range(2)]

    def level(li):
        h = LEVELS[li]
        PE.wait(*marks["qf"], *marks["km"])
        got = []
        for t in range(2):
            b = take("m")
            for hd in range(NH):
                o = hd * T + t * P
                q = QB[h][:, :, o:o + P].rearrange("p two (b q h) -> p q b two h", q=2, h=h)[:, 0]
                op = lambda e, b=b, hd=hd, t=t, q=q: e.matmul(bank[b][:, hd * P:(hd + 1) * P],
                                                              KM[:, hd, t * P:(t + 1) * P], q, start=True, stop=True)
                m = PE.do(op) if hd == NH - 1 else PE.go(op)
            got.append((b, m))
        for t, (b, m) in enumerate(got):
            VE.wait(m, *marks["a"])
            a = VE.do(lambda e, b=b, t=t: e.copy_predicated(
                A[:, t, :, t * P:(t + 1) * P],
                masks[:, li, :].unsqueeze(1).to_broadcast([P, NH, P]),
                bank[b][:, :].rearrange("p (h t) -> p h t", h=NH)))
            freed[b].append(a)
            marks["ap"] = a
        marks["level_pe"] = [got[-1][1]]
        grow(h, got[-1][1])
        if li + 1 < len(LEVELS):
            merge_keys(li + 1)

    def blocks(d, h):
        f = F[:, 0, d, :, :].rearrange("p a t -> p (a t)")
        return f.rearrange("p (b two h) -> p b two h", two=2, h=h)[:, :, :, 0]

    def grow(h, read):
        nb = NH * T // (2 * h)
        VE.wait(read)
        q0, q1 = (halves(QF[:, 1 - d, :, :].rearrange("p a t -> p (a t)"), h) for d in range(2))
        k0, k1 = (halves(K[:, 0, d, :, :].rearrange("p a t -> p (a t)"), h) for d in range(2))
        f0, f1 = blocks(0, h), blocks(1, h)

        def times(x, f):
            return VE.do(lambda e: e.tensor_tensor(x, x, f.unsqueeze(2).to_broadcast([P, nb, h]), ALU.mult))

        VE.wait(*marks.get("bp", f_ready[0] + f_ready[1]))
        marks["qf"] = [times(q0[:, :, 1, :], f0[:, :, 0]), times(q1[:, :, 0, :], f1[:, :, 1])]
        if 2 * h < T:
            marks["kf"] = [times(k0[:, :, 0, :], f0[:, :, 1]), times(k1[:, :, 1, :], f1[:, :, 0])]
            VE.wait(*marks["kf"])
            marks["bp"] = [VE.do(lambda e, f=f: e.tensor_tensor(f[:, :, 0], f[:, :, 0], f[:, :, 1], ALU.mult))
                           for f in (f0, f1)]

    def level_wide():
        PE.wait(*marks["qf"], *marks["kf"])
        marks["aw"] = []
        for d in range(2):
            b = take("m")
            ks, ts = (slice(0, P), slice(P, T)) if d == 0 else (slice(P, T), slice(0, P))
            for h in range(NH):
                op = lambda e, b=b, d=d, h=h, ks=ks, ts=ts: e.matmul(
                    bank[b][:, h * P:(h + 1) * P], K[:, 0, d, h, ks], QF[:, 1 - d, h, ts], start=True, stop=True)
                m = PE.do(op) if h == NH - 1 else PE.go(op)
            SC.wait(m, *marks["turned"])
            a = SC.do(lambda e, b=b, d=d, ts=ts: e.activation(
                A[:, d, :, ts], bank[b][:, :].rearrange("p (h t) -> p h t", h=NH), ACT.Copy))
            freed[b].append(a)
            marks["aw"].append(a)
        marks["wide_pe"] = m
        grow(P, m)

    def outputs():
        PE.wait(marks["ap"], *marks["aw"], *marks["a"], *marks["qf"], *marks["state"], *marks["vx"])
        marks["o"] = []
        for hp in range(2):
            b = take("m")
            for j in range(2):
                h = 2 * hp + j
                o = bank[b][:, j * T:(j + 1) * T]
                for t in range(2):
                    PE.go(lambda e, o=o, h=h, t=t: e.matmul(o, VX[:, t, h, :], A[:, t, h, :], start=t == 0,
                                                            stop=False))
                PE.go(lambda e, o=o, h=h: e.matmul(o, ST[:, 0, h, :], QF[:, 1, h, :], start=False, stop=False))
                op = lambda e, o=o, h=h: e.matmul(o, ST[:, 1, h, :], QF[:, 0, h, :], start=False, stop=True)
                m = PE.do(op) if j == 1 else PE.go(op)
            marks["o"].append((b, m))

    def readout_squares():
        for hp, (b, m) in enumerate(marks["o"]):
            a = evict(b, m, flat(ON[:, 2 * hp:2 * hp + 2, :]), after=marks["vx"] + marks["yf", 0] + marks["yf", 1])
            SC.wait(a, *marks["t1_free"])
            a = SC.do(lambda e, hp=hp: e.activation(SQo[:, 2 * hp:2 * hp + 2, :], ON[:, 2 * hp:2 * hp + 2, :],
                                                    ACT.Square))
            marks["sqo", hp] = a

    def readout_columns():
        b = take("m")
        for h in range(NH):
            PE.wait(marks["sqo", h // 2])
            for t in range(2):
                m = column(b, 2 * h + t, SQo[:, h, t * P:(t + 1) * P], h + t == 0, h + t == NH)
        marks["rco"] = rstd_columns(b, 8, P, 8, m)

    def readout_norm():
        for hp in range(2):
            b = take("m")
            r = rows(b, [wide(8 + 4 * hp + i) for i in range(4)], marks["rco"])
            VE.wait(r, marks["sg"])
            for j in range(2):
                h = 2 * hp + j
                g = VE.do(lambda e, h=h, b=b, j=j: e.scalar_tensor_tensor(
                    RSo[:, h, :], bank[b][:, j * T:(j + 1) * T], v("onorm", h, 1), SG[:, h, :], ALU.mult, ALU.mult))
            freed[b].append(g)
            VE.wait(g)
            y = VE.do(lambda e, hp=hp: e.tensor_tensor(ON[:, 2 * hp:2 * hp + 2, :], ON[:, 2 * hp:2 * hp + 2, :],
                                                       RSo[:, 2 * hp:2 * hp + 2, :], ALU.mult))
            SC.wait(y, marks["wide_pe"])
            yh = SC.do(lambda e, hp=hp: e.activation(YHh[:, 2 * hp:2 * hp + 2, :], ON[:, 2 * hp:2 * hp + 2, :],
                                                     ACT.Copy))
            VE.wait(yh)
            yl = VE.do(lambda e, hp=hp: e.tensor_tensor(YHl[:, 2 * hp:2 * hp + 2, :], ON[:, 2 * hp:2 * hp + 2, :],
                                                        YHh[:, 2 * hp:2 * hp + 2, :].bitcast(F32), ALU.subtract))
            marks["yh", hp] = [yh, yl]

    dft_l = c("dft_l").rearrange("p (t s n) -> p t s n", t=2, s=2)

    def fourier_1():
        PE.wait(*marks["fu"])
        marks["t1"] = []
        H = P // 2
        for t in range(2):
            b = take("m")
            for g in range(NH):
                op = lambda e, b=b, t=t, g=g: e.matmul(
                    bank[b][:, g * P:(g + 1) * P], FU[:, g, t * P:(t + 1) * P], c("dft_c"), start=True, stop=True)
                m = PE.do(op) if g == NH - 1 else PE.go(op)
            src = bank[b][:, :].rearrange("p (g n) -> p g n", g=NH)
            dst = T1[:, t, :, :]
            marks["t1"] += [evict(b, m, dst[:, :, 0:H + 1], after=[marks["state_pe"]], src=src[:, :, 0:H + 1]),
                            evict(b, m, dst[:, :, P + 1:P + H], src=src[:, :, H + 1:P])]
        marks["fu_free"] = m

    def fourier_mirror():
        H = P // 2
        VE.wait(*marks["t1"])
        for t in range(2):
            dst = T1[:, t, :, :]
            marks["t1"] += [
                VE.do(lambda e, dst=dst: e.tensor_copy(dst[:, :, H + 1:P], dst[:, :, H - 1:0:-1])),
                VE.do(lambda e, dst=dst: e.tensor_scalar(dst[:, :, P + H + 1:2 * P], dst[:, :, P + H - 1:P:-1],
                                                         -1.0, None, ALU.mult)),
                VE.do(lambda e, dst=dst: e.memset(dst[:, :, P:2 * P:H], 0.0))]

    def fourier_2():
        PE.wait(*marks["t1"])
        H = T // 2
        for gp in range(2):
            b = take("m")
            for j in range(2):
                g = 2 * gp + j
                for s, o, n0, n1 in ((0, j * T, 0, H + 1), (1, j * T + H + 1, 1, H)):
                    for t in range(2):
                        op = lambda e, b=b, g=g, j=j, t=t, s=s, o=o, n0=n0, n1=n1: e.matmul(
                            bank[b][:, o:o + n1 - n0], T1[:, t, g, s * P:(s + 1) * P], dft_l[:, t, s, n0:n1],
                            start=(j, s, t) == (0, 0, 0), stop=t == 1, skip_group_check=True)
                        m = PE.do(op) if (j, s, t) == (1, 1, 1) else PE.go(op)
            y = YF[:, 2 * gp:2 * gp + 2, :]
            src = bank[b][:, :].rearrange("p (a t) -> p a t", a=2)
            cos, sin = src[:, :, 1:H], src[:, :, H + 1:T]
            a = evict(b, m, y[:, :, 0:H + 1], after=marks["vx"], src=src[:, :, 0:H + 1])
            VE.wait(a)
            d = [VE.do(lambda e, y=y, sin=sin: e.tensor_tensor(y[:, :, T - 1:H:-1], y[:, :, 1:H], sin, ALU.subtract)),
                 VE.do(lambda e, y=y, sin=sin: e.tensor_tensor(y[:, :, 1:H], y[:, :, 1:H], sin, ALU.add))]
            freed[b] += d
            SC.wait(*d, marks["diag_pe"], marks["fu_free"])
            a = SC.do(lambda e, y=y, gp=gp: e.activation(YFh[:, 2 * gp:2 * gp + 2, :], y, ACT.Copy))
            VE.wait(a)
            marks["yf", gp] = [a, VE.do(lambda e, y=y, gp=gp: e.tensor_tensor(
                YFl[:, 2 * gp:2 * gp + 2, :], y, YFh[:, 2 * gp:2 * gp + 2, :].bitcast(F32), ALU.subtract))]
        marks["t1_free"] = [m]

    for i in range(20):
        if i < 2:
            if i == 0:
                b, m = opened_all
            else:
                first(1, [6])
                br.append(take("m"))
                rs.append(rows(br[1], [wide(2), wide(3)], rcs[1]))
                b, m = first(1, [7])
        elif i < 8:
            m = h1c_done = (both_inputs if i < 6 else values)(i)
        else:
            s, h, l = chunk("w_in", i)
            b = take("g")
            for k in range(KT):
                PE.wait(his[0][k], h1[0][k])
                for j in range(2):
                    m = mm3(bank[b][:, j * T:(j + 1) * T], h, l, (j * KT + k) * P, hx[:, k, :], hl[:, k, :],
                            k + j == 0, k == KT - 1)
            chunk_done(s, m)
        if i < 2:
            if i == 1:
                input_tiles(1, CX, br[1], range(4))
            marks.setdefault("q", []).append(evict(b, m, flat(Q[:, 2 * i:2 * i + 2, :]), ACT.Silu))
            if i == 1:
                input_tiles(1, CX, br[1], range(4, KT))
                h1_all = [his[1][-1], h1[1][-1]]
                prep_upto(order["w_in", 3])
                VE.wait(masks_in)
                m_masks = VE.do(lambda e: e.tensor_copy(masks[:, :, :], MASKF[:, :, :]))
        elif i < 8:
            if i == 5:
                ctx_decay()
                x_start()
        elif i < 10:
            marks.setdefault("fu", []).append(
                evict(b, m, flat(FU[:, 2 * (i - 8):2 * (i - 8) + 2, :]), after=kc))
        elif i < 12:
            marks["sg"] = evict(b, m, flat(SG[:, 2 * (i - 10):2 * (i - 10) + 2, :]), ACT.Silu,
                                after=[marks["state_pe"]])
        elif i < 16:
            marks["ga"] = evict(b, m, flat(GA[:, 2 * (i - 12):2 * (i - 12) + 2, :]), ACT.Sigmoid, after=[h1c_done])
        else:
            marks["gb"] = evict(b, m, flat(GB[:, 2 * (i - 16):2 * (i - 16) + 2, :]), ACT.Sigmoid, after=[h1c_done])
        if i == 6:
            ctx_turn()
            diagonal()
            merge_keys(0)
        elif i == 7:
            level(0)
        elif i == 8:
            level(1)
        elif i == 9:
            ctx_state()
            level(2)
        elif i == 10:
            fourier_1()
            level(3)
        elif i == 11:
            level(4)
            fourier_mirror()
        elif i == 12:
            level(5)
        elif i == 13:
            level(6)
        elif i == 14:
            fourier_2()
            level_wide()
        elif i == 15:
            outputs()
            readout_squares()
        elif i == 16:
            readout_columns()
        elif i == 17:
            readout_norm()
    hx_done = m

    def quad(name, i, xh, xl):
        s, h, l = chunk(name, i)
        out = []
        for jp in range(2):
            b = take("g")
            for k in range(NH):
                for j in range(2):
                    m = mm3(bank[b][:, j * T:(j + 1) * T], h, l, ((2 * jp + j) * NH + k) * P, xh[:, k, :], xl[:, k, :],
                            k + j == 0, k == NH - 1)
            out.append((b, m))
        chunk_done(s, m)
        return out

    def gated(b, m, g, ready, f):
        VE.wait(m, ready)
        a = VE.do(lambda e: e.tensor_tensor(flat(g[:, f:f + 2, :]), bank[b][:, :], flat(g[:, f:f + 2, :]), ALU.mult))
        freed[b].append(a)
        return a

    PE.wait(*marks["yf", 0], *marks["yf", 1])
    ya = {}
    for i in range(2):
        for jp, (b, m) in enumerate(quad("w_a", i, YFh, YFl)):
            f = 4 * i + 2 * jp
            ya[f] = gated(b, m, GA, marks["ga"], f)
    PE.wait(*marks["yh", 0], *marks["yh", 1])
    mg = {}
    for i in range(2):
        for jp, (b, m) in enumerate(quad("w_b", i, YHh, YHl)):
            f = 4 * i + 2 * jp
            yb = gated(b, m, GB, marks["gb"], f)
            VE.wait(yb, ya[f])
            s = VE.do(lambda e, f=f: e.tensor_tensor(GA[:, f:f + 2, :], GA[:, f:f + 2, :], GB[:, f:f + 2, :],
                                                     ALU.add))
            SC.wait(s, hx_done)
            a = SC.do(lambda e, f=f: e.activation(MGh[:, f:f + 2, :], GA[:, f:f + 2, :], ACT.Copy))
            VE.wait(a)
            y = VE.do(lambda e, f=f: e.tensor_tensor(MGl[:, f:f + 2, :], GA[:, f:f + 2, :],
                                                     MGh[:, f:f + 2, :].bitcast(F32), ALU.subtract))
            mg[f] = mg[f + 1] = [a, y]

    mod_ready = {}

    def mods(a, n):
        prep_upto(max(order[("ada_hi", i)] for i in range(a // 2, (a + n) // 2)))
        VE.wait(side_done[(a + n) // 2 - 1])
        mod_ready[a] = VE.do(lambda e: e.tensor_tensor(MODX[:, a:a + n], MODX[:, a:a + n], v("ada_b", 16 + a, n),
                                                       ALU.add))

    mods(0, 32)
    VE.wait(mod_ready[0])
    g2 = [VE.do(lambda e: e.tensor_copy(G2[:, :, 0], ones[:, 0:KT])),
          VE.do(lambda e: e.tensor_tensor(G2[:, :, 1], v("final_g"), v("final_g"), ALU.mult))]
    gg = VE.do(lambda e: e.tensor_tensor(GG[:, :], v("final_g"), v("norm1_g_2"), ALU.mult))
    a2 = VE.do(lambda e: e.scalar_tensor_tensor(A2[:, :], MODX[:, 16:24], 1.0, v("norm2_g"), ALU.add, ALU.mult))

    def add_to_x(b, ready, f, gate, js=(0, 1)):
        VE.wait(ready)
        for j in js:
            g = 1.0 if gate is None else MODX[:, gate + f + j:gate + f + j + 1]
            a = VE.do(lambda e, j=j, g=g: e.scalar_tensor_tensor(
                XR[:, f + j, :], bank[b][:, j * T:(j + 1) * T], g, XR[:, f + j, :], ALU.mult, ALU.add))
        freed[b].append(a)
        return a

    def squares(sq, f, after, n=2):
        SC.wait(after)
        return SC.do(lambda e: e.activation(sq[:, f:f + n, :], XR[:, f:f + n, :], ACT.Square))

    def scaled_high(gain, xh, f, after, n=2):
        SC.wait(after)
        return [SC.do(lambda e, k=k: e.activation(xh[:, k, :], XR[:, k, :], ACT.Identity, scale=gain[:, k:k + 1]))
                for k in range(f, f + n)]

    def scaled_low(gain, xh, xl, f, highs):
        out = {}
        for k, a in enumerate(highs, f):
            VE.wait(a)
            out[k] = [a, VE.do(lambda e, k=k: e.scalar_tensor_tensor(
                xl[:, k, :], XR[:, k, :], gain[:, k:k + 1], xh[:, k, :].bitcast(F32), ALU.mult, ALU.subtract))]
        return out

    def square_columns(b, sq, f, ready, n=2):
        PE.wait(ready)
        for k in range(f, f + n):
            for t in range(2):
                m = column(b, t, sq[:, k, t * P:(t + 1) * P], k + t == 0, k == KT - 1)
        return m

    def project(name, xh, xl, ready, ks, gate, sq, split=None):
        bs = take("m")
        warm(ACT.Sqrt)
        out, now = {}, None
        for i in range(3):
            b, m = pair_when(name, i, xh, xl, ready, ks)
            x = add_to_x(b, m, 2 * i, gate)
            before, now = now, squares(sq, 2 * i, x)
            if split:
                out.update(split(2 * i, x))
            if i:
                VE.wait(before, now)
                now = VE.do(lambda e, i=i: e.tensor_tensor(sq[:, 0:2, :], sq[:, 0:2, :], sq[:, 2 * i:2 * i + 2, :],
                                                           ALU.add))
        ends = pair_when(name, 3, xh, xl, ready, ks, True)
        parts = []
        for j, (b, m) in enumerate(ends):
            x = add_to_x(b, m, 6, gate, (j,))
            parts.append(squares(sq, 6 + j, x, 1))
            if split:
                out.update(split(6 + j, x, 1))
        square_columns(bs, sq, 0, now)

        def finish():
            for j in range(2):
                done = square_columns(bs, sq, 6 + j, parts[j], 1)
            return rstd_columns(bs, 2, D, 0, done)

        return finish, ends[1][1], out

    def normed(rs, b, gain, shift, tmp, xh, xl):
        out, hs = [], []
        VE.wait(rs)
        for k in range(KT + 1):
            if k < KT:
                t = VE.do(lambda e, k=k: e.scalar_tensor_tensor(tmp[:, k, :], XR[:, k, :], gain[:, k:k + 1],
                                                                bank[b][:, 0:T], ALU.mult, ALU.mult))
                SC.wait(t)
                hs.append(SC.do(lambda e, k=k: e.activation(xh[:, k, :], tmp[:, k, :], ACT.Identity,
                                                            bias=shift[:, k:k + 1])))
            if k:
                VE.wait(hs[k - 1])
                out.append([hs[k - 1], VE.do(lambda e, k=k - 1: e.scalar_tensor_tensor(
                    xl[:, k, :], tmp[:, k, :], shift[:, k:k + 1], xh[:, k, :].bitcast(F32), ALU.add, ALU.subtract))])
        freed[b].append(t)
        return out

    def pair_when(name, i, xh, xl, ready, ks=range(KT), apart=False, midway=None):
        s, h, l = chunk(name, i)
        bs = [take("g"), take("g")] if apart else [take("g")] * 2
        todo = [(n, k, j) for j in range(2) for n, k in enumerate(ks)] if apart else [
            (n, k, j) for n, k in enumerate(ks) for j in range(2)]
        marks_ = []
        for n, k, j in todo:
            if midway and (n, j) == (5, 0):
                midway()
            PE.wait(*ready[k])
            m = mm3(bank[bs[j]][:, j * T:(j + 1) * T], h, l, (j * KT + k) * P, xh[:, k, :], xl[:, k, :],
                    n == 0 and (j == 0 or apart), n == KT - 1)
            if n == KT - 1:
                marks_.append((bs[j], m))
        chunk_done(s, m)
        return marks_ if apart else (bs[0], m)

    SQ1 = area("SQ1", [P, KT, T], 48)
    TMP1 = area("TMP1", [P, KT, T], 40)
    H2h = area("H2h", [P, KT, T], 24, F32R)
    H2l = area("H2l", [P, KT, T], 32, F32R)
    finish, merge_done, _ = project("w_out", MGh, MGl, mg, range(KT), 0, SQ1)
    rc = finish()
    warm(ACT.Silu)
    br = claim(3)
    h2 = normed(rows(br, [wide(0), wide(1)], rc), br, A2, MODX[:, 8:16], TMP1, H2h, H2l)

    BI = area("BI", [P, 8, 384], 72)
    PW = area("PW", [P, 2, P], 96)
    SY.wait(merge_done)
    bias_in = load(SY, "bias", BI[:, :, :], io["bias"])
    pw_in = load(SY, "pool_w", PW[:, :, :], io["pool_w"])
    NA = 8
    AH = area("AH", [P, NA, T], 0, F32R)
    AL = area("AL", [P, NA, T], 8, F32R)
    Y = [area(f"Y{i}", [P, 2, T], (56, 58, 64, 66)[i]) for i in range(4)]
    SI = [area(f"SI{i}", [P, T], 60 + i) for i in range(2)]
    AT = [area(f"AT{i}", [P, T], 62 + i) for i in range(2)]
    cw = v("conv_w").rearrange("p (f w) -> p f w", w=9)
    taps = [(dr, dc) for dr in (0, -1, 1) for dc in (0, -1, 1) if (dr, dc) != (0, 0)]
    ring["m"] = [3]
    acc = [claim(b) for b in (4, 5, 6, 7)]
    mids = {}
    a_done, a_read, conv_done, silu_done, ah_done = {}, {}, {}, {}, {}
    y_free = [[], [], [], []]

    def up(i):
        b, m = pair_when("ffn_up", i, H2h, H2l, h2)
        y = Y[i % 4]
        SC.wait(m, *y_free[i % 4])
        for s in range(2):
            f = i + 22 * s
            mid = SC.do(lambda e, s=s, f=f: e.activation(
                y[:, s, :], bank[b][:, s * T:(s + 1) * T], ACT.Identity, bias=v("conv_b", f, 1), scale=cw[:, f, 4:5]))
        mids[i] = b, mid

    def convolve(i):
        y = Y[i % 4]
        b, mid = mids[i]
        VE.wait(mid)
        prev = [mid, mid]
        for dr, dc in taps:
            for s in range(2):
                f = i + 22 * s
                z = bank[b][:, s * T:(s + 1) * T].rearrange("p (r c) -> p r c", c=64)
                o = y[:, s, :].rearrange("p (r c) -> p r c", c=64)
                r0, r1, c0, c1 = max(0, -dr), min(4, 4 - dr), max(0, -dc), min(64, 64 - dc)
                w = cw[:, f, 3 * (dr + 1) + dc + 1:3 * (dr + 1) + dc + 2]
                VE.wait(prev[s])
                prev[s] = VE.do(lambda e, o=o[:, r0:r1, c0:c1], z=z[:, r0 + dr:r1 + dr, c0 + dc:c1 + dc], w=w:
                                e.scalar_tensor_tensor(o, z, w, o, ALU.mult, ALU.add))
        freed[b].append(prev[1])
        conv_done[i] = prev

    def gate(i):
        SC.wait(conv_done[i][0])
        silu_done[i] = SC.do(lambda e: e.activation(SI[i % 2][:, :], Y[i % 4][:, 0, :], ACT.Silu))

    def gated_high(i):
        at = AT[i % 2]
        VE.wait(silu_done[i], conv_done[i][1])
        m = VE.do(lambda e: e.tensor_tensor(at[:, :], SI[i % 2][:, :], Y[i % 4][:, 1, :], ALU.mult))
        y_free[i % 4] = [m]
        SC.wait(m, merge_done, *a_read.get(i - NA, []))
        ah_done[i] = SC.do(lambda e: e.activation(AH[:, i % NA, :], at[:, :], ACT.Copy))

    def gated_low(i):
        at = AT[i % 2]
        VE.wait(ah_done[i], *a_read.get(i - NA, []))
        a_done[i] = [ah_done[i], VE.do(lambda e: e.tensor_tensor(
            AL[:, i % NA, :], at[:, :], AH[:, i % NA, :].bitcast(F32), ALU.subtract))]

    def contract(name, j, xh, xl, slots, ready, last, tell):
        s, h, l = chunk(name, j)
        ends = last == 2 * j + 1
        blocks_ = [(kk_, f) for kk_ in range(2) for f in range(KT)]
        if ends:
            blocks_ = [(kk_, f) for fp in range(4) for kk_ in range(2) for f in (2 * fp, 2 * fp + 1)]
        for n, (kk_, f) in enumerate(blocks_):
            k = 2 * j + kk_
            PE.wait(*ready[k])
            m = mm3(bank[acc[f // 2]][:, f % 2 * T:(f % 2 + 1) * T], h, l, (kk_ * KT + f) * P,
                    xh[:, k % slots, :], xl[:, k % slots, :], k == 0 and f % 2 == 0, ends and n % 4 == 3 or n == 15)
            if ends and n % 4 == 3:
                tell(n // 4, m)
        chunk_done(s, m)
        return m

    def down(j):
        m = contract("ffn_down", j, AH, AL, NA, a_done, 21, residual)
        a_read[2 * j] = a_read[2 * j + 1] = [m]

    SQ2 = area("SQ2", [P, KT, T], 48)
    rb = 3
    sqs, h3, highs = {}, {}, {}
    H3h = area("H3h", [P, KT, T], 24, F32R)
    H3l = area("H3l", [P, KT, T], 32, F32R)

    acc_free = {}

    def residual(i, m):
        acc_free[i] = m
        x = add_to_x(acc[i], m, 2 * i, 24)
        SC.wait(gg)
        highs[i] = scaled_high(GG, H3h, 2 * i, x)
        sqs[i] = squares(SQ2, 2 * i, x)
        if i:
            h3.update(scaled_low(GG, H3h, H3l, 2 * i - 2, highs[i - 1]))
        if i == 3:
            h3.update(scaled_low(GG, H3h, H3l, 6, highs[3]))

    def residual_columns(i):
        PE.wait(sqs[i], *g2)
        for k in (2 * i, 2 * i + 1):
            for t in range(2):
                op = lambda e, k=k, t=t: e.matmul(
                    bank[rb][:, 2 * t:2 * t + 2], SQ2[:, k, t * P:(t + 1) * P], G2[:, k, :],
                    start=k == 0 and t == 0, stop=k == KT - 1, skip_group_check=True)
                m = PE.do(op) if (k, t) == (KT - 1, 1) else PE.go(op)
        return m

    for i in range(24):
        if i < 22:
            up(i)
            prep_ahead(order["ffn_up", i] + 1)
        if i >= 2:
            gated_high(i - 2)
        if i < 22:
            convolve(i)
        if i >= 2:
            gated_low(i - 2)
        if 1 <= i < 23:
            gate(i - 1)
        if i == 22:
            warm(ACT.Sqrt)
        if i >= 5 and i % 2:
            down((i - 5) // 2)
    down(10)
    down_done = acc_free[3]
    ring["m"] = [3, 4, 5, 6, 7]

    def residual_rms():
        residual_columns(2)
        m = residual_columns(3)
        VE.wait(m)
        t = [VE.do(lambda e: e.tensor_scalar(RC[:, 0:2], bank[rb][:, 0:4:2], 1.0 / D, EPS, ALU.mult, ALU.add)),
             VE.do(lambda e: e.tensor_scalar(RC[:, 2:4], bank[rb][:, 1:4:2], 1.0 / D, None, ALU.mult))]
        freed[rb] += t
        VE.wait(*t)
        t = VE.do(lambda e: e.scalar_tensor_tensor(RC[:, 2:4], RC[:, 0:2], EPS, RC[:, 2:4], ALU.mult, ALU.add))
        SC.wait(t)
        t = SC.do(lambda e: e.activation(RC[:, 0:4], RC[:, 0:4], ACT.Sqrt))
        VE.wait(t)
        r12 = VE.do(lambda e: e.reciprocal(RC[:, 0:4], RC[:, 0:4]))
        return r12

    def residual_rows(r12):
        b = take("m")
        rs = rows(b, [wide(2), wide(3), wide(0), wide(1)], r12)
        SC.wait(rs)
        SC.do(lambda e: e.activation(RR1[:, :], bank[b][:, T:2 * T], ACT.Copy))
        a = SC.do(lambda e: e.activation(RR[:, :], bank[b][:, 0:T], ACT.Copy))
        freed[b].append(a)
        return a

    def residual_norm():
        VE.wait(*h3[KT - 1], *sqs.values())
        for f in range(KT):
            VE.do(lambda e, f=f: e.scalar_tensor_tensor(XR[:, f, :], XR[:, f, :], v("final_g", f, 1),
                                                            RR1[:, :], ALU.mult, ALU.mult))

    def midway_0():
        claim(rb)
        residual_columns(0)
        residual_columns(1)

    def midway_1():
        got["rr"] = residual_rows(got["r12"])
        project_in(0)

    def project_in(i):
        b, m = got[i]
        VE.wait(m, got["rr"], down_done)
        pp[i] = VE.do(lambda e: e.tensor_tensor(
            PP[:, 2 * i:2 * i + 2, :], bank[b][:, :].rearrange("p (a t) -> p a t", a=2),
            RR[:, :].unsqueeze(1).to_broadcast([P, 2, T]), ALU.mult))
        freed[b].append(pp[i])
        if i < 4:
            SC.wait(pp[i], *([qk_cols[i - 2]] if i >= 2 else []))
            qk_sq[i] = SC.do(lambda e: e.activation(SQq[i % 2][:, :, :], PP[:, 2 * i:2 * i + 2, :], ACT.Square))

    def values_2(i):
        s, _, _ = chunk("w_in_2", i)
        b = take("g")
        m = by_tokens(b, s, H3h, H3l, h3)
        chunk_done(s, m)
        two = slice(2 * (i - 4), 2 * (i - 4) + 2)
        VE.wait(m, got["r12"], down_done)
        for t in range(2):
            vv.append(VE.do(lambda e, t=t: e.tensor_scalar(
                VV[:, t, two, :], bank[b][:, t * T:(t + 1) * T].rearrange("p (f c) -> p f c", f=2),
                RC[:, 2 + t:3 + t], None, ALU.mult)))
        freed[b].append(vv[-1])

    got = {}
    vv = []
    PP = area("PP", [P, 20, T], 0)
    SQq = [area(f"SQq{i}", [P, 2, T], 20 + 2 * i) for i in range(2)]
    PT = area("PT", [P, 3, 8, P], 56)
    VV = area("VV", [P, 2, NH, P], 68)
    SCR = area("SCR", [P, 8 * 384], 84)
    S0 = SCR[:, 0:8 * P].rearrange("p (h s) -> p h s", h=8)
    S1 = SCR[:, 8 * P:8 * 384].rearrange("p (h s) -> p h s", h=8)
    MXh = area("MXh", [P, KT, T], 40, F32R)
    MXl = area("MXl", [P, KT, T], 48, F32R)
    Z = area("Z", [P, 2, T], 72)
    YC = area("YC", [P, 2, T], 74)
    M2 = area("M2", [P, 2, T], 76)
    M4 = area("M4", [P, 2, T], 78)
    M8 = area("M8", [P, T], 80)
    M16 = area("M16", [P, T], 81)
    PM = area("PM", [P, 2, T], 82)
    UP = area("UP", [P, 2, T], 97)
    pp, qk, qk_sq, qk_rc, qk_cols = {}, {}, {}, {}, {}
    halves2 = c("blk")[:, 0:P:64]

    def qk_columns(i):
        PE.wait(qk_sq[i], con_in)
        b = take("m")
        for j in range(2):
            for t in range(2):
                o = 2 * (2 * j + t)
                op = lambda e, j=j, t=t, o=o: e.matmul(bank[b][:, o:o + 2], SQq[i % 2][:, j, t * P:(t + 1) * P],
                                                       halves2, start=True, stop=True)
                m = PE.do(op) if j + t == 2 else PE.go(op)
        qk_cols[i] = m
        qk_rc[i] = rstd_columns(b, 8, 64, 16 + 8 * i, m)

    def qk_gain():
        VE.wait(vec_in)
        g = VE.do(lambda e: e.scalar_tensor_tensor(v("k_g"), v("q_g"), 0.125, v("k_g"), ALU.mult, ALU.mult))
        VE.wait(g)

    def qk_norm(i):
        b = take("m")
        at = 16 + 8 * i
        PE.wait(qk_rc[i], con_in)
        for n in range(8):
            half = slice(64 * (n % 2), 64 * (n % 2) + 64)
            col = RC[:, at + n:at + n + 1].to_broadcast([P, 64])
            op = lambda e, n=n, half=half, col=col: e.matmul(bank[b][half, n // 2 * P:(n // 2 + 1) * P], col, ident,
                                                            start=True, stop=True)
            r = PE.do(op) if n == 7 else PE.go(op)
        VE.wait(r, pp[i])
        x = PP[:, 2 * i:2 * i + 2, :].rearrange("p a b -> p (a b)")
        qk[i] = VE.do(lambda e: e.scalar_tensor_tensor(x, x, v("k_g"), bank[b][:, :], ALU.mult, ALU.mult))
        freed[b].append(qk[i])

    S = [S0, S1]
    probs = {}

    def scores(g):
        PE.wait(*qk.values(), pp[0], pp[1])
        VE.wait(bias_in, qk_rc[0], qk_rc[1])
        bi = BI[:, :, :].rearrange("p a b -> p (a b)")
        ready = []
        for t, n0, per in ((0, 4 * g, 4), (1, 4 * g, 2), (1, 4 * g + 2, 2)):
            ns = P * (t + 1)
            b = take("m")
            for n in range(per):
                h = HORDER[n0 + n]
                lo_p, tile = 64 * (h % 2), h // 2
                op = lambda e, b=b, n=n, ns=ns, lo_p=lo_p, tile=tile, t=t: e.matmul(
                    bank[b][:, n * ns:(n + 1) * ns], PP[lo_p:lo_p + 64, tile, t * P:(t + 1) * P],
                    PP[lo_p:lo_p + 64, 4 + tile, 0:ns], start=True, stop=True)
                m = PE.do(op) if n == per - 1 else PE.go(op)
            VE.wait(m)
            for n in range(per):
                h = HORDER[n0 + n]
                col = 16 + 8 * (h // 4) + 2 * (2 * (h // 2 % 2) + t) + h % 2
                off = 8 * P * t + (n0 + n) * ns
                a = VE.do(lambda e, b=b, n=n, ns=ns, n0=n0, t=t, col=col, off=off: e.scalar_tensor_tensor(
                    S[t][:, n0 + n, :], bank[b][:, n * ns:(n + 1) * ns], RC[:, col:col + 1], bi[:, off:off + ns],
                    ALU.mult, ALU.add))
            freed[b].append(a)
            ready.append(a)
        VE.wait(*ready)
        mx = [VE.do(lambda e, t=t, g=g: e.tensor_reduce(MX[:, 8 * t + 4 * g:8 * t + 4 * g + 4],
                                                       S[t][:, 4 * g:4 * g + 4, :], AX.X, ALU.max, negate=True))
              for t in range(2)]
        SC.wait(*mx)
        for t in range(2):
            for n in range(4 * g, 4 * g + 4):
                ex = SC.do(lambda e, t=t, n=n, g=g: e.activation(
                    S[t][:, n, :], S[t][:, n, :], ACT.Exp, bias=MX[:, 8 * t + n:8 * t + n + 1],
                    accum_out=SM[:, 8 * g + 4 * t + n % 4:8 * g + 4 * t + n % 4 + 1]))
        probs[g] = ex

    def probabilities(g):
        VE.wait(probs[g])
        rc = VE.do(lambda e: e.reciprocal(SM[:, 8 * g:8 * g + 8], SM[:, 8 * g:8 * g + 8]))
        VE.wait(rc)
        probs["n", g] = [VE.do(lambda e, t=t: e.tensor_tensor(
            S[t][:, 4 * g:4 * g + 4, :], S[t][:, 4 * g:4 * g + 4, :],
            SM[:, 8 * g + 4 * t:8 * g + 4 * t + 4].unsqueeze(2).to_broadcast([P, 4, P * (t + 1)]), ALU.mult))
            for t in range(2)]

    def turn_probabilities(g):
        srcs = [[S[t][:, 4 * g + n, s:s + P] for n in range(4)] for t, s in ((0, 0), (1, 0), (1, P))]
        outs = [PT[:, blk, 4 * g:4 * g + 4, :].rearrange("p a b -> p (a b)") for blk in range(3)]
        probs["t", g] = transposes(srcs, outs, probs["n", g], [down_done])

    pool_m = {}

    def pooling():
        U = PP[:, 12:14, :]
        VE.wait(pp[6])

        def shifted(dst, src, w):
            a = VE.do(lambda e: e.tensor_copy(dst[..., 0:w], src[..., 0:w]))
            return [a, VE.do(lambda e: e.tensor_tensor(dst[..., w:T], src[..., w:T], src[..., 0:T - w], ALU.add))]

        VE.wait(*shifted(M2[:, :, :], U, 1))
        VE.wait(*shifted(M4[:, :, :], M2[:, :, :], 2))
        VE.wait(*shifted(M8[:, :], M4[:, 1, :], 4))
        VE.wait(*shifted(M16[:, :], M8[:, :], 8))
        pr = c("poolr").rearrange("p (f n) -> p f n", f=2)
        groups = [(0, M2[0:64, 0, :], 2), (0, M4[64:128, 0, :], 4), (1, M8[0:64, :], 8), (1, M16[64:128, :], 16)]
        for n, (f, src, w) in enumerate(groups):
            lo_p = 64 * (n % 2)
            y = VE.do(lambda e, f=f, src=src, w=w, lo_p=lo_p: e.tensor_scalar(
                PM[lo_p:lo_p + 64, f, :], src, 1.0 / w, None, ALU.mult))
        VE.wait(y)
        y = VE.do(lambda e: e.tensor_tensor(PM[:, :, 0:16], PM[:, :, 0:16], pr, ALU.mult))
        VE.wait(y)
        pool_m["m"] = VE.do(lambda e: e.tensor_tensor(PM[:, :, :], PM[:, :, :], U, ALU.subtract))

    def pool_product():
        PE.wait(pool_m["m"], pw_in)
        b = take("m")
        for f in range(2):
            m = PE.do(lambda e, f=f: e.matmul(bank[b][:, f * T:(f + 1) * T], PW[:, f, :], PM[:, f, :], start=True,
                                              stop=True))
        VE.wait(m)
        for f in range(2):
            y = VE.do(lambda e, f=f: e.tensor_scalar(UP[:, f, :], bank[b][:, f * T:(f + 1) * T],
                                                     v("pool_scale", f, 1), None, ALU.mult))
        freed[b].append(y)
        mix[6] = mix[7] = to_mix(UP[:, :, :], 6, 2, y)

    def short_conv():
        VE.wait(pp[7], pp[8])
        z = VE.do(lambda e: e.tensor_tensor(Z[:, :, :], PP[:, 14:16, :], PP[:, 16:18, :], ALU.mult))
        VE.wait(z)
        cw2 = v("conv_w_2").rearrange("p (f w) -> p f w", w=3)
        for f in range(2):
            y = VE.do(lambda e, f=f: e.tensor_scalar(YC[:, f, :], Z[:, f, :], cw2[:, f, 2:3], None, ALU.mult))
        for s in (1, 2):
            VE.wait(y)
            for f in range(2):
                y = VE.do(lambda e, f=f, s=s: e.scalar_tensor_tensor(
                    YC[:, f, s:T], Z[:, f, 0:T - s], cw2[:, f, 2 - s:3 - s], YC[:, f, s:T], ALU.mult, ALU.add))
        pool_m["conv"] = y

    def short_conv_gate():
        VE.wait(pool_m["conv"], pp[9])
        y = VE.do(lambda e: e.tensor_tensor(YC[:, :, :], YC[:, :, :], PP[:, 18:20, :], ALU.mult))
        mix[4] = mix[5] = to_mix(YC[:, :, :], 4, 2, y)

    mix = {}

    def to_mix(src, k, n, after):
        SC.wait(after)
        a = SC.do(lambda e: e.activation(MXh[:, k:k + n, :], src, ACT.Copy))
        VE.wait(a)
        return [a, VE.do(lambda e: e.tensor_tensor(MXl[:, k:k + n, :], src, MXh[:, k:k + n, :].bitcast(F32),
                                                   ALU.subtract))]

    for i in range(10):
        if i in (4, 5):
            values_2(i)
        else:
            got[i] = pair_when("w_in_2", i, H3h, H3l, h3, midway={0: midway_0, 1: midway_1}.get(i))
        if i == 0:
            got["r12"] = residual_rms()
        elif i in (4, 5):
            pass
        else:
            project_in(i)
        if i == 2:
            residual_norm()
        if i == 3:
            qk_gain()
        if 4 <= i < 6:
            qk_norm(i - 2)
        if 1 <= i < 5:
            qk_columns(i - 1)
        if i == 6:
            scores(0)
        if i == 7:
            scores(1)
            probabilities(0)
            pooling()
            probabilities(1)
        if i == 8:
            turn_probabilities(0)
            short_conv()
    turn_probabilities(1)
    pool_product()
    short_conv_gate()
    PE.wait(*probs["t", 0], *probs["t", 1], *vv)
    for tp in range(2):
        b = take("m")
        for j in range(2):
            for par in range(2):
                h = 2 * (2 * tp + j) + par
                n = HORDER.index(h)
                o = bank[b][64 * par:64 * par + 64, j * T:(j + 1) * T]
                w = [VV[:, t, h // 2, 64 * par:64 * par + 64] for t in range(2)]
                PE.go(lambda e, o=o, w=w, n=n: e.matmul(o[:, 0:P], w[0], PT[:, 0, n, :], start=True, stop=True))
                PE.go(lambda e, o=o, w=w, n=n: e.matmul(o[:, P:T], w[0], PT[:, 1, n, :], start=True, stop=False))
                m = PE.do(lambda e, o=o, w=w, n=n: e.matmul(o[:, P:T], w[1], PT[:, 2, n, :], start=False, stop=True))
        src = bank[b][:, :].rearrange("p (a t) -> p a t", a=2)
        mix[2 * tp] = mix[2 * tp + 1] = to_mix(src, 2 * tp, 2, m)
        freed[b].append(mix[2 * tp][1])

    SQ3 = area("SQ3", [P, KT, T], 72)
    H4h = area("H4h", [P, KT, T], 8, F32R)
    H4l = area("H4l", [P, KT, T], 16, F32R)
    ready = [mix[k] for k in range(KT)]
    finish, out2_done, h4 = project("w_out_2", MXh, MXl, ready, [6, 7, 4, 5, 0, 1, 2, 3], None, SQ3,
                                    lambda f, x, n=2: scaled_low(
                                        v("norm2_g_2"), H4h, H4l, f, scaled_high(v("norm2_g_2"), H4h, f, x, n)))

    NF = 8
    FH = area("FH", [P, NF, T], 24, F32R)
    FL = area("FL", [P, NF, T], 32, F32R)
    FR = [area(f"FR{i}", [P, 2, T], 88 + 2 * i) for i in range(2)]
    FQ = [area(f"FQ{i}", [P, 2, T], 92 + 2 * i) for i in range(2)]
    f_done, f_read = {}, {}

    def finish_norm():
        got["rc"] = finish()

    def norm_rows():
        b = take("m")
        rs = rows(b, [wide(0), wide(1)], got["rc"])
        SC.wait(rs)
        got["rr2"] = SC.do(lambda e: e.activation(RR[:, :], bank[b][:, 0:T], ACT.Copy))
        freed[b].append(got["rr2"])

    s_out = sem("stores")

    def mlp_out(i, m):
        x = add_to_x(acc[i], m, 2 * i, None)
        SY.wait(x)
        SY.go(lambda e: e.dma_start(io["out"][:, 2 * i:2 * i + 2, :], XR[:, 2 * i:2 * i + 2, :]).then_inc(s_out, 16))

    def mlp_up(i):
        b, m = pair_when("w_mlp1", i, H4h, H4l, h4, midway=finish_norm if i == 0 else None)
        if i == 0:
            norm_rows()
        fr, fq = FR[i % 2], FQ[i % 2]
        at = 2 * i % NF
        VE.wait(m, got["rr2"])
        r = VE.do(lambda e: e.scalar_tensor_tensor(
            fr[:, :, :], bank[b][:, :].rearrange("p (a t) -> p a t", a=2), 0.0,
            RR[:, :].unsqueeze(1).to_broadcast([P, 2, T]), ALU.max, ALU.mult))
        freed[b].append(r)
        VE.wait(r)
        q = VE.do(lambda e: e.tensor_tensor(fq[:, :, :], fr[:, :, :], fr[:, :, :], ALU.mult))
        SC.wait(q, out2_done, *f_read.get(i - NF // 2, []))
        a = SC.do(lambda e: e.activation(FH[:, at:at + 2, :], fq[:, :, :], ACT.Copy))
        VE.wait(a, *f_read.get(i - NF // 2, []))
        l = VE.do(lambda e: e.tensor_tensor(FL[:, at:at + 2, :], fq[:, :, :], FH[:, at:at + 2, :].bitcast(F32),
                                            ALU.subtract))
        f_done[2 * i] = f_done[2 * i + 1] = [a, l]

    acc = None
    for i in range(18):
        if i < 16:
            mlp_up(i)
        if i == 2:
            acc = [claim(b) for b in (4, 5, 6, 7)]
        if i >= 2:
            f_read[i - 2] = [contract("w_mlp2", i - 2, FH, FL, NF, f_done, 31, mlp_out)]
    SY.wait((s_out, 64))

    with nc.Block() as block:
        block.sync(SY.replay)
        block.scalar(SC.replay)
        block.vector(VE.replay)
        block.gpsimd(PO.replay)
        block.tensor(PE.replay)


def tiles(w, ft, order=None):
    k, n = w.shape
    b = w.reshape(k // P, P, n // P, P).transpose(2, 1, 0, 3)
    if order is not None:
        b = b[order]
    if ft:
        b = b.reshape(-1, ft, P, k // P, P).transpose(0, 2, 1, 3, 4)
        return np.ascontiguousarray(b.reshape(b.shape[0], P, -1))
    b = b.transpose(2, 1, 0, 3).reshape(k // P // 2, 2, P, n // P, P).transpose(0, 2, 1, 3, 4)
    return np.ascontiguousarray(b.reshape(k // P // 2, P, -1))


def wide_rows(w):
    k, n = w.shape
    return np.ascontiguousarray(w.T.reshape(n // P // 2, 2, P, k).transpose(0, 2, 1, 3).reshape(-1, P, 2 * k))


def columns(a):
    a = np.asarray(a)
    return a.reshape(-1, P).T


def constants():
    con = np.zeros((P, NC), np.float32)

    def put(name, x):
        a, w = CON[name]
        con[:, a:a + w] = x.reshape(P, w)

    put("ident", np.eye(P))
    i = np.arange(P)
    ang = 2 * np.pi * (np.outer(i, i) % P) / P
    put("dft_c", np.concatenate([np.cos(ang)[:, 0:65], np.sin(ang)[:, 1:64]], 1))
    j = np.arange(T)
    ang = 2 * np.pi * (np.outer(j, j) % T) / T
    s = 1.0 / np.sqrt(T * P)
    both = np.stack([np.cos(ang) * s, -np.sin(ang) * s])
    put("dft_l", both.reshape(2, 2, P, T).transpose(2, 1, 0, 3))
    put("blk", (i[:, None] // 64 == i[None, :] // 64).astype(np.float32))
    r = np.zeros((P, 2, 16))
    for f in range(2):
        for p in range(P):
            w = 2 ** (2 * f + p // 64 + 1)
            r[p, f] = w / np.minimum(np.arange(16) + 1, w)
    put("poolr", r)
    masks = np.zeros((P, len(LEVELS), P), np.float32)
    for n, h in enumerate(LEVELS):
        masks[:, n] = (i[:, None] // (2 * h) == i[None, :] // (2 * h)) & (i[:, None] // h != i[None, :] // h)
    return con, masks


def bias_rows(rel):
    t, s = np.arange(T)[:, None], np.arange(T)[None, :]
    full = rel[:, np.clip(t - s, -128, 128) + 128]
    full = np.where((s // 64 <= t // 64)[None], full, np.float32(-1e30)).astype(rel.dtype)
    full = full[HORDER]
    a = full[:, 0:P, 0:P].transpose(1, 0, 2).reshape(P, -1)
    b = full[:, P:T, :].transpose(1, 0, 2).reshape(P, -1)
    return np.ascontiguousarray(np.concatenate([a, b], 1).reshape(P, 8, 384))


def kernel(**inputs):
    import concourse.bacc as bacc
    from concourse.bass_utils import run_bass_kernel_spmd as run

    g = {k: np.asarray(x) for k, x in inputs.items()}
    con, masks = constants()
    dup = lambda a: np.concatenate([a.reshape(-1), a.reshape(-1)])[:, None]
    cols = {
        "norm1_g": columns(g["norm1_g"]), "ada_b": columns(g["ada_b"]), "hg_lb": columns(g["hg_lb"]),
        "onorm": columns(g["hg_onorm_g"]), "norm2_g": columns(g["norm2_g"]), "conv_b": columns(g["ffn_conv_b"]),
        "conv_w": g["ffn_conv_w"].reshape(9, 44, P).transpose(2, 1, 0).reshape(P, -1),
        "final_g": columns(g["final_g"]), "norm1_g_2": columns(g["norm1_g_2"]),
        "q_g": dup(g["q_norm_g_2"]), "k_g": dup(g["k_norm_g_2"]),
        "conv_w_2": g["conv_w_2"].reshape(3, 2, P).transpose(2, 1, 0).reshape(P, -1),
        "pool_scale": columns(g["pool_scale_2"]), "norm2_g_2": columns(g["norm2_g_2"]),
        "c2": np.stack([g["c"].reshape(KT, P), g["c_ctx"].reshape(KT, P)], 2).transpose(1, 0, 2).reshape(P, -1),
    }
    pw = np.zeros((P, 2, P), np.float32)
    for n in range(4):
        a = 64 * (n % 2)
        pw[a:a + 64, n // 2, a:a + 64] = g["pool_w_2"][0, n]
    w_in = g["w_in"][0]
    arrays = {
        "vec": np.ascontiguousarray(np.concatenate([cols[n] for n in VEC], 1)),
        "con": con, "masks": masks,
        "xT": np.ascontiguousarray(g["x"][0].T.reshape(KT, P, T).transpose(1, 0, 2)),
        "ctxT": np.ascontiguousarray(g["ctx"][0].T.reshape(KT, P, T).transpose(1, 0, 2)),
        "c_row": np.ascontiguousarray(g["c"].reshape(1, D)),
        "c_ctx_row": np.ascontiguousarray(g["c_ctx"].reshape(1, D)),
        "bias": bias_rows(g["rel_bias_2"][0]), "pool_w": pw,
        "ada_p": tiles(g["ada_w"][0][:, :1024], 2), "ada_s": wide_rows(g["ada_w"][0][:, 1024:2048]),
        "ada_hi": wide_rows(g["ada_w"][0][:, 2048:]),
        "w_in": tiles(w_in, 2, [*range(4, 20), *range(0, 4), *range(20, 40)]),
        "w_a": tiles(g["w_a"][0], 4), "w_b": tiles(g["w_b"][0], 4), "w_out": tiles(g["w_out"][0], 2),
        "ffn_up": tiles(g["ffn_up"][0], 2, [f for i in range(22) for f in (i, i + 22)]),
        "ffn_down": tiles(g["ffn_down"][0], 0),
        "w_in_2": tiles(g["w_in_2"][0], 2, [*range(12), 18, 19, *range(14, 18), 12, 13]), "w_out_2": tiles(g["w_out_2"][0], 2),
        "w_mlp1": tiles(g["w_mlp1_2"][0], 2), "w_mlp2": tiles(g["w_mlp2_2"][0], 0),
    }
    nc = bacc.Bacc("TRN2", target_bir_lowering=False, num_devices=1)
    io, feed = {}, {}
    for name, a in arrays.items():
        feed[f"in_{name}"] = a
        io[name] = nc.dram_tensor(f"in_{name}", a.shape, mybir.dt.from_np(a.dtype), kind="ExternalInput").ap()
    io["out"] = nc.dram_tensor("out_x", (P, KT, T), F32, kind="ExternalOutput").ap()
    build(nc, io)
    r = run(nc, [feed], core_ids=[0])
    got = r.results[0]["out_x"]
    return np.ascontiguousarray(got.transpose(2, 1, 0).reshape(1, T, D))
```
